# Optimizing a Trainium2 kernel written in Bass

```python
import math
import jax, jax.numpy as jnp
from jax import lax
import numpy as np
import jax
import jax.numpy as jnp

D_MODEL = 1024
BATCH = 1
SEQ = 256
DEPTH = 2

A_HEADS = 4
A_QK_DIM = 64
A_V_DIM = 2 * A_QK_DIM
A_QK_COLS = A_HEADS * 2 * A_QK_DIM
A_WIDTH = A_HEADS * A_V_DIM
ROPE_THETA = 500000.0
ROPE_DIM = A_QK_DIM // 4
Q_BLOCK = 128
NEG_INF = -1e30
C_WIDTH = 512
CONV_WIDTH = 3
R_HEADS = 4
R_QK_DIM = 64
R_V_DIM = 2 * R_QK_DIM
R_QK_COLS = R_HEADS * R_QK_DIM
R_WIDTH = R_HEADS * R_V_DIM
R_CHUNK = 128
RET_THETA = 10000.0
N_BRANCH = 3
BRANCH_WIDTH = 512
EPS = 1e-6

SPLIT_SIZES = (A_QK_COLS, A_QK_COLS, A_WIDTH, A_WIDTH,
               C_WIDTH, C_WIDTH, C_WIDTH, C_WIDTH,
               R_QK_COLS, R_QK_COLS, R_WIDTH, R_WIDTH,
               N_BRANCH * D_MODEL)
IN_COLS = sum(SPLIT_SIZES)


def rms_norm(x, g=None):
    xf = x.astype(jnp.float32)
    y = xf * lax.rsqrt(jnp.mean(xf * xf, axis=-1, keepdims=True) + EPS)
    return y if g is None else y * g.astype(jnp.float32)

def rotate(x, cos, sin):
    x1, x2 = jnp.split(x, 2, axis=-1)
    return jnp.concatenate([x1 * cos - x2 * sin, x2 * cos + x1 * sin], axis=-1)

def diff_attention(q, k, v, lam, subln_g, lam_init):
    b, s = q.shape[0], q.shape[1]
    pos = jnp.arange(s, dtype=jnp.float32)
    inv = ROPE_THETA ** (-jnp.arange(0, ROPE_DIM, 2, dtype=jnp.float32) / ROPE_DIM)
    ang = pos[:, None] * inv[None, :]
    cos = jnp.cos(ang)[:, None, None, :]
    sin = jnp.sin(ang)[:, None, None, :]
    q = jnp.concatenate([rotate(q[..., :ROPE_DIM], cos, sin), q[..., ROPE_DIM:]], axis=-1)
    k = jnp.concatenate([rotate(k[..., :ROPE_DIM], cos, sin), k[..., ROPE_DIM:]], axis=-1)
    q = q * (A_QK_DIM ** -0.5)
    kh = k.transpose(0, 2, 3, 1, 4)
    vh = v.transpose(0, 2, 1, 3)
    nb = s // Q_BLOCK
    qb = q.transpose(0, 2, 3, 1, 4).reshape(b, A_HEADS, 2, nb, Q_BLOCK, A_QK_DIM)
    qb = qb.transpose(3, 0, 1, 2, 4, 5)
    kpos = jnp.arange(s)

    def block(args):
        qi, start = args
        sc = jnp.einsum('bhcqd,bhckd->bhcqk', qi, kh).astype(jnp.float32)
        qpos = start + jnp.arange(Q_BLOCK)
        mask = kpos[None, :] <= qpos[:, None]
        p = jax.nn.softmax(jnp.where(mask, sc, NEG_INF), axis=-1)
        w = p[:, :, 0] - lam * p[:, :, 1]
        return jnp.einsum('bhqk,bhkv->bhqv', w, vh)

    out = lax.map(block, (qb, jnp.arange(nb, dtype=jnp.int32) * Q_BLOCK))
    out = out.transpose(1, 0, 3, 2, 4).reshape(b, s, A_HEADS, A_V_DIM)
    out = rms_norm(out, subln_g) * (1.0 - lam_init)
    return out.reshape(b, s, A_WIDTH)

def short_conv(x_in, gate_b, gate_c, w):
    u = gate_c * x_in
    y = lax.conv_general_dilated(u, w[:, None, :].astype(u.dtype), window_strides=(1,),
                                 padding=[(CONV_WIDTH - 1, 0)],
                                 dimension_numbers=('NWC', 'WIO', 'NWC'),
                                 feature_group_count=C_WIDTH)
    return gate_b * y

def retention(q, k, v):
    b, s = q.shape[0], q.shape[1]
    pos = jnp.arange(s, dtype=jnp.float32)
    inv = 1.0 / (RET_THETA ** jnp.linspace(0.0, 1.0, R_QK_DIM // 2, dtype=jnp.float32))
    ang = pos[:, None] * inv[None, :]
    cos = jnp.cos(ang)[:, None, :]
    sin = jnp.sin(ang)[:, None, :]
    q = rotate(q, cos, sin)
    k = rotate(k, cos, sin) * (R_QK_DIM ** -0.5)
    log_g = jnp.log(1.0 - 2.0 ** (-5.0 - jnp.arange(R_HEADS, dtype=jnp.float32)))
    nc = s // R_CHUNK

    def chunks(t):
        return t.reshape(b, nc, R_CHUNK, R_HEADS, t.shape[-1]).transpose(0, 3, 1, 2, 4)

    qc, kc, vc = chunks(q), chunks(k), chunks(v)
    idx = jnp.arange(R_CHUNK, dtype=jnp.float32)
    diff = idx[:, None] - idx[None, :]
    dmask = jnp.where(diff >= 0,
                      jnp.exp(jnp.where(diff >= 0, diff, 0.0)[None] * log_g[:, None, None]),
                      0.0)
    inner = jnp.einsum('bhncd,bhnmd->bhncm', qc, kc) * dmask[None, :, None]
    inner = jnp.einsum('bhncm,bhnme->bhnce', inner, vc)
    zeta = jnp.exp((R_CHUNK - 1 - idx)[None, :] * log_g[:, None])
    kv = jnp.einsum('bhnmd,bhnme->bhnde', kc * zeta[None, :, None, :, None], vc)
    chunk_decay = jnp.exp(R_CHUNK * log_g)[None, :, None, None]

    def step(state, kv_n):
        return (chunk_decay * state + kv_n).astype(kv_n.dtype), state

    init = jnp.zeros((b, R_HEADS, R_QK_DIM, R_V_DIM), kv.dtype)
    _, prev = lax.scan(step, init, kv.transpose(2, 0, 1, 3, 4))
    prev = prev.transpose(1, 2, 0, 3, 4)
    xi = jnp.exp((idx + 1.0)[None, :] * log_g[:, None])
    cross = jnp.einsum('bhncd,bhnde->bhnce', qc, prev) * xi[None, :, None, :, None]
    out = (inner + cross).transpose(0, 2, 3, 1, 4).reshape(b, s, R_HEADS, R_V_DIM)
    out = rms_norm(out)
    return out.reshape(b, s, R_WIDTH)

def hybrid_layer(x, norm_g, w_in, attn_lambda, attn_subln_g, conv_w, w_branch, w_out, layer):
    b, s, _ = x.shape
    h = rms_norm(x, norm_g)
    proj = h @ w_in
    split_points = [int(p) for p in np.cumsum(SPLIT_SIZES)[:-1]]
    (aq, ak, av, az, cx, cb, cc, cz, rq, rk, rv, rz, gates) = jnp.split(proj, split_points, axis=-1)

    lam_init = 0.8 - 0.6 * math.exp(-0.3 * layer)
    lp = attn_lambda.astype(jnp.float32)
    lam = jnp.exp(jnp.sum(lp[0] * lp[1])) - jnp.exp(jnp.sum(lp[2] * lp[3])) + lam_init
    a = diff_attention(aq.reshape(b, s, A_HEADS, 2, A_QK_DIM),
                       ak.reshape(b, s, A_HEADS, 2, A_QK_DIM),
                       av.reshape(b, s, A_HEADS, A_V_DIM),
                       lam, attn_subln_g, lam_init) * jax.nn.silu(az)
    c = short_conv(cx, cb, cc, conv_w) * jax.nn.silu(cz)
    r = retention(rq.reshape(b, s, R_HEADS, R_QK_DIM),
                  rk.reshape(b, s, R_HEADS, R_QK_DIM),
                  rv.reshape(b, s, R_HEADS, R_V_DIM)) * jax.nn.silu(rz)

    g = jax.nn.sigmoid(gates.astype(jnp.float32)).reshape(b, s, N_BRANCH, D_MODEL)
    branches = (a, c, r)
    merged = g[:, :, 0] * (branches[0] @ w_branch[0])
    for i in range(1, N_BRANCH):
        merged = merged + g[:, :, i] * (branches[i] @ w_branch[i])
    return x + (merged @ w_out).astype(x.dtype)

def first_inputs(seed: int = 0) -> dict:
    key = jax.random.key(seed)
    ks = jax.random.split(key, 10)
    f32 = jnp.float32
    x = jax.random.normal(ks[0], (BATCH, SEQ, D_MODEL), f32)
    norm_g = 1.0 + 0.01 * jax.random.normal(ks[1], (DEPTH, D_MODEL), f32)
    w_in = jax.random.normal(ks[2], (DEPTH, D_MODEL, IN_COLS), f32) * D_MODEL ** -0.5
    attn_lambda = 0.1 * jax.random.normal(ks[3], (DEPTH, 4, A_QK_DIM), f32)
    attn_subln_g = 1.0 + 0.01 * jax.random.normal(ks[4], (DEPTH, A_V_DIM), f32)
    conv_w = jax.random.normal(ks[5], (DEPTH, CONV_WIDTH, C_WIDTH), f32) * CONV_WIDTH ** -0.5
    w_branch = jax.random.normal(ks[6], (DEPTH, N_BRANCH, BRANCH_WIDTH, D_MODEL), f32) * BRANCH_WIDTH ** -0.5
    w_out = jax.random.normal(ks[7], (DEPTH, D_MODEL, D_MODEL), f32) * D_MODEL ** -0.5
    final_norm_g = 1.0 + 0.01 * jax.random.normal(ks[8], (D_MODEL,), f32)
    return {"x": x, "norm_g": norm_g, "w_in": w_in, "attn_lambda": attn_lambda,
            "attn_subln_g": attn_subln_g, "conv_w": conv_w, "w_branch": w_branch,
            "w_out": w_out, "final_norm_g": final_norm_g}

def first_block(x, norm_g, w_in, attn_lambda, attn_subln_g, conv_w, w_branch, w_out, final_norm_g):
    for layer in range(DEPTH):
        x = hybrid_layer(x, norm_g[layer], w_in[layer], attn_lambda[layer], attn_subln_g[layer],
                         conv_w[layer], w_branch[layer], w_out[layer], layer)
    return rms_norm(x, final_norm_g).astype(x.dtype)


FOX_HEADS = 8
FOX_HEAD_DIM = 64
MLA_HEADS = 8
MLA_Q_RANK = 256
MLA_KV_RANK = 128
MLA_NOPE_DIM = 64
MLA_ROPE_DIM = 32
MLA_V_DIM = 64
ROPE_THETA_2 = 10000.0
DN_HEADS = 8
DN_HEAD_DIM = 64
DN_CONV_WIDTH = 4
DN_CHUNK = 64
D_FF = 2816
NORM_EPS = 1e-6

FOX_WIDTH = FOX_HEADS * FOX_HEAD_DIM
MLA_QK_DIM = MLA_NOPE_DIM + MLA_ROPE_DIM
MLA_WIDTH = MLA_HEADS * MLA_V_DIM
DN_WIDTH = DN_HEADS * DN_HEAD_DIM
IN_WIDTHS = (FOX_WIDTH, FOX_WIDTH, FOX_WIDTH, FOX_HEADS,
             MLA_Q_RANK, MLA_KV_RANK, MLA_ROPE_DIM,
             DN_WIDTH, DN_WIDTH, DN_WIDTH, DN_WIDTH, DN_HEADS, DN_HEADS,
             N_BRANCH * D_MODEL)
N_IN = sum(IN_WIDTHS)


def rmsnorm(x, gain):
    xf = x.astype(jnp.float32)
    y = xf * lax.rsqrt(jnp.mean(xf * xf, axis=-1, keepdims=True) + NORM_EPS)
    return (y * gain.astype(jnp.float32)).astype(x.dtype)

def l2norm(x):
    xf = x.astype(jnp.float32)
    return xf * lax.rsqrt(jnp.sum(xf * xf, axis=-1, keepdims=True) + NORM_EPS)

def swiglu(h, w_gu, w_down):
    gate, up = jnp.split(h @ w_gu, 2, axis=-1)
    return (jax.nn.silu(gate) * up) @ w_down

def rope_tables(positions):
    half = MLA_ROPE_DIM // 2
    inv_freq = ROPE_THETA_2 ** (-jnp.arange(half, dtype=jnp.float32) / half)
    ang = positions.astype(jnp.float32)[..., None] * inv_freq
    return jnp.cos(ang)[:, :, None, :], jnp.sin(ang)[:, :, None, :]

def apply_rope(x, cos, sin):
    x1, x2 = jnp.split(x.astype(jnp.float32), 2, axis=-1)
    return jnp.concatenate([x1 * cos - x2 * sin, x2 * cos + x1 * sin], axis=-1).astype(x.dtype)

def causal_short_conv(x, w):
    width = w.shape[0]
    s = x.shape[1]
    xp = jnp.pad(x, ((0, 0), (width - 1, 0), (0, 0)))
    return sum(xp[:, i:i + s] * w[i] for i in range(width))

def block_causal_attention(q, k, v, scale, log_decay_cum=None):
    b, s, h, dqk = q.shape
    dv = v.shape[-1]
    nb = s // Q_BLOCK
    q_blocks = q.reshape(b, nb, Q_BLOCK, h, dqk).transpose(1, 0, 3, 2, 4)
    k_pos = jnp.arange(s)
    xs = (jnp.arange(nb), q_blocks)
    if log_decay_cum is not None:
        c = log_decay_cum.astype(jnp.float32).transpose(0, 2, 1)
        c_blocks = c.reshape(b, h, nb, Q_BLOCK).transpose(2, 0, 1, 3)
        xs = (jnp.arange(nb), q_blocks, c_blocks)

    def one_block(args):
        idx, q_blk = args[0], args[1]
        logits = jnp.einsum('bhqd,bkhd->bhqk', q_blk, k).astype(jnp.float32) * scale
        if log_decay_cum is not None:
            logits = logits + args[2][..., :, None] - c[:, :, None, :]
        q_pos = idx * Q_BLOCK + jnp.arange(Q_BLOCK)
        logits = jnp.where(k_pos[None, :] <= q_pos[:, None], logits, -jnp.inf)
        p = jax.nn.softmax(logits, axis=-1).astype(v.dtype)
        return jnp.einsum('bhqk,bkhd->bqhd', p, v)

    out = lax.map(one_block, xs)
    return out.transpose(1, 0, 2, 3, 4).reshape(b, s, h, dv)

def chunk_gated_delta_rule(q, k, v, g, beta):
    b, s, h, dk = q.shape
    dv = v.shape[-1]
    nc = s // DN_CHUNK

    def to_chunks(t):
        return jnp.moveaxis(t.reshape((b, nc, DN_CHUNK, h) + t.shape[3:]), 3, 2)

    q, k, v, g, beta = (to_chunks(t) for t in (q, k, v, g, beta))
    gc = jnp.cumsum(g, axis=-1)
    idx = jnp.arange(DN_CHUNK)
    causal = idx[:, None] >= idx[None, :]
    strict = idx[:, None] > idx[None, :]
    decay_mat = jnp.exp(jnp.where(causal, gc[..., :, None] - gc[..., None, :], -jnp.inf))
    k_beta = k * beta[..., None]
    v_beta = v * beta[..., None]
    m = jnp.where(strict, jnp.einsum('bnhid,bnhjd->bnhij', k_beta, k) * decay_mat, 0.0)
    eye = jnp.eye(DN_CHUNK, dtype=jnp.float32)
    t_inv = lax.linalg.triangular_solve(eye + m, jnp.broadcast_to(eye, m.shape),
                                        left_side=True, lower=True, unit_diagonal=True)
    w = t_inv @ (k_beta * jnp.exp(gc)[..., None])
    u = t_inv @ v_beta
    qk = jnp.einsum('bnhid,bnhjd->bnhij', q, k) * decay_mat
    q_dec = q * jnp.exp(gc)[..., None]
    k_dec = k * jnp.exp(gc[..., -1:] - gc)[..., None]
    g_last = jnp.exp(gc[..., -1])

    def step(state, xs_c):
        w_c, u_c, qk_c, q_c, k_c, gl = xs_c
        v_new = u_c - w_c @ state
        o_c = q_c @ state + qk_c @ v_new
        state = state * gl[..., None, None] + jnp.einsum('bhcd,bhce->bhde', k_c, v_new)
        return state, o_c

    xs = tuple(jnp.moveaxis(t, 1, 0) for t in (w, u, qk, q_dec, k_dec, g_last))
    state0 = jnp.zeros((b, h, dk, dv), jnp.float32)
    _, o = lax.scan(step, state0, xs)
    return o.transpose(1, 0, 3, 2, 4).reshape(b, s, h, dv)

def hybrid_mixer(h, cos, sin, w_in, b_gate, fox_b_f, mla_q_norm, mla_w_uq, mla_kv_norm, mla_w_ukv,
                 dn_conv_w, dn_a_log, dn_dt_bias, dn_o_norm, w_br_fox, w_br_mla, w_br_dn, w_out):
    b, s, _ = h.shape
    f32 = jnp.float32
    splits = np.cumsum(IN_WIDTHS)[:-1]
    (fox_q, fox_k, fox_v, fox_f, mla_cq, mla_ckv, mla_kr,
     dn_q, dn_k, dn_v, dn_z, dn_b, dn_a, gate_logits) = jnp.split(h @ w_in, splits, axis=-1)

    fox_shape = (b, s, FOX_HEADS, FOX_HEAD_DIM)
    log_f = jax.nn.log_sigmoid(fox_f.astype(f32) + fox_b_f.astype(f32))
    fox_out = block_causal_attention(fox_q.reshape(fox_shape), fox_k.reshape(fox_shape),
                                     fox_v.reshape(fox_shape), FOX_HEAD_DIM ** -0.5,
                                     jnp.cumsum(log_f, axis=1))
    y_fox = fox_out.reshape(b, s, FOX_WIDTH) @ w_br_fox

    q = (rmsnorm(mla_cq, mla_q_norm) @ mla_w_uq).reshape(b, s, MLA_HEADS, MLA_QK_DIM)
    q_nope, q_rope = jnp.split(q, [MLA_NOPE_DIM], axis=-1)
    kv = (rmsnorm(mla_ckv, mla_kv_norm) @ mla_w_ukv).reshape(b, s, MLA_HEADS, MLA_NOPE_DIM + MLA_V_DIM)
    k_nope, mla_v = jnp.split(kv, [MLA_NOPE_DIM], axis=-1)
    k_rope = apply_rope(mla_kr[:, :, None, :], cos, sin)
    q_full = jnp.concatenate([q_nope, apply_rope(q_rope, cos, sin)], axis=-1)
    k_full = jnp.concatenate([k_nope, jnp.broadcast_to(k_rope, (b, s, MLA_HEADS, MLA_ROPE_DIM))], axis=-1)
    mla_out = block_causal_attention(q_full, k_full, mla_v, MLA_QK_DIM ** -0.5)
    y_mla = mla_out.reshape(b, s, MLA_WIDTH) @ w_br_mla

    qkv = jax.nn.silu(causal_short_conv(jnp.concatenate([dn_q, dn_k, dn_v], axis=-1), dn_conv_w))
    cq, ck, cv = jnp.split(qkv, 3, axis=-1)
    dn_shape = (b, s, DN_HEADS, DN_HEAD_DIM)
    q_dn = l2norm(cq.reshape(dn_shape)) * (DN_HEAD_DIM ** -0.5)
    k_dn = l2norm(ck.reshape(dn_shape))
    v_dn = cv.reshape(dn_shape).astype(f32)
    beta = jax.nn.sigmoid(dn_b.astype(f32))
    g = -jnp.exp(dn_a_log.astype(f32)) * jax.nn.softplus(dn_a.astype(f32) + dn_dt_bias.astype(f32))
    o = chunk_gated_delta_rule(q_dn, k_dn, v_dn, g, beta)
    o = rmsnorm(o, dn_o_norm).astype(h.dtype) * jax.nn.silu(dn_z.reshape(dn_shape))
    y_dn = o.reshape(b, s, DN_WIDTH) @ w_br_dn

    g_fox, g_mla, g_dn = jnp.split(jax.nn.sigmoid(gate_logits + b_gate), N_BRANCH, axis=-1)
    return (g_fox * y_fox + g_mla * y_mla + g_dn * y_dn) @ w_out

def second_inputs(seed: int = 0) -> dict:
    key = jax.random.key(seed)
    ks = iter(list(jax.random.split(key, 32)))
    f32 = jnp.float32
    L = DEPTH

    def nrm(shape, scale):
        return jax.random.normal(next(ks), shape, f32) * scale

    def gain(shape):
        return 1.0 + nrm(shape, 0.1)

    x = jax.random.normal(next(ks), (BATCH, SEQ, D_MODEL), f32)
    positions = (jnp.arange(SEQ, dtype=jnp.int32)[None, :]
                 + jax.random.randint(next(ks), (BATCH, 1), 0, 1024, dtype=jnp.int32))
    ffn1_norm = gain((L, D_MODEL))
    ffn1_w_gu = nrm((L, D_MODEL, 2 * D_FF), D_MODEL ** -0.5)
    ffn1_w_down = nrm((L, D_FF, D_MODEL), D_FF ** -0.5)
    mix_norm = gain((L, D_MODEL))
    w_in = nrm((L, D_MODEL, N_IN), D_MODEL ** -0.5)
    b_gate = nrm((L, N_BRANCH * D_MODEL), 0.1)
    fox_b_f = 4.0 + nrm((L, FOX_HEADS), 0.5)
    mla_q_norm = gain((L, MLA_Q_RANK))
    mla_w_uq = nrm((L, MLA_Q_RANK, MLA_HEADS * MLA_QK_DIM), MLA_Q_RANK ** -0.5)
    mla_kv_norm = gain((L, MLA_KV_RANK))
    mla_w_ukv = nrm((L, MLA_KV_RANK, MLA_HEADS * (MLA_NOPE_DIM + MLA_V_DIM)), MLA_KV_RANK ** -0.5)
    dn_conv_w = nrm((L, DN_CONV_WIDTH, 3 * DN_WIDTH), DN_CONV_WIDTH ** -0.5)
    dn_a_log = jnp.log(jax.random.uniform(next(ks), (L, DN_HEADS), f32, 1.0, 16.0))
    dt = jnp.exp(jax.random.uniform(next(ks), (L, DN_HEADS), f32,
                                    float(np.log(1e-3)), float(np.log(1e-1))))
    dn_dt_bias = dt + jnp.log(-jnp.expm1(-dt))
    dn_o_norm = gain((L, DN_HEAD_DIM))
    w_br_fox = nrm((L, FOX_WIDTH, D_MODEL), FOX_WIDTH ** -0.5)
    w_br_mla = nrm((L, MLA_WIDTH, D_MODEL), MLA_WIDTH ** -0.5)
    w_br_dn = nrm((L, DN_WIDTH, D_MODEL), DN_WIDTH ** -0.5)
    w_out = nrm((L, D_MODEL, D_MODEL), D_MODEL ** -0.5)
    ffn2_norm = gain((L, D_MODEL))
    ffn2_w_gu = nrm((L, D_MODEL, 2 * D_FF), D_MODEL ** -0.5)
    ffn2_w_down = nrm((L, D_FF, D_MODEL), D_FF ** -0.5)
    final_norm = gain((D_MODEL,))
    return {'x': x, 'positions': positions,
            'ffn1_norm': ffn1_norm, 'ffn1_w_gu': ffn1_w_gu, 'ffn1_w_down': ffn1_w_down,
            'mix_norm': mix_norm, 'w_in': w_in, 'b_gate': b_gate, 'fox_b_f': fox_b_f,
            'mla_q_norm': mla_q_norm, 'mla_w_uq': mla_w_uq, 'mla_kv_norm': mla_kv_norm, 'mla_w_ukv': mla_w_ukv,
            'dn_conv_w': dn_conv_w, 'dn_a_log': dn_a_log, 'dn_dt_bias': dn_dt_bias, 'dn_o_norm': dn_o_norm,
            'w_br_fox': w_br_fox, 'w_br_mla': w_br_mla, 'w_br_dn': w_br_dn, 'w_out': w_out,
            'ffn2_norm': ffn2_norm, 'ffn2_w_gu': ffn2_w_gu, 'ffn2_w_down': ffn2_w_down,
            'final_norm': final_norm}

def second_block(x, positions, ffn1_norm, ffn1_w_gu, ffn1_w_down, mix_norm, w_in, b_gate, fox_b_f,
              mla_q_norm, mla_w_uq, mla_kv_norm, mla_w_ukv, dn_conv_w, dn_a_log, dn_dt_bias, dn_o_norm,
              w_br_fox, w_br_mla, w_br_dn, w_out, ffn2_norm, ffn2_w_gu, ffn2_w_down, final_norm):
    cos, sin = rope_tables(positions)
    for l in range(DEPTH):
        x = x + 0.5 * swiglu(rmsnorm(x, ffn1_norm[l]), ffn1_w_gu[l], ffn1_w_down[l])
        x = x + hybrid_mixer(rmsnorm(x, mix_norm[l]), cos, sin, w_in[l], b_gate[l], fox_b_f[l],
                             mla_q_norm[l], mla_w_uq[l], mla_kv_norm[l], mla_w_ukv[l],
                             dn_conv_w[l], dn_a_log[l], dn_dt_bias[l], dn_o_norm[l],
                             w_br_fox[l], w_br_mla[l], w_br_dn[l], w_out[l])
        x = x + 0.5 * swiglu(rmsnorm(x, ffn2_norm[l]), ffn2_w_gu[l], ffn2_w_down[l])
    return rmsnorm(x, final_norm)


def setup_inputs(seed=0):
    out = dict(first_inputs(seed))
    for name, value in second_inputs(seed + 1).items():
        if name != "x":
            out[name + "_2"] = value
    return out


def reference(
    x, norm_g, w_in, attn_lambda, attn_subln_g, conv_w, w_branch, w_out, final_norm_g,
    positions_2, ffn1_norm_2, ffn1_w_gu_2, ffn1_w_down_2, mix_norm_2, w_in_2, b_gate_2,
    fox_b_f_2, mla_q_norm_2, mla_w_uq_2, mla_kv_norm_2, mla_w_ukv_2, dn_conv_w_2, dn_a_log_2,
    dn_dt_bias_2, dn_o_norm_2, w_br_fox_2, w_br_mla_2, w_br_dn_2, w_out_2, ffn2_norm_2,
    ffn2_w_gu_2, ffn2_w_down_2, final_norm_2,
):
    x = first_block(
        x, norm_g, w_in, attn_lambda, attn_subln_g, conv_w, w_branch, w_out, final_norm_g,
    )
    return second_block(
        x, positions_2, ffn1_norm_2, ffn1_w_gu_2, ffn1_w_down_2, mix_norm_2, w_in_2, b_gate_2,
        fox_b_f_2, mla_q_norm_2, mla_w_uq_2, mla_kv_norm_2, mla_w_ukv_2, dn_conv_w_2,
        dn_a_log_2, dn_dt_bias_2, dn_o_norm_2, w_br_fox_2, w_br_mla_2, w_br_dn_2, w_out_2,
        ffn2_norm_2, ffn2_w_gu_2, ffn2_w_down_2, final_norm_2,
    )


_drawn_inputs = setup_inputs


def setup_inputs(seed=0):
    import zlib

    import numpy as np

    out = dict(_drawn_inputs(seed))
    spreads = {}
    factors = {'attn_lambda': 2.945,
     'attn_subln_g': 99.177,
     'final_norm_g': 124.15,
     'b_gate_2': 8.209,
     'mla_q_norm_2': 35.2,
     'ffn1_norm_2': 3.762,
     'fox_b_f_2': 41.784,
     'dn_o_norm_2': 24.822,
     'ffn2_norm_2': 3.876,
     'mix_norm_2': 3.025,
     'mla_kv_norm_2': 8.0,
     'dn_a_log_2': 2.771,
     'w_br_fox_2': 6.742}
    for name, (base, spread) in spreads.items():
        noise = np.random.default_rng([zlib.crc32(name.encode()), seed]).standard_normal(out[name].shape)
        drawn = base * np.exp(spread * noise) if base else spread * noise
        out[name] = jnp.asarray(drawn.astype(out[name].dtype))
    for name, factor in factors.items():
        out[name] = (out[name] * factor).astype(out[name].dtype)
    return out
```

```python
import math
from contextlib import ExitStack

import numpy as np

import concourse.bass as bass
from concourse import mybir
from concourse.alu_op_type import AluOpType as ALU

F32 = mybir.dt.float32
I32 = mybir.dt.int32
ACT = mybir.ActivationFunctionType
X = mybir.AxisListType.X

P = 128
SEQ = 256
TT = SEQ // P
DM = 1024
KD = DM // P
DEPTH = 2
EPS = 1e-6
NEG = -1e30

A_HEADS, A_QK, A_V, A_ROT = 4, 64, 128, 16
R_HEADS, R_QK, R_V = 4, 64, 128
IN1 = 8704
D_FF = 2816
FT = D_FF // P
FOX_H, MLA_H, DN_H, HD = 8, 8, 8, 64
M_QR, M_KVR, M_ROPE, M_QK = 256, 128, 32, 96
IN2 = 7096
CHUNK = 64

RING = 4
SLOT = 4096


def norm_steps(m):
    return [("norm", m, t, half) for t in range(TT) for half in range(2)]


def dense(a, b):
    return [("d", o) for o in range(a, b)]


def merge(*streams):
    at, out = [0] * len(streams), []
    total = sum(map(len, streams))
    for _ in range(total):
        i = min((k for k in range(len(streams)) if at[k] < len(streams[k])),
                key=lambda k: (at[k] + 1) / len(streams[k]))
        out.append(streams[i][at[i]])
        at[i] += 1
    return out


def attention_slots(kind):
    slots = []
    for s in range(10):
        if s < 8:
            slots.append(("S", kind, s))
        if 0 <= s - 1 < 8:
            slots.append(("T", kind, s - 1))
        if 0 <= s - 2 < 8:
            slots.append(("V", kind, s - 2))
        if s - 2 in (3, 7):
            slots.append(("F", kind, (s - 2) // 4))
        if s - 3 == 3:
            slots.append(("F2", kind, 0))
    return slots + [("F2", kind, 1), ("FT", kind, 0), ("FT", kind, 1)]


STEPS1 = (
    norm_steps(0) + dense(0, 6) + [("AT", 0), ("d", 6), ("AT", 1), ("d", 7), ("RT", 0), ("d", 8), ("RT", 1)]
    + merge(attention_slots("diff"), dense(9, 28))
    + merge([("RI", 0), ("RK",), ("RI", 1), ("RV", 0), ("RC",), ("RF", 0), ("RV", 1),
             ("RF2", 0), ("RF", 1)], dense(28, 34))
    + [("br", 1, jp) for jp in range(4)] + [("br", 0, 0), ("RFT", 0), ("RF2", 1), ("br", 0, 1), ("br", 0, 2), ("RFT", 1), ("br", 0, 3)]
    + [("br", 2, jp) for jp in range(4)] + [("wo", q) for q in range(4)]
)


def ffn_steps(f):
    out = []
    for j in range(FT):
        out.append(("gu", f, j))
        if j >= 5 and (j - 5) % 4 == 0:
            out.append(("dn", f, (j - 5) // 4))
    return out + [("dn", f, FT // 4)]


def delta_steps(t):
    out = [("DT", t, s) for s in range(3)] + [("DP", t), ("DG", t), ("R1", t, 0), ("R1", t, 1), ("DP2", t)]
    out += [("DX", t, s, g) for s in range(3) for g in range(2)]
    for name in ("QK", "K1", "L1"):
        out += [(name, t, g) for g in range(2)]
    for b in (2, 4, 8, 16):
        out += [("Y", t, b, g) for g in range(2)] + [("Z", t, b, g) for g in range(2)]
    out += [("Y", t, 32, g) for g in range(2)] + [("ZT", t, g) for g in range(2)]
    out += [("W", t, g) for g in range(2)] + [("U", t)]
    if t:
        out.append(("DF2", t - 1))
    for c in range(2):
        out += [("X1", t, c), ("X2", t, c)]
        if (t, c) != (TT - 1, 1):
            out += [("X3", t, c)]
    return out + [("IN", t), ("DF", t)]


STEPS2 = (
    norm_steps(0) + ffn_steps(0) + norm_steps(1)
    + dense(0, 4) + [("SM",)] + dense(4, 6) + [("FC",), ("MC", 0), ("d", 6), ("MC", 1), ("d", 7)]
    + merge(attention_slots("fox"), dense(8, 14))
    + [("u", t, i) for t in range(TT) for i in range(4)]
    + [("MT", t, w, half) for t in range(TT) for w in range(2) for half in range(2)]
    + merge(attention_slots("mla"), dense(14, 16))
    + merge(delta_steps(0) + delta_steps(1),
            dense(16, 28) + [("br", i, jp) for i in (0, 1) for jp in range(4)])
    + [("DFT", 0), ("DF2", 1), ("DFT", 1)]
    + [("br", 2, jp) for jp in range(4)] + [("wo", q) for q in range(4)]
    + norm_steps(2) + ffn_steps(1)
)


def banks_of(blk, step):
    k = step[0]
    if k in ("d", "u", "br", "wo"):
        return ["dense"]
    if k == "gu":
        return ["dense"]
    if k == "norm":
        return [4 + 2 * step[2] + step[3]]
    if k == "dn":
        return [4, 5, 6, 7] if step[2] == 0 else []
    if k == "S":
        return [4, 5]
    if k in ("T", "FT", "RFT", "DFT"):
        return [6]
    if k == "V":
        return [7]
    if k in ("R1", "QK", "K1", "L1", "Y", "W"):
        return [4 + step[-1]]
    if k in ("DX", "MT", "ZT"):
        return [6 + step[-1]]
    if k == "Z":
        return [6 + step[-1], 4 + step[-1]]
    return {"AT": [6, 7], "RT": [7], "RI": [4, 5], "RK": [6], "RV": [7], "RC": [4, 5], "FC": [7],
            "MC": [7], "DT": [6], "DG": [7], "U": [6], "X1": [4], "X2": [5], "X3": [6],
            "IN": [7]}.get(k, [])


def piece_of(blk, step):
    k = step[0]
    if k == "d":
        return ("in", step[1] // 2)
    if k == "br":
        return ("br", step[1])
    if k == "wo":
        return ("wo", step[1])
    if k == "u":
        return ("u",)
    if k == "gu":
        return ("gu", step[1], step[2] // 2)
    if k == "dn":
        return ("down", step[1], step[2])
    return None


class Plan:

    def __init__(self, blk, steps):
        self.steps, self.uses, self.dense_uses = steps, {}, 0
        self.per_layer = [0] * 8
        self.filled_extra = {}
        self.pieces, self.slot, self.last = [], {}, {}
        for s in steps:
            got = []
            for b in banks_of(blk, s):
                if b == "dense":
                    b = self.dense_uses % 4
                    self.dense_uses += 1
                got.append((b, self.per_layer[b]))
                self.per_layer[b] += 1
            self.uses[s] = got
            p = piece_of(blk, s)
            if p is not None:
                if p not in self.slot:
                    self.slot[p] = len(self.pieces) % RING
                    self.pieces.append(p)
                self.last[p] = s
        assert len(self.pieces) % RING == 0, len(self.pieces)


PLANS = [Plan(0, STEPS1), Plan(1, STEPS2)]


def shape_constants():
    f = np.float32
    i, j = np.arange(P)[:, None], np.arange(P)[None, :]
    cols, at = [], {}

    def add(name, a):
        a = np.asarray(a, np.float64).astype(f).reshape(P, -1)
        at[name] = (sum(c.shape[1] for c in cols), a.shape[1])
        cols.append(a)

    add("ident", np.eye(P))
    add("causal", np.concatenate([np.zeros((P, P)), np.where(j > i, NEG, 0.0)], 1))
    for b in (1, 2, 4, 8, 16, 32):
        add(f"below{b}", -1.0 * ((i // (2 * b) == j // (2 * b)) & (j % (2 * b) >= b) & (i % (2 * b) < b)))
    same = i // CHUNK == j // CHUNK
    add("decay_mask", np.where((j >= i) & same, 0.0, NEG))
    add("tri", 1.0 * (i <= j))
    add("tri_chunk", 1.0 * ((i <= j) & same))
    add("same_chunk", 1.0 * same)
    add("ones", np.ones((P, P)))
    log_g = np.log(1.0 - 2.0 ** (-5.0 - np.arange(R_HEADS)))
    add("ret_decay", np.stack([np.where(j >= i, np.exp(np.maximum(j - i, 0) * g), 0.0) for g in log_g], 1))
    add("zeta", np.exp((P - 1 - np.arange(P))[:, None] * log_g[None]))
    add("xi", np.exp((np.arange(P) + 1.0)[:, None] * log_g[None]))
    pos = np.arange(SEQ, dtype=f).reshape(TT, P)
    inv = (500000.0 ** (-np.arange(0, A_ROT, 2) / A_ROT)).astype(f)
    ang = (pos[..., None] * inv).astype(f).astype(np.float64).transpose(1, 0, 2)
    add("rope_cos", np.concatenate([np.cos(ang)] * 2, -1))
    add("rope_nsin", -np.sin(ang))
    add("rope_sin", np.sin(ang))
    inv = (1.0 / (10000.0 ** np.linspace(0.0, 1.0, R_QK // 2))).astype(f)
    ang = (pos[..., None] * inv).astype(f).astype(np.float64).transpose(1, 0, 2)
    k_scale = np.array([1.0, R_QK ** -0.5])[None, None, :, None]
    add("ret_cos", np.concatenate([np.cos(ang)] * 2, -1)[:, :, None] * k_scale)
    add("ret_nsin", -np.sin(ang)[:, :, None] * k_scale)
    add("ret_sin", np.sin(ang)[:, :, None] * k_scale)
    add("inv_freq", np.tile((10000.0 ** (-np.arange(M_ROPE // 2) / (M_ROPE // 2))).astype(f), (P, 1)))
    add("minus_half", np.full((P, 8), -0.5))
    add("eps", np.full((P, 8), EPS))
    return np.concatenate(cols, 1), at


CONSTS, CONST_AT = shape_constants()

ROWS1 = [("norm_g", 8), ("conv_w", 12)]
ROWS2 = [("ffn1_norm_2", 8), ("mix_norm_2", 8), ("ffn2_norm_2", 8), ("b_gate_2", 24),
         ("dn_conv_w_2", 48), ("mla_q_norm_2", 2), ("mla_kv_norm_2", 1)]
NR1, NR2 = sum(n for _, n in ROWS1), sum(n for _, n in ROWS2)
PAR1 = {"norm_g": 0, "conv_w": 8, "neg_lam": NR1, "subln": NR1 + 1}
NP1 = NR1 + 1 + A_V
PAR2 = {"ffn1_norm_2": 0, "mix_norm_2": 8, "ffn2_norm_2": 16, "b_gate_2": 24, "dn_conv_w_2": 48,
        "mla_q_norm_2": 96, "mla_kv_norm_2": 98, "f_bias": NR2, "dt_bias": NR2 + 8, "neg_a": NR2 + 16,
        "o_norm": NR2 + 24}
NP2 = NR2 + 24 + HD

LAMBDA_INIT = [0.8 - 0.6 * math.exp(-0.3 * layer) for layer in range(DEPTH)]


def build(nc, a, out):
    stack = ExitStack()
    with stack:
        def sb(name, n, dt=F32):
            return stack.enter_context(nc.sbuf_tensor(name, [P, n], dt))

        def v(ap, **kw):
            names = list(kw)
            return ap.rearrange("p (%s) -> p %s" % (" ".join(names), " ".join(names)),
                                **{n: kw[n] for n in names[:-1]})

        const = sb("const", CONSTS.shape[1])

        def cst(name):
            o, n = CONST_AT[name]
            return const[:, o:o + n]

        ident = cst("ident")
        x = sb("x", TT * DM)
        xv = v(x[:, :], t=TT, n=DM)
        hT_ = sb("hT", KD * SEQ)
        hT = v(hT_[:, :], k=KD, n=SEQ)
        merged = hT
        ring = sb("ring", RING * SLOT)

        def slot(n):
            return ring[:, n * SLOT:(n + 1) * SLOT]

        gates_ = sb("gates", 3 * KD * SEQ)
        gates = v(gates_[:, :], i=3, j=KD, n=SEQ)
        xs = v(gates_[:, 0:TT * DM], t=TT, n=DM)
        squares = v(gates_[:, 2048:4096], t=TT, n=DM)
        hid = v(gates_[:, 0:8 * SEQ], j=8, n=SEQ)
        ffn_tanh = v(gates_[:, 2048:2048 + 4 * SEQ], j=4, n=SEQ)
        ffn_gate = v(gates_[:, 3072:3072 + 4 * SEQ], j=4, n=SEQ)
        final_gain = gates_[:, 4096:4096 + DM]
        par1 = v(sb("par1", DEPTH * NP1)[:, :], l=DEPTH, n=NP1)
        par2 = v(sb("par2", DEPTH * NP2)[:, :], l=DEPTH, n=NP2)
        par = sb("par", max(NP1, NP2))
        stat = sb("stat", 8)
        pos_tab = sb("pos_tab", TT * 64)
        pcos = v(pos_tab[:, 0:64], t=TT, n=32)
        pnsin = v(pos_tab[:, 64:96], t=TT, n=16)
        psin = v(pos_tab[:, 96:128], t=TT, n=16)

        SCRATCH = 22200
        stat_all = sb("stat_all", 40)
        stat2 = sb("stat2", 48)
        x_ss, x_var, x_rstd = stat_all[:, 24:26], stat_all[:, 26:28], stat_all[:, 28:30]
        neg_half = cst("minus_half")
        scratch = sb("scratch", SCRATCH)

        class Room:

            def __init__(self, memory, size, at=0):
                self.memory, self.size, self.at = memory, size, at

            def take(self, **kw):
                n = math.prod(kw.values())
                assert self.at + n <= self.size, (self.at, n, self.size)
                view = self.memory[:, self.at:self.at + n]
                self.at += n
                return v(view, **kw) if len(kw) > 1 else view

        def par_(name, n, table):
            return par[:, table[name]:table[name] + n]

        r = Room(scratch, SCRATCH)
        fox_T = r.take(j=4, n=SEQ)
        mla_T = r.take(j=4, n=SEQ)
        conv_y = r.take(s=3, j=4, n=SEQ)
        dz = r.take(t=TT, n=512)
        small = Room(scratch, SCRATCH, r.at)
        r.at += 640
        delta_from = r.at
        at_sc = r.take(u=2, c=2, n=SEQ)
        at_wT = r.take(u=2, n=2 * SEQ)
        at_bias = r.take(u=2, c=2)
        at_max = r.take(u=2, c=2)
        at_sum = r.take(t=TT, h=8)
        at_rcp = r.take(t=TT, h=8)
        at_o = r.take(t=TT, n=512)
        at_sq = r.take(n=512)
        th = r.take(u=2, n=512)
        attention_to = r.at
        fqT = r.take(j=4, n=SEQ)
        fkT = r.take(j=4, n=SEQ)
        fv = r.take(t=TT, n=512)
        craw = r.take(u=2, j=2, n=SEQ)
        both = v(scratch[:, attention_to:attention_to + 4096], w=2, h=8, n=SEQ)
        mqkT = both
        neg_c = r.take(n=SEQ)
        mv = r.take(t=TT, n=512)
        g = Room(gates_, 3 * KD * SEQ)
        mraw = g.take(t=TT, n=440)
        cT3 = g.take(j=3, n=SEQ)
        mqk = g.take(w=2, t=TT, n=MLA_H * M_QK)
        m_rope_a = g.take(n=256)
        m_rope_b = g.take(n=256)
        z = small.take(t=TT, n=16)
        z_abs = small.take(t=TT, n=16)
        z_log = small.take(t=TT, n=16)
        beta_t = small.take(t=TT, n=8)
        beta = small.take(t=TT, n=8)
        half_beta = small.take(t=TT, n=8)
        log_f = small.take(t=TT, n=8)
        dgate = small.take(t=TT, n=8)
        m_ss = small.take(t=TT, n=2)
        m_rstd = small.take(t=TT, n=2)
        gc = small.take(n=24)
        eg = small.take(n=16)
        gl_raw = small.take(c=2, h=8)
        gl = small.take(c=2, h=8)
        gc_rows = small.take(n=P)
        d_ss = small.take(n=16)
        d_rs = small.take(n=16)
        r = Room(scratch, SCRATCH, delta_from)
        d_tok = r.take(s=3, n=512)
        d_kb = r.take(n=512)
        d_w = r.take(n=512)
        d_vb = r.take(n=512)
        d_kdec = r.take(n=512)
        d_T3 = r.take(s=3, h=8, n=P)
        d_decay = r.take(h=8, n=P)
        d_M = r.take(h=8, n=P)
        d_QK = r.take(h=8, n=P)
        d_inv = r.take(h=8, n=P)
        d_invT = r.take(h=8, n=P)
        d_wT = r.take(h=8, n=P)
        d_S = r.take(n=512)
        d_S1 = r.take(n=512)
        d_cross = r.take(n=512)
        br_tmp2 = r.take(u=2, n=512)
        d_sq, d_o = d_S1, d_cross
        d_C = d_decay
        d_Y = d_T3[:, 2]
        d_u = d_kb
        d_vn = d_tok[:, 0]
        dn_T = conv_y[:, 0]
        r = Room(scratch, SCRATCH, attention_to)
        at_w = r.take(u=2, n=SEQ)
        aqk = r.take(t=TT, n=1024)
        rqk = r.take(t=TT, n=512)
        av = r.take(t=TT, n=512)
        rv = r.take(t=TT, n=512)
        az = r.take(t=TT, n=512)
        r = Room(scratch, SCRATCH)
        aqT = r.take(j=4, n=SEQ)
        akT = r.take(j=4, n=SEQ)
        rqkT = r.take(j=4, n=SEQ)
        cu = r.take(j=4, n=SEQ)
        cy = r.take(j=4, n=SEQ)
        rz = r.take(t=TT, n=512)
        assert r.at <= delta_from
        r = Room(scratch, SCRATCH, attention_to + 512 + 2048 + 4096)
        kz = r.take(n=256)
        r_state = r.take(n=256)
        rope_a = r.take(n=512)
        rope_b = r.take(n=512)
        th_c = r.take(u=2, n=512)
        inner = v(aqk[:, 0], t=TT, n=512)
        r_cross = aqk[:, 1, 0:512]
        r_sq = aqk[:, 1, 512:1024]
        r_o = rqk
        br_tmps = v(scratch[:, delta_from:delta_from + 1024], u=2, n=512), br_tmp2
        aT, rT, cT = aqT, akT, cu
        a_ss = stat_all[:, 8:16]
        a_rs = stat_all[:, 16:24]
        r_ss2, r_rs2 = stat2[:, 0:8], stat2[:, 8:16]
        d_ss2, d_rs2 = stat2[:, 16:32], stat2[:, 32:48]
        m_junk = g.take(t=TT, n=M_QR + M_KVR)
        g0 = Room(gates_, 3 * KD * SEQ, 4096)
        par_rows = g0.take(i=2 * DEPTH, n=P)
        lam_rows = g0.take(n=DEPTH * 4 * A_QK)
        lam_p = g0.take(l=DEPTH, r=2, d=A_QK)
        lam_s = g0.take(l=DEPTH, r=2)
        lam_e = g0.take(l=DEPTH, r=2)
        pos_f = g0.take(t=TT, o=1).rearrange("p t o -> p (t o)")
        ang = g0.take(t=TT, n=M_ROPE // 2)
        turns = g0.take(i=2, t=TT, n=M_ROPE // 2)
        trig = g0.take(i=2, t=TT, n=M_ROPE // 2)
        pos_i = sb("pos_i", TT, I32)

        bank = [stack.enter_context(nc.psum_tensor(f"bank{b}", [P, 512], F32)) for b in range(8)]

        class Signal:
            def __init__(self, name, k1=0, k2=0, before=0, between=0):
                self.sem = stack.enter_context(nc.semaphore(name))
                self.k, self.start = (k1, k2), (before, before + DEPTH * k1 + between)

            def __call__(self, L, n):
                blk, l = L
                if self.k[blk] == 0:
                    return self.sem, self.start[blk] + n
                return self.sem, l * self.k[blk] + (self.start[blk] + n)

        filled_ = [Signal(f"filled{b}", *(p.per_layer[b] for p in PLANS)) for b in range(8)]
        drained_ = [Signal(f"drained{b}", *(p.per_layer[b] for p in PLANS)) for b in range(8)]

        def filled(L, step, j=0):
            b, n = PLANS[L[0]].uses[step][j]
            return filled_[b](L, n + 1)

        def drained(L, step, j=0):
            b, n = PLANS[L[0]].uses[step][j]
            return drained_[b](L, n + 1)

        def bank_of(L, step, j=0):
            return bank[PLANS[L[0]].uses[step][j][0]]

        def fills(L, step, j=0):
            return filled_[PLANS[L[0]].uses[step][j][0]].sem

        def drains(L, step, j=0):
            return drained_[PLANS[L[0]].uses[step][j][0]].sem

        def piece_dmas(piece):
            kind = piece[0]
            if kind == "gu":
                f, i = piece[1:]
                w = f"ffn{f + 1}_w_gu_2"
                return [(w, 0, KD, 256 * i, 256, 0, 512), (w, 0, KD, D_FF + 256 * i, 256, 256, 512)]
            if kind == "down":
                f, d = piece[1:]
                return [(f"ffn{f + 1}_w_down_2", 512 * d, min(4, FT - 4 * d), 0, DM, 0, DM)]
            return None

        def dmas_of(blk, piece):
            kind = piece[0]
            if kind in ("gu", "down"):
                return piece_dmas(piece)
            if blk == 0:
                if kind == "in":
                    start = [0, 512, 4096, 1024, 4608, 1536, 5120, 2048, 3072, 2560, 3584]
                    n = piece[1]
                    return [("w_in", 0, KD, start[n] if n < 11 else 5632 + 512 * (n - 11), 512, 0, 512)]
                if kind == "br":
                    return [("w_branch", piece[1], 4, 0, DM, 0, DM)]
                return [("w_out", 0, KD, 256 * piece[1], 256, 0, 256)]
            if kind == "in":
                n = piece[1]
                if n == 0:
                    return [("w_in_2", 0, KD, 1536, 424, 0, 440), ("w_in_2", 0, KD, 4008, 16, 424, 440)]
                start = [None, 0, 512, 1024, 1960, 2472, 2984, 3496]
                return [("w_in_2", 0, KD, start[n] if n < 8 else 4024 + 512 * (n - 8), 512, 0, 512)]
            if kind == "u":
                return [("mla_w_uq_2", 0, 2, 0, 768, 0, 768), ("mla_w_ukv_2", 0, 1, 0, 1024, 1536, 1024)]
            if kind == "br":
                return [(("w_br_fox_2", "w_br_mla_2", "w_br_dn_2")[piece[1]], 0, 4, 0, DM, 0, DM)]
            return [("w_out_2", 0, KD, 256 * piece[1], 256, 0, 256)]

        landed_count = [{}, {}]
        slot_total = [[0] * RING, [0] * RING]
        for blk in range(2):
            for piece in PLANS[blk].pieces:
                s = PLANS[blk].slot[piece]
                slot_total[blk][s] += 16 * len(dmas_of(blk, piece))
                landed_count[blk][piece] = slot_total[blk][s]
        landed_ = [Signal(f"weights_landed{s}", slot_total[0][s], slot_total[1][s]) for s in range(RING)]

        def landed(L, piece):
            return landed_[PLANS[L[0]].slot[piece]](L, landed_count[L[0]][piece])

        def weights(L, piece):
            return slot(PLANS[L[0]].slot[piece])

        x_new = Signal("x_new", 1, 3, before=1, between=1)
        ss_done = Signal("ss_done", 2, 6)
        rstd_done = Signal("rstd_done", 1, 3)
        xs_done = Signal("xs_done", 2, 6)
        end_ss = Signal("end_ss", 0, 0)
        end_rstd = Signal("end_rstd")
        end_gain = Signal("end_gain")
        end_out = Signal("end_out")
        bias_done = Signal("bias_done", 8, 16)
        exp_done = Signal("exp_done", 16, 32)
        mix_done = Signal("mix_done", 8, 0)
        o_var = Signal("o_var", 4, 0)
        o_rstd = Signal("o_rstd", 4, 0)
        o_done = Signal("o_done", 4, 6)
        tanh_done = Signal("tanh_done", 6, 2)
        par_done = Signal("par_done", 1, 1)
        roped = Signal("roped", 5, 0)
        c_done = Signal("c_done", 2, 0)
        added = Signal("added", 8, 8)
        ffn_tanh_done = Signal("ffn_tanh_done", 0, 2 * FT)
        hid_used = Signal("hid_used", 0, 2 * (FT // 4))
        craw_done = Signal("craw_done", 0, 6)
        taps_done = Signal("taps_done", 0, 6)
        ctanh_done = Signal("ctanh_done", 0, 6)
        conv2_done = Signal("conv2_done", 0, 6)
        z_done = Signal("z_done", 0, 1)
        zlog_done = Signal("zlog_done", 0, 1)
        small_done = Signal("small_done", 0, 1)
        m_ss_done = Signal("m_ss_done", 0, 1)
        m_norm_done = Signal("m_norm_done", 0, 2)
        m_roped = Signal("m_roped", 0, 2)
        dlt_done = Signal("dlt_done", 0, 2)
        eg_done = Signal("eg_done", 0, 2)
        l2_var = Signal("l2_var", 0, 2)
        l2_rstd = Signal("l2_rstd", 0, 2)
        kn_done = Signal("kn_done", 0, 2)
        kw_done = Signal("kw_done", 0, 2)
        arg_done = Signal("arg_done", 0, 4)
        decay_done = Signal("decay_done", 0, 4)
        inv2_done = Signal("inv2_done", 0, 4)
        level_done = Signal("level_done", 0, 20)
        state_zero = Signal("state_zero", 0, 1)
        dn_var = Signal("dn_var", 0, 2)
        dn_rstd = Signal("dn_rstd", 0, 2)
        setup_dma = Signal("setup_dma")
        setup_x = Signal("setup_x")
        setup_pe = Signal("setup_pe")
        setup_act = Signal("setup_act")
        setup_dve = Signal("setup_dve")

        setup_shared = Signal("setup_shared")
        setup_chain = stack.enter_context(nc.semaphore("setup_chain"))
        end_var = stack.enter_context(nc.semaphore("end_var"))
        stored = stack.enter_context(nc.semaphore("stored"))
        waits_met = stack.enter_context(nc.semaphore("waits_met"))
        pool_half = stack.enter_context(nc.semaphore("pool_half"))
        ROWS_LANDED = 16 * (1 + DEPTH * (len(ROWS1) + len(ROWS2)))
        FOX_DONE = 4

        class Chain:

            def __init__(self, name, k1, k2, before):
                self.links = Signal(name, k1, k2, before=before)
                self.n, self.before = 0, before

            def layer(self, eng, L):
                self.eng, self.L, self.n = eng, L, 0

            def link(self, ins):
                self.n += 1
                ins.then_inc(self.links.sem, 1)
                self.eng.wait_ge(*self.links(self.L, self.n))

            def end(self):
                k = self.links.k[self.L[0]]
                assert self.n < k, (self.n, k)
                self.eng.sem_inc(self.links.sem, k - self.n)

        block = stack.enter_context(nc.Block())
        dve_chain = Chain("dve_chain", 120, 300, 0)
        pool_chain = Chain("pool_chain", 60, 100, 0)
        act_chain = Chain("act_chain", 10, 10, 0)
        def layers(eng, blk, layer):
            with eng.Fori(0, DEPTH) as l:
                layer((blk, l))

        def of_layer(t, l):
            if isinstance(l, int):
                return t[l]
            names = " ".join("abcd"[:len(t.shape) - 1])
            first = names.split()[0]
            return t[bass.ds(l, 1)].rearrange(f"o {names} -> (o {first}){names[1:]}")

        def half(t, i):
            return t[:, i * 512:(i + 1) * 512]

        FOX_SCALE = HD ** -0.5

        @block.sync
        def _(sp):
            sp.dma_start(const[:, :], a["consts"][:, :]).then_inc(setup_dma.sem, 16)
            for i, (names, n) in enumerate(((ROWS1, NR1), (ROWS2, NR2))):
                for l in range(DEPTH):
                    at = 0
                    for name, rows in names:
                        src = a[name][l]
                        if len(src.shape) == 2:
                            src = src.rearrange("w c -> (w c)")
                        sp.dma_start(par_rows[at:at + rows, 2 * i + l, :],
                                     src.rearrange("(r c) -> r c", c=P)).then_inc(setup_dma.sem, 16)
                        at += rows
            sp.dma_start(xv, a["x"][0].rearrange("(t p) n -> p t n", p=P)).then_inc(setup_x.sem, 16)

            def load(L, piece):
                blk, l = L
                room = weights(L, piece)
                for name, row, tiles, col, n, to, width in dmas_of(blk, piece):
                    src = a[name]
                    if name == "w_branch":
                        src = src.rearrange("l b r c -> l (b r) c")
                        row = row * 512
                    src = of_layer(src, l)[row:row + tiles * P, col:col + n].rearrange("(k p) c -> p k c", p=P)
                    base = to if name == "mla_w_ukv_2" else 0
                    dst = v(room[:, base:base + tiles * width], k=tiles, n=width)
                    dst = dst[:, :, 0:n] if base else dst[:, :, to:to + n]
                    sp.dma_start(dst, src).then_inc(landed_[PLANS[blk].slot[piece]].sem, 16)

            def used(L, piece):
                step = PLANS[L[0]].last[piece]
                if step[0] == "dn" and step[2] < FT // 4:
                    return hid_used(L, step[1] * (FT // 4) + step[2] + 1)
                return filled(L, step, len(PLANS[L[0]].uses[step]) - 1) if step[0] != "dn" else \
                    filled(L, ("dn", step[1], 0), 3)

            def head(L, before):
                for n, piece in enumerate(PLANS[L[0]].pieces[:RING]):
                    if before is not None:
                        sp.wait_ge(*used(before, PLANS[before[0]].pieces[n - RING]))
                    load(L, piece)

            def tail(L):
                pieces = PLANS[L[0]].pieces
                for n in range(RING, len(pieces)):
                    sp.wait_ge(*used(L, pieces[n - RING]))
                    load(L, pieces[n])

            head((0, 0), None)
            for blk in range(2):
                with sp.Fori(0, DEPTH - 1) as l:
                    tail((blk, l))
                    head((blk, l + 1), (blk, l))
                last = (blk, DEPTH - 1)
                tail(last)
                if blk == 0:
                    head((1, 0), last)
                sp.wait_ge(*drained(last, ("br", 2, 3)))
                if blk == 1:
                    sp.wait_ge(*xs_done(last, 6))
                gain = a["final_norm_g"] if blk == 0 else a["final_norm_2"]
                sp.dma_start(final_gain, gain.partition_broadcast(P)).then_inc(end_gain.sem, 16)
            for t in range(TT):
                sp.wait_ge(end_out.sem, TT + t + 1)
                sp.dma_start(out[0, t * P:(t + 1) * P, :], xs[:, t, :]).then_inc(stored, 16)
            sp.wait_ge(stored, 16 * TT)

        @block.tensor
        def _(pe):
            seen = set()

            def claim(L, step, j=0):
                b, n = PLANS[L[0]].uses[step][j]
                if n:
                    pe.wait_ge(*drained_[b](L, n))
                return bank[b]

            def arrived(L, piece):
                if piece not in seen:
                    seen.add(piece)
                    pe.wait_ge(*landed(L, piece))

            def stand_alone():
                pe.sem_inc(waits_met, 1)

            def tmajor(acc, lhs, rhs, n_k):
                for k in range(n_k):
                    mm = pe.matmul(acc, lhs(k), rhs(k), start=(k == 0), stop=(k == n_k - 1))
                return mm

            def turn(out_, in_):
                n = in_.shape[0]
                return pe.transpose(out_, in_, ident[0:n, 0:n])

            def norm(L, m, t, half_):
                acc = claim(L, ("norm", m, t, half_))
                if half_ == 0:
                    pe.wait_ge(*xs_done(L, 2 * m + t + 1))
                for i in range(4):
                    mm = turn(acc[:, i * P:(i + 1) * P], xs[:, t, (4 * half_ + i) * P:(4 * half_ + i + 1) * P])
                mm.then_inc(fills(L, ("norm", m, t, half_)), 1)

            def h_ready(L, m):
                for t in range(TT):
                    for h in range(2):
                        pe.wait_ge(*drained(L, ("norm", m, t, h)))

            def tokens_out(o, blk):
                return o // 2 < 7 if blk == 0 else o // 2 in (0, 3, 7)

            def d(L, o):
                step = ("d", o)
                if o == 0:
                    h_ready(L, 0 if L[0] == 0 else 1)
                arrived(L, ("in", o // 2))
                acc = claim(L, step)
                n = 440 if L[0] == 1 and o < 2 else 512
                w = v(weights(L, ("in", o // 2))[:, 0:KD * n], k=KD, n=n)
                if tokens_out(o, L[0]):
                    t = o % 2
                    mm = tmajor(acc[:, 0:n], lambda k: hT[:, k, t * P:(t + 1) * P], lambda k: w[:, k, :], KD)
                else:
                    for jj in range(2):
                        c = (2 * (o % 2) + jj) * P
                        mm = tmajor(acc[:, jj * SEQ:(jj + 1) * SEQ], lambda k: w[:, k, c:c + P],
                                    lambda k: hT[:, k, :], KD)
                mm.then_inc(fills(L, step), 1)

            def branch(L, i, jp):
                step = ("br", i, jp)
                if L[0] == 0:
                    if i == 1:
                        src = cT
                        if jp == 0:
                            pe.wait_ge(*c_done(L, 2))
                    else:
                        src = aT if i == 0 else rT
                        if jp == 0:
                            pe.wait_ge(*drained(L, ("FT", "diff", TT - 1) if i == 0 else ("RFT", TT - 1)))
                else:
                    src = (fox_T, mla_T, dn_T)[i]
                    if jp == 0:
                        pe.wait_ge(*drained(L, (("FT", "fox", TT - 1), ("FT", "mla", TT - 1), ("DFT", TT - 1))[i]))
                arrived(L, ("br", i))
                acc = claim(L, step)
                w = v(weights(L, ("br", i)), k=4, n=DM)
                for jj in range(2):
                    c = (2 * jp + jj) * P
                    mm = tmajor(acc[:, jj * SEQ:(jj + 1) * SEQ], lambda k: w[:, k, c:c + P],
                                lambda k: src[:, k, :], 4)
                mm.then_inc(fills(L, step), 1)

            def wo(L, q):
                step = ("wo", q)
                if q == 0:
                    pe.wait_ge(*added(L, 8))
                arrived(L, ("wo", q))
                acc = claim(L, step)
                w = v(weights(L, ("wo", q))[:, 0:KD * 256], k=KD, n=256)
                for t in range(TT):
                    mm = tmajor(acc[:, t * 256:(t + 1) * 256], lambda k: merged[:, k, t * P:(t + 1) * P],
                                lambda k: w[:, k, :], KD)
                mm.then_inc(fills(L, step), 1)

            def unit(kind, u):
                return u // 4, u % 4, u + 8 * (kind == "mla")

            def scores(L, kind, u):
                qb, pair, _ = unit(kind, u)
                n = (qb + 1) * P
                q_cols = slice(qb * P, (qb + 1) * P)
                if u % 4 == 0:
                    if kind == "diff":
                        for j in range(2):
                            pe.wait_ge(*drained(L, ("AT", qb), j))
                    elif kind == "fox" and u == 0:
                        for o in range(2, 6):
                            pe.wait_ge(*drained(L, ("d", o)))
                        pe.wait_ge(*drained(L, ("FC",)))
                    elif kind == "mla" and u == 0:
                        for h in range(2):
                            pe.wait_ge(*drained(L, ("MT", TT - 1, 1, h)))
                for c in range(2):
                    acc = claim(L, ("S", kind, u), c)
                    rows = slice(64 * c, 64 * c + 64)
                    if kind == "diff":
                        mm = pe.matmul(acc[:, 0:n], aqT[rows, pair, q_cols], akT[rows, pair, 0:n],
                                       start=True, stop=True)
                    elif kind == "fox":
                        pe.matmul(acc[:, 0:n], fqT[rows, pair, q_cols], fkT[rows, pair, 0:n],
                                  start=True, stop=False)
                        h = 2 * pair + c
                        mm = pe.matmul(acc[:, 0:n], ident[:, h:h + 1].to_broadcast([P, P]), neg_c[:, 0:n],
                                       start=False, stop=True)
                    else:
                        h = 2 * pair + c
                        mm = pe.matmul(acc[:, 0:n], mqkT[0:M_QK, 0, h, q_cols], mqkT[0:M_QK, 1, h, 0:n],
                                       start=True, stop=True)
                    mm.then_inc(fills(L, ("S", kind, u), c), 1)

            def probabilities_turned(L, kind, u):
                qb, pair, n_u = unit(kind, u)
                acc = claim(L, ("T", kind, u))
                nk = qb + 1
                if kind == "diff":
                    pe.wait_ge(*mix_done(L, n_u + 1))
                    for kb in range(nk):
                        mm = turn(acc[:, kb * P:(kb + 1) * P], at_w[:, u % 2, kb * P:(kb + 1) * P])
                else:
                    pe.wait_ge(*exp_done(L, 2 * n_u + 2))
                    for c in range(2):
                        for kb in range(nk):
                            to = (c * nk + kb) * P
                            mm = turn(acc[:, to:to + P], at_sc[:, u % 2, c, kb * P:(kb + 1) * P])
                mm.then_inc(fills(L, ("T", kind, u)), 1)

            def values(L, kind, u):
                qb, pair, _ = unit(kind, u)
                nk = qb + 1
                acc = claim(L, ("V", kind, u))
                pe.wait_ge(*drained(L, ("T", kind, u)))
                if u % 4 == 0:
                    pe.wait_ge(*drained(L, {"diff": ("d", 6 + qb), "fox": ("d", 6 + qb),
                                            "mla": ("u", qb, 3)}[kind]))
                    if kind == "mla":
                        pe.wait_ge(*drained(L, ("u", qb, 2)))
                if kind == "diff":
                    mm = tmajor(acc[:, 0:P], lambda kb: at_wT[:, u % 2, kb * P:(kb + 1) * P],
                                lambda kb: av[:, kb, pair * P:(pair + 1) * P], nk)
                else:
                    vals = fv if kind == "fox" else mv
                    for c in range(2):
                        h = 2 * pair + c
                        mm = tmajor(acc[:, c * HD:(c + 1) * HD],
                                    lambda kb: at_wT[:, u % 2, (c * nk + kb) * P:(c * nk + kb + 1) * P],
                                    lambda kb: vals[:, kb, h * HD:(h + 1) * HD], nk)
                mm.then_inc(fills(L, ("V", kind, u)), 1)

            def four_turned(L, step, src):
                acc = claim(L, step)
                for i in range(4):
                    mm = turn(acc[:, i * P:(i + 1) * P], src[:, i * P:(i + 1) * P])
                mm.then_inc(fills(L, step), 1)

            def result_turned(L, kind, qb):
                pe.wait_ge(*o_done(L, {"diff": 0, "fox": 0, "mla": 2}[kind] + qb + 1))
                four_turned(L, ("FT", kind, qb), at_o[:, qb])

            def a_turned(L, t):
                pe.wait_ge(*roped(L, t + 1))
                for j in range(2):
                    acc = claim(L, ("AT", t), j)
                    for i in range(4):
                        mm = turn(acc[:, i * P:(i + 1) * P], aqk[:, t, (4 * j + i) * P:(4 * j + i + 1) * P])
                    mm.then_inc(fills(L, ("AT", t), j), 1)

            def r_turned(L, t):
                pe.wait_ge(*roped(L, t + 3))
                four_turned(L, ("RT", t), rqk[:, t])

            def r_inner(L, t):
                pe.wait_ge(*drained(L, ("RT", t)))
                for par_h in range(2):
                    acc = claim(L, ("RI", t), par_h)
                    rows = slice(64 * par_h, 64 * par_h + 64)
                    for hh in range(2):
                        mm = pe.matmul(acc[:, hh * P:(hh + 1) * P], rqkT[rows, 2 + hh, t * P:(t + 1) * P],
                                       rqkT[rows, hh, t * P:(t + 1) * P], start=True, stop=True)
                    mm.then_inc(fills(L, ("RI", t), par_h), 1)

            def r_state_(L):
                acc = claim(L, ("RK",))
                pe.wait_ge(*roped(L, 5))
                pe.wait_ge(*drained(L, ("d", 8)))
                for h in range(R_HEADS):
                    rows = slice(64 * (h % 2), 64 * (h % 2) + 64)
                    mm = pe.matmul(acc[rows, (h // 2) * P:(h // 2 + 1) * P], kz[:, h * R_QK:(h + 1) * R_QK],
                                   rv[:, 0, h * P:(h + 1) * P], start=True, stop=True)
                mm.then_inc(fills(L, ("RK",)), 1)

            def r_values(L, t):
                acc = claim(L, ("RV", t))
                pe.wait_ge(*drained(L, ("d", 8 + t)))
                for j in range(2):
                    pe.wait_ge(*drained(L, ("RI", t), j))
                for h in range(R_HEADS):
                    at = (h % 2) * 256 + (h // 2) * P
                    mm = pe.matmul(acc[:, h * P:(h + 1) * P], inner[:, t, at:at + P],
                                   rv[:, t, h * P:(h + 1) * P], start=True, stop=True)
                mm.then_inc(fills(L, ("RV", t)), 1)

            def r_cross_(L):
                pe.wait_ge(*drained(L, ("RK",)))
                for par_h in range(2):
                    acc = claim(L, ("RC",), par_h)
                    rows = slice(64 * par_h, 64 * par_h + 64)
                    for hh in range(2):
                        mm = pe.matmul(acc[:, hh * P:(hh + 1) * P], rqkT[rows, hh, P:SEQ],
                                       r_state[rows, hh * P:(hh + 1) * P], start=True, stop=True)
                    mm.then_inc(fills(L, ("RC",), par_h), 1)

            def r_result_turned(L, t):
                pe.wait_ge(*o_done(L, 2 + t + 1))
                four_turned(L, ("RFT", t), r_o[:, t])

            def gate_up(L, f, j):
                if j == 0:
                    h_ready(L, 0 if f == 0 else 2)
                piece = ("gu", f, j // 2)
                arrived(L, piece)
                acc = claim(L, ("gu", f, j))
                w = v(weights(L, piece), k=KD, n=512)
                for s in range(2):
                    c = 256 * s + P * (j % 2)
                    mm = tmajor(acc[:, s * SEQ:(s + 1) * SEQ], lambda k: w[:, k, c:c + P],
                                lambda k: hT[:, k, :], KD)
                mm.then_inc(fills(L, ("gu", f, j)), 1)

            def down(L, f, dd):
                piece = ("down", f, dd)
                arrived(L, piece)
                first = ("dn", f, 0)
                if dd == 0:
                    for j in range(4):
                        claim(L, first, j)
                tiles = min(4, FT - 4 * dd)
                w = v(weights(L, piece)[:, 0:tiles * DM], k=tiles, n=DM)
                for kk in range(tiles):
                    j = 4 * dd + kk
                    pe.wait_ge(*drained(L, ("gu", f, j)))
                    for t in range(TT):
                        for h in range(2):
                            mm = pe.matmul(bank[4 + 2 * t + h][:, :], hid[:, j % 8, t * P:(t + 1) * P],
                                           w[:, kk, h * 512:(h + 1) * 512], start=(j == 0), stop=(j == FT - 1))
                            if j == FT - 1:
                                mm.then_inc(fills(L, first, 2 * t + h), 1)
                if dd < FT // 4:
                    mm.then_inc(hid_used.sem, 1)

            def fox_decays(L):
                acc = claim(L, ("FC",))
                pe.wait_ge(*small_done(L, 1))
                tri, ones = cst("tri"), cst("ones")
                pe.matmul(acc[0:8, 0:P], log_f[:, 0], tri, start=True, stop=True)
                pe.matmul(acc[0:8, P:SEQ], log_f[:, 0], ones, start=True, stop=False)
                pe.matmul(acc[0:8, P:SEQ], log_f[:, 1], tri, start=False, stop=True)\
                  .then_inc(fills(L, ("FC",)), 1)

            def latents_turned(L, t):
                acc = claim(L, ("MC", t))
                pe.wait_ge(*m_norm_done(L, t + 1))
                for i in range(3):
                    mm = turn(acc[:, i * P:(i + 1) * P], mraw[:, t, 8 + i * P:8 + (i + 1) * P])
                mm.then_inc(fills(L, ("MC", t)), 1)

            def up(L, t, i):
                if i == 0:
                    arrived(L, ("u",))
                    pe.wait_ge(*drained(L, ("MC", t)))
                acc = claim(L, ("u", t, i))
                w = weights(L, ("u",))
                tok = slice(t * P, (t + 1) * P)
                if i < 2:
                    wq = v(w[:, 0:1536], k=2, n=768)
                    n = 512 if i == 0 else 256
                    mm = tmajor(acc[:, 0:n], lambda k: cT3[:, k, tok], lambda k: wq[:, k, i * 512:i * 512 + n], 2)
                else:
                    c = 1536 + (i - 2) * 512
                    mm = pe.matmul(acc[:, :], cT3[:, 2, tok], w[:, c:c + 512], start=True, stop=True)
                mm.then_inc(fills(L, ("u", t, i)), 1)

            def mla_turned(L, t, w, half_):
                step = ("MT", t, w, half_)
                acc = claim(L, step)
                pe.wait_ge(*m_roped(L, t + 1))
                for i in range(4):
                    c = (4 * half_ + i) * M_QK
                    mm = turn(acc[0:M_QK, i * P:(i + 1) * P], mqk[:, w, t, c:c + M_QK])
                mm.then_inc(fills(L, step), 1)

            def heads(g):
                return range(4 * g, 4 * g + 4)

            def grid(acc, g, h, n=P):
                return acc[:, (h - 4 * g) * n:(h - 4 * g + 1) * n]

            def d_tokens(L, t, s):
                step = ("DT", t, s)
                acc = claim(L, step)
                pe.wait_ge(*conv2_done(L, 2 * s + 2))
                for i in range(4):
                    mm = turn(acc[:, i * P:(i + 1) * P], conv_y[:, s, i, t * P:(t + 1) * P])
                mm.then_inc(fills(L, step), 1)

            def d_decays(L, t):
                acc = claim(L, ("DG", t))
                pe.wait_ge(*small_done(L, 1))
                g = dgate[:, t]
                same = cst("same_chunk")
                pe.matmul(acc[:, 0:8], cst("tri_chunk"), g, start=True, stop=True)
                pe.matmul(acc[:, 8:16], same, g, start=True, stop=True)
                for c in range(2):
                    pe.matmul(acc[0:64, 16 + 8 * c:24 + 8 * c], same[:, 64 * c:64 * c + 64], g,
                              start=True, stop=True)
                pe.matmul(acc[0:8, 32:32 + P], g, cst("tri_chunk"), start=True, stop=True)\
                  .then_inc(fills(L, ("DG", t)), 1)

            def d_rows(L, t, g):
                acc = claim(L, ("R1", t, g))
                pe.wait_ge(*drained(L, ("DG", t)))
                for h in heads(g):
                    mm = pe.matmul(grid(acc, g, h), ident[0:8, h:h + 1].to_broadcast([8, P]),
                                   gc_rows[0:8, :], start=True, stop=True)
                mm.then_inc(fills(L, ("R1", t, g)), 1)

            def d_turned(L, t, s, g):
                step = ("DX", t, s, g)
                acc = claim(L, step)
                pe.wait_ge(*kn_done(L, t + 1))
                src = (d_tok[:, 0], d_tok[:, 1], d_kb)[s]
                stand_alone()
                for h in heads(g):
                    mm = turn(grid(acc, g, h)[0:64], src[:, h * HD:(h + 1) * HD])
                mm.then_inc(fills(L, step), 1)

            def d_products(L, name, t, g):
                acc = claim(L, (name, t, g))
                s = 0 if name == "QK" else 2
                pe.wait_ge(*drained(L, ("DX", t, max(s, 1), g)))
                for h in heads(g):
                    mm = pe.matmul(grid(acc, g, h), d_T3[0:64, 1, h], d_T3[0:64, s, h], start=True, stop=True)
                mm.then_inc(fills(L, (name, t, g)), 1)

            def d_first(L, t, g):
                acc = claim(L, ("L1", t, g))
                pe.wait_ge(*inv2_done(L, 2 * t + g + 1))
                for h in heads(g):
                    mm = turn(grid(acc, g, h), d_invT[:, h])
                mm.then_inc(fills(L, ("L1", t, g)), 1)

            def d_y(L, t, b, g):
                acc = claim(L, ("Y", t, b, g))
                i = (2, 4, 8, 16, 32).index(b)
                pe.wait_ge(*level_done(L, 10 * t + 2 * i + g + 1))
                for h in heads(g):
                    mm = pe.matmul(grid(acc, g, h), d_C[:, h], d_inv[:, h], start=True, stop=True)
                mm.then_inc(fills(L, ("Y", t, b, g)), 1)

            def d_z(L, t, b, g):
                step = ("Z", t, b, g)
                acc = claim(L, step, 0)
                pe.wait_ge(*drained(L, ("Y", t, b, g)))
                for h in heads(g):
                    mm = pe.matmul(grid(acc, g, h), d_Y[:, h], d_invT[:, h], start=True, stop=True)
                mm.then_inc(fills(L, step, 0), 1)
                acc = claim(L, step, 1)
                for h in heads(g):
                    mm = pe.matmul(grid(acc, g, h), d_invT[:, h], d_Y[:, h], start=True, stop=True)
                mm.then_inc(fills(L, step, 1), 1)

            def d_zt(L, t, g):
                acc = claim(L, ("ZT", t, g))
                pe.wait_ge(*drained(L, ("Y", t, 32, g)))
                for h in heads(g):
                    mm = pe.matmul(grid(acc, g, h), d_Y[:, h], d_invT[:, h], start=True, stop=True)
                mm.then_inc(fills(L, ("ZT", t, g)), 1)

            def d_wt(L, t, g):
                acc = claim(L, ("W", t, g))
                pe.wait_ge(*drained(L, ("ZT", t, g)))
                pe.wait_ge(*kw_done(L, t + 1))
                for h in heads(g):
                    mm = pe.matmul(grid(acc, g, h)[0:64], d_w[:, h * HD:(h + 1) * HD], d_invT[:, h],
                                   start=True, stop=True)
                mm.then_inc(fills(L, ("W", t, g)), 1)

            def d_ut(L, t):
                acc = claim(L, ("U", t))
                for h in range(DN_H):
                    mm = pe.matmul(acc[:, h * HD:(h + 1) * HD], d_invT[:, h], d_vb[:, h * HD:(h + 1) * HD],
                                   start=True, stop=True)
                mm.then_inc(fills(L, ("U", t)), 1)

            def state_ready(L, t, c):
                if (t, c) == (0, 0):
                    pe.wait_ge(*state_zero(L, 1))
                else:
                    pe.wait_ge(*drained(L, ("X3", t, 0) if c else ("X3", t - 1, 1)))

            def d_x1(L, t, c):
                acc = claim(L, ("X1", t, c))
                if c == 0:
                    pe.wait_ge(*drained(L, ("W", t, 1)))
                state_ready(L, t, c)
                rows = slice(64 * c, 64 * c + 64)
                stand_alone()
                for h in range(DN_H):
                    mm = pe.matmul(acc[rows, h * HD:(h + 1) * HD], d_wT[0:64, h, rows],
                                   d_S[0:64, h * HD:(h + 1) * HD], start=True, stop=True)
                mm.then_inc(fills(L, ("X1", t, c)), 1)

            def d_x2(L, t, c):
                acc = claim(L, ("X2", t, c))
                rows = slice(64 * c, 64 * c + 64)
                stand_alone()
                for h in range(DN_H):
                    mm = pe.matmul(acc[rows, h * HD:(h + 1) * HD], d_T3[0:64, 0, h, rows],
                                   d_S[0:64, h * HD:(h + 1) * HD], start=True, stop=True)
                mm.then_inc(fills(L, ("X2", t, c)), 1)

            def d_x3(L, t, c):
                acc = claim(L, ("X3", t, c))
                pe.wait_ge(*drained(L, ("X1", t, c)))
                rows = slice(64 * c, 64 * c + 64)
                stand_alone()
                for h in range(DN_H):
                    mm = pe.matmul(acc[0:64, h * HD:(h + 1) * HD], d_kdec[rows, h * HD:(h + 1) * HD],
                                   d_vn[rows, h * HD:(h + 1) * HD], start=True, stop=True)
                mm.then_inc(fills(L, ("X3", t, c)), 1)

            def d_in(L, t):
                acc = claim(L, ("IN", t))
                pe.wait_ge(*drained(L, ("X1", t, 1)))
                pe.wait_ge(*drained(L, ("QK", t, 1)))
                for h in range(DN_H):
                    mm = pe.matmul(acc[:, h * HD:(h + 1) * HD], d_QK[:, h], d_vn[:, h * HD:(h + 1) * HD],
                                   start=True, stop=True)
                mm.then_inc(fills(L, ("IN", t)), 1)

            def d_result_turned(L, t):
                pe.wait_ge(*o_done(L, FOX_DONE + t + 1))
                four_turned(L, ("DFT", t), dz[:, t])

            parts = {
                "norm": norm, "d": d, "br": branch, "wo": wo, "S": scores, "T": probabilities_turned,
                "V": values, "FT": result_turned, "AT": a_turned, "RT": r_turned, "RI": r_inner,
                "RK": r_state_, "RV": r_values, "RC": r_cross_, "RFT": r_result_turned, "gu": gate_up,
                "dn": down, "FC": fox_decays, "MC": latents_turned, "u": up, "MT": mla_turned,
                "DT": d_tokens, "DG": d_decays, "R1": d_rows, "DX": d_turned,
                "QK": lambda L, t, g: d_products(L, "QK", t, g), "K1": lambda L, t, g: d_products(L, "K1", t, g),
                "L1": d_first, "Y": d_y, "Z": d_z, "ZT": d_zt, "W": d_wt, "U": d_ut, "X1": d_x1,
                "X2": d_x2, "X3": d_x3, "IN": d_in, "DFT": d_result_turned,
            }

            def layer(L):
                seen.clear()
                for step in PLANS[L[0]].steps:
                    if step[0] in parts:
                        parts[step[0]](L, *step[1:])

            pe.wait_ge(setup_dma.sem, ROWS_LANDED)
            for i, n in enumerate((NR1, NR1, NR2, NR2)):
                mm = pe.transpose(bank[0][:, i * P:i * P + n], par_rows[0:n, i, :], ident[0:n, 0:n])
            mm.then_inc(setup_pe.sem, 1)
            layers(pe, 0, layer)
            layers(pe, 1, layer)

        @block.scalar
        def _(act):
            def copy(o, i):
                return act.activation(o, i, ACT.Copy)

            def norm_sums(L, m):
                act.wait_ge(*x_new(L, m))
                for t in range(TT):
                    act.activation(squares[:, t], xv[:, t], ACT.Square, scale=DM ** -0.5,
                                   accum_out=x_ss[:, t:t + 1])\
                       .then_inc(ss_done.sem, 1)

            def norm(L, m, t, h):
                if (t, h) == (0, 0):
                    norm_sums(L, m)

            def read(L, step, o, rows=slice(0, P), n=None, j=0):
                act.wait_ge(*filled(L, step, j))
                src = bank_of(L, step, j)[rows, 0:n if n else math.prod(o.shape[1:])]
                if len(o.shape) == 3:
                    src = v(src, a=o.shape[1], b=o.shape[2])
                copy(o, src).then_inc(drains(L, step, j), 1)

            def tanh_half(L, step, n_done, done, o):
                act.wait_ge(*filled(L, step))
                act.activation(o, bank_of(L, step)[:, :], ACT.Tanh, scale=0.5).then_inc(done.sem, 1)

            def pair(t_, j):
                return t_[:, 2 * j:2 * j + 2, :]

            def d1(L, o):
                step, n, part = ("d", o), o // 2, o % 2
                if n < 2:
                    read(L, step, aqk[:, part, n * 512:(n + 1) * 512])
                elif n == 2:
                    read(L, step, rqk[:, part])
                elif n == 3:
                    read(L, step, av[:, part])
                elif n == 4:
                    read(L, step, rv[:, part])
                elif n in (5, 6, 10):
                    i = {5: 0, 6: 2, 10: 4}[n] + part
                    if i >= 2:
                        before = {2: 10, 3: 11, 4: 12, 5: 13}[i]
                        act.wait_ge(*drained(L, ("d", before)))
                    tanh_half(L, step, i, tanh_done, th[:, i % 2])
                elif n == 7:
                    read(L, step, pair(cu, part))
                elif n >= 11:
                    i, j = (n - 11) // 2, ((n - 11) % 2) * 4 + 2 * part
                    act.wait_ge(*filled(L, step))
                    act.activation(gates[:, i, j:j + 2, :], v(bank_of(L, step)[:, :], a=2, b=SEQ), ACT.Tanh,
                                   scale=0.5).then_inc(drains(L, step), 1)

            def d2(L, o):
                step, n, part = ("d", o), o // 2, o % 2
                if n == 0:
                    read(L, step, mraw[:, part])
                elif n == 1:
                    read(L, step, pair(fqT, part))
                elif n == 2:
                    read(L, step, pair(fkT, part))
                elif n == 3:
                    read(L, step, fv[:, part])
                elif n < 7:
                    i, s = o - 8, n - 4
                    act.wait_ge(*filled(L, step))
                    acc = bank_of(L, step)
                    if i >= 2:
                        act.wait_ge(*taps_done(L, i - 1))
                    copy(craw[:, i % 2], v(acc[:, :], a=2, b=SEQ)).then_inc(craw_done.sem, 1)
                    for jj in range(2):
                        col = 3 * 12 + 4 * s + 2 * part + jj
                        ins = act.activation(conv_y[:, s, 2 * part + jj], acc[:, jj * SEQ:(jj + 1) * SEQ],
                                             ACT.Copy, scale=par_("dn_conv_w_2", 48, PAR2)[:, col:col + 1])
                    ins.then_inc(drains(L, step), 1)
                    if i >= 1:
                        conv_tanh(L, i - 1)
                    if i == 5:
                        conv_tanh(L, 5)
                elif n == 7:
                    if part == 0:
                        act.wait_ge(*conv2_done(L, 6))
                    tanh_half(L, step, part, tanh_done, th[:, part])
                else:
                    i, j = (n - 8) // 2, ((n - 8) % 2) * 4 + 2 * part
                    act.wait_ge(*filled(L, step))
                    for jj in range(2):
                        col = 8 * i + j + jj
                        ins = act.activation(gates[:, i, j + jj, :], bank_of(L, step)[:, jj * SEQ:(jj + 1) * SEQ],
                                             ACT.Tanh, scale=0.5,
                                             bias=par_("b_gate_2", 24, PAR2)[:, col:col + 1])
                    ins.then_inc(drains(L, step), 1)

            def conv_tanh(L, i):
                act.wait_ge(*taps_done(L, i + 1))
                if i >= 2:
                    act.wait_ge(*conv2_done(L, i - 1))
                s, part = i // 2, i % 2
                act.activation(th[:, i % 2], conv_y[:, s, 2 * part:2 * part + 2].rearrange("p a b -> p (a b)"),
                               ACT.Tanh, scale=0.5).then_inc(ctanh_done.sem, 1)

            def scores(L, kind, u):
                qb, pair_, n_u = u // 4, u % 4, u + 8 * (kind == "mla")
                n = (qb + 1) * P
                scale = M_QK ** -0.5 if kind == "mla" else HD ** -0.5
                act.wait_ge(*bias_done(L, n_u + 1))
                for c in range(2):
                    act.activation(at_sc[:, u % 2, c, 0:n], at_sc[:, u % 2, c, 0:n], ACT.Exp,
                                   bias=at_bias[:, u % 2, c:c + 1], scale=scale,
                                   accum_out=at_sum[:, qb, 2 * pair_ + c:2 * pair_ + c + 1])\
                       .then_inc(exp_done.sem, 1)

            def turned(L, kind, u):
                n = (u // 4 + 1) * P * (1 if kind == "diff" else 2)
                if u >= 2:
                    act.wait_ge(*filled(L, ("V", kind, u - 2)))
                read(L, ("T", kind, u), at_wT[:, u % 2, 0:n])

            def values(L, kind, u):
                read(L, ("V", kind, u), at_o[:, u // 4, (u % 4) * P:(u % 4 + 1) * P])

            def result(L, kind, qb):
                dst = {"diff": aT, "fox": fox_T, "mla": mla_T}[kind]
                read(L, ("FT", kind, qb), dst[:, :, qb * P:(qb + 1) * P])

            def a_turned(L, t):
                read(L, ("AT", t), aqT[:, :, t * P:(t + 1) * P], j=0)
                read(L, ("AT", t), akT[:, :, t * P:(t + 1) * P], j=1)

            def gate_up(L, f, j):
                act.wait_ge(*filled(L, ("gu", f, j)))
                if j >= 4:
                    act.wait_ge(*drained(L, ("gu", f, j - 4)))
                act.activation(ffn_tanh[:, j % 4], bank_of(L, ("gu", f, j))[:, 0:SEQ], ACT.Tanh, scale=0.5)\
                   .then_inc(ffn_tanh_done.sem, 1)

            def small_values(L):
                act.wait_ge(*z_done(L, 1))
                act_chain.link(act.activation(z_log[:, :, :], z_abs[:, :, :], ACT.Exp, scale=-1.0))
                for t in range(TT):
                    ins = act.activation(beta_t[:, t], mraw[:, t, 424:432], ACT.Tanh, scale=0.5)
                act_chain.link(ins)
                act.activation(z_log[:, :, :], z_log[:, :, :], ACT.Ln, bias=cst("ones")[:, 0:1])\
                   .then_inc(zlog_done.sem, 1)
                for t in range(TT):
                    act.activation(m_junk[:, t, 0:M_QR], mraw[:, t, 8:8 + M_QR], ACT.Square, scale=M_QR ** -0.5,
                                   accum_out=m_ss[:, t, 0:1])
                    ins = act.activation(m_junk[:, t, M_QR:M_QR + M_KVR], mraw[:, t, 264:392], ACT.Square, scale=M_KVR ** -0.5,
                                         accum_out=m_ss[:, t, 1:2])
                ins.then_inc(m_ss_done.sem, 1)

            def up(L, t, i):
                step = ("u", t, i)
                if i < 2:
                    read(L, step, mqk[:, 0, t, i * 512:i * 512 + (512 if i == 0 else 256)])
                else:
                    act.wait_ge(*filled(L, step))
                    src = v(bank_of(L, step)[:, :], a=4, b=P)
                    hs = slice(4 * (i - 2), 4 * (i - 2) + 4)
                    copy(v(mqk[:, 1, t], h=8, n=M_QK)[:, hs, 0:HD], src[:, :, 0:HD])
                    copy(v(mv[:, t], h=8, n=HD)[:, hs, :], src[:, :, HD:P]).then_inc(drains(L, step), 1)

            def mla_turned(L, t, w, h_):
                step = ("MT", t, w, h_)
                act.wait_ge(*filled(L, step))
                if (t, w, h_) == (0, 0, 0):
                    act.wait_ge(*conv2_done(L, 6))
                copy(mqkT[0:M_QK, w, 4 * h_:4 * h_ + 4, t * P:(t + 1) * P],
                     v(bank_of(L, step)[0:M_QK, :], a=4, b=P)).then_inc(drains(L, step), 1)

            def d_decays(L, t):
                act.wait_ge(*dlt_done(L, t + 1))
                act.activation(eg[:, 0:16], gc[:, 0:16], ACT.Exp)
                act.activation(gl[0:64], gl_raw[0:64], ACT.Exp).then_inc(eg_done.sem, 1)

            def d_rows(L, t, g):
                act.wait_ge(*arg_done(L, 2 * t + g + 1))
                act.activation(d_decay[:, 4 * g:4 * g + 4], d_decay[:, 4 * g:4 * g + 4], ACT.Exp)\
                   .then_inc(decay_done.sem, 1)

            def quarter(t_, g):
                return t_[:, 4 * g:4 * g + 4, :]

            def small_rows(L, step, t_, g):
                act.wait_ge(*filled(L, step))
                copy(t_[0:64, 4 * g:4 * g + 4, :], v(bank_of(L, step)[0:64, :], a=4, b=P))\
                    .then_inc(drains(L, step), 1)

            parts1 = {
                "norm": norm, "d": d1, "S": scores, "T": turned, "V": values, "FT": result, "AT": a_turned,
                "RT": lambda L, t: read(L, ("RT", t), rqkT[:, :, t * P:(t + 1) * P]),
                "RK": lambda L: read(L, ("RK",), r_state[:, :]),
                "RFT": lambda L, t: read(L, ("RFT", t), rT[:, :, t * P:(t + 1) * P]),
            }
            parts2 = {
                "norm": norm, "d": d2, "S": scores, "T": turned, "V": values, "FT": result, "gu": gate_up,
                "SM": small_values, "u": up, "MT": mla_turned,
                "DT": lambda L, t, s: read(L, ("DT", t, s), d_tok[:, s]),
                "DG": d_decays, "R1": d_rows,
                "DX": lambda L, t, s, g: small_rows(L, ("DX", t, s, g), d_T3[:, s], g),
                "L1": lambda L, t, g: read(L, ("L1", t, g), quarter(d_inv, g)),
                "Y": lambda L, t, b, g: read(L, ("Y", t, b, g), quarter(d_Y, g)),
                "W": lambda L, t, g: small_rows(L, ("W", t, g), d_wT, g),
                "U": lambda L, t: read(L, ("U", t), d_u),
                "DFT": lambda L, t: read(L, ("DFT", t), dn_T[:, :, t * P:(t + 1) * P]),
            }

            def layer(L):
                act_chain.layer(act, L)
                if L[0] == 1:
                    act.wait_ge(*par_done(L, 1))
                for step in PLANS[L[0]].steps:
                    part = (parts1, parts2)[L[0]].get(step[0])
                    if part:
                        part(L, *step[1:])
                act_chain.end()

            def last_norm(blk):
                act.wait_ge(*x_new((blk, DEPTH), 0 if blk == 0 else 0))
                for t in range(TT):
                    act.activation(squares[:, t], xv[:, t], ACT.Square, scale=DM ** -0.5,
                                   accum_out=x_ss[:, t:t + 1])\
                       .then_inc(end_ss.sem, 1)

            for l in range(DEPTH):
                for name, table, dst, n in (("attn_subln_g", par1, PAR1["subln"], A_V),
                                            ("fox_b_f_2", par2, PAR2["f_bias"], 8),
                                            ("dn_dt_bias_2", par2, PAR2["dt_bias"], 8),
                                            ("dn_a_log_2", par2, PAR2["neg_a"], 8),
                                            ("dn_o_norm_2", par2, PAR2["o_norm"], HD)):
                    act.dma_start(table[:, l, dst:dst + n], a[name][l].partition_broadcast(P))\
                       .then_inc(setup_shared.sem, 16)
            act.dma_start(lam_rows, a["attn_lambda"].rearrange("l r d -> (l r d)").partition_broadcast(P))\
               .then_inc(setup_shared.sem, 16)
            act.dma_start(pos_i[:, :], a["positions_2"][0].rearrange("(t p) -> p t", p=P),
                          allow_slow_non_contiguous=True).then_inc(setup_shared.sem, 16)
            act.wait_ge(setup_shared.sem, 16 * (5 * DEPTH + 2))
            act.activation(par2[:, :, PAR2["neg_a"]:PAR2["neg_a"] + 8], par2[:, :, PAR2["neg_a"]:PAR2["neg_a"] + 8],
                           ACT.Exp)
            act.wait_ge(setup_dve.sem, 1)
            act.activation(lam_e, lam_s, ACT.Exp).then_inc(setup_act.sem, 1)
            act.wait_ge(setup_dve.sem, 2)
            act.activation(trig[:, :, :, :], trig[:, :, :, :], ACT.Sin).then_inc(setup_act.sem, 1)
            layers(act, 0, layer)
            last_norm(0)
            layers(act, 1, layer)
            last_norm(1)

        @block.vector
        def _(dve):
            link = dve_chain.link

            def tt(o, i0, i1, op):
                return dve.tensor_tensor(o, i0, i1, op)

            def stt(o, i0, s, i1, op0, op1):
                return dve.scalar_tensor_tensor(o, i0, s, i1, op0, op1)

            def over(t_, n):
                return t_.unsqueeze(2).to_broadcast([t_.shape[0], t_.shape[1], n])

            def again(t_, n):
                return t_.unsqueeze(1).to_broadcast([t_.shape[0], n, t_.shape[1]])

            def parameters(L):
                dve.wait_ge(*x_new(L, 0))
                n, table = (NP1, par1) if L[0] == 0 else (NP2, par2)
                src = table[:, bass.ds(L[1], 1), :].rearrange("p o n -> p (o n)")
                dve.tensor_copy(par[:, 0:n], src).then_inc(par_done.sem, 1)
                dve.wait_ge(*par_done(L, 1))

            def norm(L, m, t, h):
                step = ("norm", m, t, h)
                if (t, h) == (0, 0):
                    dve.wait_ge(*rstd_done(L, m + 1))
                    for tok in range(TT):
                        dve.tensor_scalar(xs[:, tok], xv[:, tok], x_rstd[:, tok:tok + 1], None, ALU.mult)\
                           .then_inc(xs_done.sem, 1)
                name, table = (("norm_g", PAR1) if L[0] == 0 else
                               (("ffn1_norm_2", "mix_norm_2", "ffn2_norm_2")[m], PAR2))
                gain = par_(name, 8, table)[:, 4 * h:4 * h + 4]
                dve.wait_ge(*filled(L, step))
                tt(hT[:, 4 * h:4 * h + 4, t * P:(t + 1) * P], v(bank_of(L, step)[:, :], a=4, b=P),
                   over(gain, P), ALU.mult).then_inc(drains(L, step), 1)

            def silu2(L, step, done, th_, o):
                dve.wait_ge(*done)
                stt(o, th_, 1.0, bank_of(L, step)[:, :], ALU.add, ALU.mult).then_inc(drains(L, step), 1)
                dve.wait_ge(*drained(L, step))

            def d1(L, o):
                step, n, part = ("d", o), o // 2, o % 2
                if n == 5:
                    silu2(L, step, tanh_done(L, part + 1), th[:, part], az[:, part])
                    link(tt(v(az[:, part], h=4, n=P), v(az[:, part], h=4, n=P),
                            again(par_("subln", A_V, PAR1), 4), ALU.mult))
                elif n == 6:
                    silu2(L, step, tanh_done(L, part + 3), th[:, part], rz[:, part])
                elif n == 8:
                    dve.wait_ge(*filled(L, step))
                    dve.wait_ge(*drained(L, ("d", 14 + part)))
                    tt(cu[:, 2 * part:2 * part + 2, :], cu[:, 2 * part:2 * part + 2, :],
                       v(bank_of(L, step)[:, :], a=2, b=SEQ), ALU.mult).then_inc(drains(L, step), 1)
                    dve.wait_ge(*drained(L, step))
                    w = par_("conv_w", 12, PAR1)
                    tiles = (2 * part, 2 * part + 1)
                    for j in tiles:
                        ins = dve.tensor_scalar(cy[:, j], cu[:, j], w[:, 8 + j:9 + j], None, ALU.mult)
                    link(ins)
                    for back, tap in ((1, 1), (2, 0)):
                        for j in tiles:
                            ins = stt(cy[:, j, back:SEQ], cu[:, j, 0:SEQ - back], w[:, 4 * tap + j:4 * tap + j + 1],
                                      cy[:, j, back:SEQ], ALU.mult, ALU.add)
                        link(ins)
                elif n == 9:
                    dve.wait_ge(*filled(L, step))
                    tt(cy[:, 2 * part:2 * part + 2, :], cy[:, 2 * part:2 * part + 2, :],
                       v(bank_of(L, step)[:, :], a=2, b=SEQ), ALU.mult).then_inc(drains(L, step), 1)
                elif n == 10:
                    silu2(L, step, tanh_done(L, part + 5), th[:, part], th_c[:, part])
                    dve.wait_ge(*drained(L, ("d", 18 + part)))
                    tt(cT[:, 2 * part:2 * part + 2, :], cy[:, 2 * part:2 * part + 2, :],
                       v(th_c[:, part], a=2, b=SEQ), ALU.mult).then_inc(c_done.sem, 1)

            def branch(L, i, jp):
                step = ("br", i, jp)
                order = (1, 0, 2) if L[0] == 0 else (0, 1, 2)
                tmps = br_tmps[L[0]]
                n = order.index(i) * 4 + jp
                dve.wait_ge(*filled(L, step))
                gate = gates[:, i, 2 * jp:2 * jp + 2].rearrange("p a b -> p (a b)")
                if n < 4:
                    o = merged[:, 2 * jp:2 * jp + 2].rearrange("p a b -> p (a b)")
                else:
                    o = tmps[:, n % 2]
                    if n >= 6:
                        dve.wait_ge(*added(L, n - 5))
                if jp == 0:
                    for p_ in range(4):
                        dve.wait_ge(*drained(L, ("d", (22 if L[0] == 0 else 16) + 4 * i + p_)))
                stt(o, gate, 1.0, bank_of(L, step)[:, :], ALU.add, ALU.mult).then_inc(drains(L, step), 1)

            def wo(L, q):
                step = ("wo", q)
                dve.wait_ge(*filled(L, step))
                cols = xv[:, :, 256 * q:256 * q + 256]
                stt(cols, v(bank_of(L, step)[:, :], a=2, b=256), 0.25 if L[0] == 0 else 0.5, cols,
                    ALU.mult, ALU.add).then_inc(drains(L, step), 1)
                if q == 3:
                    for i in range(4):
                        dve.wait_ge(*drained(L, ("wo", i)))
                    dve.memset(stat_all[:, 32:33], 0.0).then_inc(x_new.sem, 1)

            def scores(L, kind, u):
                qb, pair, n_u = u // 4, u % 4, u + 8 * (kind == "mla")
                n = (qb + 1) * P
                scale = M_QK ** -0.5 if kind == "mla" else HD ** -0.5
                if u >= 2:
                    dve.wait_ge(*filled(L, ("T", kind, u - 2)))
                for c in range(2):
                    dve.wait_ge(*filled(L, ("S", kind, u), c))
                    tt(at_sc[:, u % 2, c, 0:n], bank_of(L, ("S", kind, u), c)[:, 0:n],
                       cst("causal")[:, SEQ - n:SEQ], ALU.add).then_inc(drains(L, ("S", kind, u), c), 1)
                for c in range(2):
                    dve.wait_ge(*drained(L, ("S", kind, u), c))
                link(dve.reduce_max(at_max[:, u % 2], at_sc[:, u % 2, :, 0:n], X))
                dve.tensor_scalar(at_bias[:, u % 2], at_max[:, u % 2], -scale, None, ALU.mult)\
                   .then_inc(bias_done.sem, 1)
                if kind == "diff":
                    s2 = at_rcp[:, qb, 2 * pair:2 * pair + 2]
                    dve.wait_ge(*exp_done(L, 2 * n_u + 2))
                    link(dve.reciprocal(s2, at_sum[:, qb, 2 * pair:2 * pair + 2]))
                    link(tt(s2[:, 1:2], s2[:, 1:2], par_("neg_lam", 1, PAR1), ALU.mult))
                    link(dve.tensor_scalar(at_w[:, u % 2, 0:n], at_sc[:, u % 2, 0, 0:n], s2[:, 0:1], None, ALU.mult))
                    stt(at_w[:, u % 2, 0:n], at_sc[:, u % 2, 1, 0:n], s2[:, 1:2], at_w[:, u % 2, 0:n],
                        ALU.mult, ALU.add).then_inc(mix_done.sem, 1)

            def variance(src, sq, ss, groups, n, inv_n, eps, done):
                link(tt(sq, src, src, ALU.mult))
                link(dve.reduce_sum(ss, v(sq, a=groups, b=n), X))
                dve.tensor_scalar(ss, ss, inv_n, eps, ALU.mult, ALU.add).then_inc(done.sem, 1)

            def normed(src, rstd, groups, n, factor, done):
                link(tt(v(src, a=groups, b=n), v(src, a=groups, b=n), over(rstd, n), ALU.mult))
                tt(factor[0], src, factor[1], ALU.mult).then_inc(done.sem, 1)

            def finish(L, kind, qb):
                dve.wait_ge(*drained(L, ("V", kind, 4 * qb + 3)))
                if kind == "diff":
                    variance(at_o[:, qb], at_sq, a_ss[:, 4 * qb:4 * qb + 4], A_HEADS, A_V, 1.0 / A_V, EPS, o_var)
                else:
                    dve.wait_ge(*exp_done(L, 2 * (4 * qb + 4) + 16 * (kind == "mla")))
                    link(dve.reciprocal(at_rcp[:, qb], at_sum[:, qb]))
                    tt(v(at_o[:, qb], h=8, n=HD), v(at_o[:, qb], h=8, n=HD), over(at_rcp[:, qb], HD),
                       ALU.mult).then_inc(o_done.sem, 1)

            def finish2(L, kind, qb):
                if kind == "diff":
                    dve.wait_ge(*o_rstd(L, qb + 1))
                    normed(at_o[:, qb], a_rs[:, 4 * qb:4 * qb + 4], A_HEADS, A_V, (at_o[:, qb], az[:, qb]), o_done)

            def r_inner(L, t):
                decay = v(cst("ret_decay"), hh=2, par=2, n=P)
                for p_ in range(2):
                    dve.wait_ge(*filled(L, ("RI", t), p_))
                    tt(v(inner[:, t, p_ * 256:(p_ + 1) * 256], a=2, b=P),
                       v(bank_of(L, ("RI", t), p_)[:, 0:256], a=2, b=P), decay[:, :, p_, :],
                       ALU.mult).then_inc(drains(L, ("RI", t), p_), 1)

            def r_cross_(L):
                xi = v(cst("xi"), hh=2, par=2)
                for p_ in range(2):
                    dve.wait_ge(*filled(L, ("RC",), p_))
                    tt(v(r_cross, hh=2, par=2, n=P)[:, :, p_, :], v(bank_of(L, ("RC",), p_)[:, 0:256], a=2, b=P),
                       over(xi[:, :, p_], P), ALU.mult).then_inc(drains(L, ("RC",), p_), 1)

            def r_values(L, t):
                dve.wait_ge(*filled(L, ("RV", t)))
                acc = bank_of(L, ("RV", t))[:, :]
                if t == 0:
                    dve.tensor_copy(r_o[:, 0], acc).then_inc(drains(L, ("RV", t)), 1)
                else:
                    for p_ in range(2):
                        dve.wait_ge(*drained(L, ("RC",), p_))
                    tt(r_o[:, 1], r_cross, acc, ALU.add).then_inc(drains(L, ("RV", t)), 1)

            def r_finish(L, t):
                dve.wait_ge(*drained(L, ("RV", t)))
                variance(r_o[:, t], r_sq, r_ss2[:, 4 * t:4 * t + 4], R_HEADS, R_V, 1.0 / R_V, EPS, o_var)

            def r_finish2(L, t):
                dve.wait_ge(*o_rstd(L, 2 + t + 1))
                normed(r_o[:, t], r_rs2[:, 4 * t:4 * t + 4], R_HEADS, R_V, (r_o[:, t], rz[:, t]), o_done)

            def gate_up(L, f, j):
                step = ("gu", f, j)
                acc = bank_of(L, step)
                dve.wait_ge(*ffn_tanh_done(L, f * FT + j + 1))
                link(stt(ffn_gate[:, j % 4], ffn_tanh[:, j % 4], 1.0, acc[:, 0:SEQ], ALU.add, ALU.mult))
                if j >= 8:
                    dve.wait_ge(*hid_used(L, f * (FT // 4) + (j - 8) // 4 + 1))
                tt(hid[:, j % 8], ffn_gate[:, j % 4], acc[:, SEQ:2 * SEQ], ALU.mult).then_inc(drains(L, step), 1)

            def down(L, f, dd):
                if dd < FT // 4:
                    return
                first = ("dn", f, 0)
                for t in range(TT):
                    for h in range(2):
                        dve.wait_ge(*filled(L, first, 2 * t + h))
                        cols = xv[:, t, h * 512:(h + 1) * 512]
                        stt(cols, bank_of(L, first, 2 * t + h)[:, :], 0.25, cols, ALU.mult, ALU.add)\
                            .then_inc(drains(L, first, 2 * t + h), 1)
                for j in range(4):
                    dve.wait_ge(*drained(L, first, j))
                dve.memset(stat_all[:, 32:33], 0.0).then_inc(x_new.sem, 1)

            def small_values(L):
                for t in range(TT):
                    dve.wait_ge(*drained(L, ("d", t)))
                    tt(z[:, t, 0:8], mraw[:, t, 0:8], par_("f_bias", 8, PAR2), ALU.add)
                    ins = tt(z[:, t, 8:16], mraw[:, t, 432:440], par_("dt_bias", 8, PAR2), ALU.add)
                link(ins)
                stt(z_abs[:, :, :], z[:, :, :], -1.0, z[:, :, :], ALU.mult, ALU.max).then_inc(z_done.sem, 1)
                dve.wait_ge(*zlog_done(L, 1))
                stt(log_f[:, :, :], z[:, :, 0:8], 0.0, z_log[:, :, 0:8], ALU.min, ALU.subtract)
                link(stt(dgate[:, :, :], z[:, :, 8:16], 0.0, z_log[:, :, 8:16], ALU.max, ALU.add))
                tt(dgate[:, :, :], dgate[:, :, :], again(par_("neg_a", 8, PAR2), TT), ALU.mult)
                dve.tensor_scalar(beta[:, :, :], beta_t[:, :, :], 0.5, 0.5, ALU.mult, ALU.add)
                dve.tensor_scalar(half_beta[:, :, :], beta_t[:, :, :], 0.25, 0.25, ALU.mult, ALU.add)\
                   .then_inc(small_done.sem, 1)

            def fox_decays(L):
                dve.wait_ge(*filled(L, ("FC",)))
                link(dve.memset(neg_c, 0.0))
                dve.tensor_scalar(neg_c[0:8], bank_of(L, ("FC",))[0:8, 0:SEQ], -1.0 / FOX_SCALE, None, ALU.mult)\
                   .then_inc(drains(L, ("FC",)), 1)

            def latents(L, t):
                step = ("MC", t)
                dve.wait_ge(*filled(L, step))
                gain = par[:, PAR2["mla_q_norm_2"]:PAR2["mla_q_norm_2"] + 3]
                tt(cT3[:, :, t * P:(t + 1) * P], v(bank_of(L, step)[:, 0:384], a=3, b=P), over(gain, P),
                   ALU.mult).then_inc(drains(L, step), 1)

            def taps(L, i):
                s, part = i // 2, i % 2
                w = par_("dn_conv_w_2", 48, PAR2)
                tiles = (2 * part, 2 * part + 1)
                dve.wait_ge(*craw_done(L, i + 1))
                dve.wait_ge(*drained(L, ("d", 8 + i)))
                for back in (1, 2, 3):
                    for jj, j in enumerate(tiles):
                        col = (3 - back) * 12 + 4 * s + j
                        ins = stt(conv_y[:, s, j, back:SEQ], craw[:, i % 2, jj, 0:SEQ - back], w[:, col:col + 1],
                                  conv_y[:, s, j, back:SEQ], ALU.mult, ALU.add)
                    if back < 3:
                        link(ins)
                ins.then_inc(taps_done.sem, 1)
                dve.wait_ge(*taps_done(L, i + 1))

            def conv_silu2(L, i):
                s, part = i // 2, i % 2
                dve.wait_ge(*ctanh_done(L, i + 1))
                y = conv_y[:, s, 2 * part:2 * part + 2].rearrange("p a b -> p (a b)")
                stt(y, th[:, i % 2], 1.0, y, ALU.add, ALU.mult).then_inc(conv2_done.sem, 1)

            def d2(L, o):
                n, part = o // 2, o % 2
                if 4 <= n < 7:
                    taps(L, o - 8)
                    if o > 8:
                        conv_silu2(L, o - 9)
                    if o == 13:
                        conv_silu2(L, 5)
                elif n == 7:
                    silu2(L, ("d", o), tanh_done(L, part + 1), th[:, part], dz[:, part])
                    link(tt(v(dz[:, part], h=8, n=HD), v(dz[:, part], h=8, n=HD),
                            again(par_("o_norm", HD, PAR2), 8), ALU.mult))

            def quarter(t_, g):
                return t_[:, 4 * g:4 * g + 4, :]

            def grid(acc):
                return v(acc[:, :], a=4, b=P)

            def d_stats(L, t):
                for s in range(2):
                    dve.wait_ge(*drained(L, ("DT", t, s)))
                    link(tt(d_sq, d_tok[:, s], d_tok[:, s], ALU.mult))
                    link(dve.reduce_sum(d_ss[:, 8 * s:8 * s + 8], v(d_sq, a=8, b=HD), X))
                dve.tensor_scalar(d_ss, d_ss, 4 * EPS, None, ALU.add).then_inc(l2_var.sem, 1)

            def d_decays(L, t):
                step = ("DG", t)
                dve.wait_ge(*filled(L, step))
                acc = bank_of(L, step)
                dve.tensor_copy(gl_raw[0:64], v(acc[0:64, 16:32], a=2, b=8))
                dve.tensor_copy(gc[:, 16:24], acc[:, 8:16])
                link(dve.tensor_copy(gc[:, 0:8], acc[:, 0:8]))
                dve.tensor_copy(gc_rows[0:8], acc[0:8, 32:32 + P]).then_inc(drains(L, step), 1)
                tt(gc[:, 8:16], gc[:, 16:24], gc[:, 0:8], ALU.subtract).then_inc(dlt_done.sem, 1)

            def d_rows(L, t, g):
                step = ("R1", t, g)
                dve.wait_ge(*filled(L, step))
                o = quarter(d_decay, g)
                tt(o, grid(bank_of(L, step)), over(gc[:, 4 * g:4 * g + 4], P), ALU.subtract)\
                    .then_inc(drains(L, step), 1)
                dve.wait_ge(*drained(L, step))
                tt(o, o, again(cst("decay_mask"), 4), ALU.add).then_inc(arg_done.sem, 1)

            def d_scaled(L, t):
                dve.wait_ge(*l2_rstd(L, t + 1))
                q_, k_ = v(d_tok[:, 0], a=8, b=HD), v(d_tok[:, 1], a=8, b=HD)
                link(tt(k_, k_, over(d_rs[:, 8:16], HD), ALU.mult))
                stt(q_, q_, HD ** -0.5, over(d_rs[:, 0:8], HD), ALU.mult, ALU.mult)
                tt(v(d_kb, a=8, b=HD), k_, over(beta[:, t], HD), ALU.mult).then_inc(kn_done.sem, 1)

            def d_products(L, name, t, g):
                step = (name, t, g)
                dve.wait_ge(*filled(L, step))
                dve.wait_ge(*decay_done(L, 2 * t + g + 1))
                tt(quarter(d_QK if name == "QK" else d_M, g), grid(bank_of(L, step)), quarter(d_decay, g),
                   ALU.mult).then_inc(drains(L, step), 1)

            def d_first(L, t, g):
                dve.wait_ge(*drained(L, ("K1", t, g)))
                o = quarter(d_invT, g)
                link(tt(o, quarter(d_M, g), again(cst("below1"), 4), ALU.mult))
                tt(o, o, again(ident, 4), ALU.add).then_inc(inv2_done.sem, 1)

            def d_z(L, t, b, g):
                step = ("Z", t, b, g)
                dve.wait_ge(*filled(L, step, 1))
                o = quarter(d_invT, g)
                tt(o, o, grid(bank_of(L, step, 0)), ALU.add).then_inc(drains(L, step, 0), 1)
                o = quarter(d_inv, g)
                tt(o, o, grid(bank_of(L, step, 1)), ALU.add).then_inc(drains(L, step, 1), 1)

            def d_zt(L, t, g):
                dve.wait_ge(*filled(L, ("ZT", t, g)))
                o = quarter(d_invT, g)
                tt(o, o, grid(bank_of(L, ("ZT", t, g))), ALU.add).then_inc(drains(L, ("ZT", t, g)), 1)

            def d_x1(L, t, c):
                if (t, c) == (0, 0):
                    dve.memset(d_S[0:64], 0.0).then_inc(state_zero.sem, 1)
                    dve.wait_ge(*state_zero(L, 1))
                rows = slice(64 * c, 64 * c + 64)
                dve.wait_ge(*filled(L, ("X1", t, c)))
                dve.wait_ge(*drained(L, ("U", t)))
                tt(d_vn[rows], d_u[rows], bank_of(L, ("X1", t, c))[rows, :], ALU.subtract)\
                    .then_inc(drains(L, ("X1", t, c)), 1)

            def d_x2(L, t, c):
                rows = slice(64 * c, 64 * c + 64)
                if (t, c) == (1, 0):
                    dve.wait_ge(*o_done(L, FOX_DONE + t))
                dve.wait_ge(*filled(L, ("X2", t, c)))
                tt(v(d_cross[rows], a=8, b=HD), v(bank_of(L, ("X2", t, c))[rows, :], a=8, b=HD),
                   over(eg[rows, 0:8], HD), ALU.mult).then_inc(drains(L, ("X2", t, c)), 1)

            def d_x3(L, t, c):
                if (t, c) != (0, 0):
                    dve.wait_ge(*drained(L, ("X3", t, 0) if c else ("X3", t - 1, 1)))
                link(tt(v(d_S1[0:64], a=8, b=HD), v(d_S[0:64], a=8, b=HD), over(gl[0:64, c], HD), ALU.mult))
                dve.wait_ge(*filled(L, ("X3", t, c)))
                tt(d_S[0:64], d_S1[0:64], bank_of(L, ("X3", t, c))[0:64, :], ALU.add)\
                    .then_inc(drains(L, ("X3", t, c)), 1)

            def d_in(L, t):
                dve.wait_ge(*filled(L, ("IN", t)))
                dve.wait_ge(*drained(L, ("X2", t, 1)))
                tt(d_o, d_cross, bank_of(L, ("IN", t))[:, :], ALU.add).then_inc(drains(L, ("IN", t)), 1)

            def d_finish(L, t):
                dve.wait_ge(*drained(L, ("IN", t)))
                variance(d_o, d_sq, d_ss2[:, 8 * t:8 * t + 8], DN_H, HD, 1.0 / HD, EPS, dn_var)

            def d_finish2(L, t):
                dve.wait_ge(*dn_rstd(L, t + 1))
                normed(d_o, d_rs2[:, 8 * t:8 * t + 8], DN_H, HD, (dz[:, t], dz[:, t]), o_done)

            parts1 = {"norm": norm, "d": d1, "br": branch, "wo": wo, "S": scores, "F": finish, "F2": finish2,
                      "RI": r_inner, "RC": r_cross_, "RV": r_values, "RF": r_finish, "RF2": r_finish2}
            parts2 = {"norm": norm, "d": d2, "br": branch, "wo": wo, "S": scores, "F": finish, "gu": gate_up,
                      "dn": down, "SM": small_values, "FC": fox_decays, "MC": latents, "DP": d_stats,
                      "DG": d_decays, "R1": d_rows, "DP2": d_scaled,
                      "QK": lambda L, t, g: d_products(L, "QK", t, g),
                      "K1": lambda L, t, g: d_products(L, "K1", t, g), "L1": d_first, "Z": d_z, "ZT": d_zt,
                      "X1": d_x1, "X2": d_x2, "X3": d_x3, "IN": d_in, "DF": d_finish, "DF2": d_finish2}

            def layer(L):
                dve_chain.layer(dve, L)
                parameters(L)
                for step in PLANS[L[0]].steps:
                    part = (parts1, parts2)[L[0]].get(step[0])
                    if part:
                        part(L, *step[1:])
                dve_chain.end()

            def last_norm(blk):
                dve.wait_ge(end_rstd.sem, blk + 1)
                dve.wait_ge(end_gain.sem, 16 * (blk + 1))
                for t in range(TT):
                    stt(xs[:, t] if blk else xv[:, t], xv[:, t], x_rstd[:, t:t + 1], final_gain, ALU.mult, ALU.mult)\
                        .then_inc(end_out.sem, 1)
                if blk == 0:
                    dve.wait_ge(end_out.sem, TT)
                    dve.memset(stat_all[:, 32:33], 0.0).then_inc(x_new.sem, 1)

            n_link = [0]

            def setup_link(ins):
                n_link[0] += 1
                ins.then_inc(setup_chain, 1)
                dve.wait_ge(setup_chain, n_link[0])

            dve.wait_ge(setup_shared.sem, 16 * (5 * DEPTH + 2))
            lr = v(lam_rows, l=DEPTH, r=4, d=A_QK)
            setup_link(tt(lam_p[:, :, :, :], lr[:, :, 0:4:2, :], lr[:, :, 1:4:2, :], ALU.mult))
            dve.reduce_sum(lam_s, lam_p[:, :, :, :], X).then_inc(setup_dve.sem, 1)
            setup_link(dve.tensor_copy(pos_f[:, :], pos_i[:, :]))
            dve.wait_ge(setup_dma.sem, ROWS_LANDED)
            n_f = M_ROPE // 2
            setup_link(tt(ang[:, :, :], over(pos_f[:, :], n_f), again(cst("inv_freq"), TT), ALU.mult))
            two_pi = 2.0 * math.pi
            c1 = float(np.float32(6.28125))
            c2 = float(np.float32(np.floor((two_pi - c1) * 2 ** 21) / 2 ** 21))
            c3 = float(np.float32(two_pi - c1 - c2))
            magic = 12582912.0
            for i, turn_ in enumerate((0.25, 0.0)):
                k_ = turns[:, i]
                setup_link(dve.tensor_scalar(k_, ang[:, :, :], 1.0 / two_pi, turn_, ALU.mult, ALU.add))
                setup_link(dve.tensor_scalar(k_, k_, magic, None, ALU.add))
                setup_link(dve.tensor_scalar(k_, k_, -magic, None, ALU.add))
                t_ = trig[:, i]
                setup_link(stt(t_, k_, -c1, ang[:, :, :], ALU.mult, ALU.add))
                setup_link(stt(t_, k_, -c2, t_, ALU.mult, ALU.add))
                setup_link(stt(t_, k_, -c3, t_, ALU.mult, ALU.add))
                setup_link(dve.tensor_scalar(t_, t_, math.pi / 2 if i == 0 else 0.0, None, ALU.add))
                ins = dve.tensor_scalar(t_, t_, 3.1415925, -3.1415925, ALU.min, ALU.max)
                setup_link(ins)
            setup_link(dve.memset(stat_all[:, 33:34], 0.0))
            dve.memset(stat_all[:, 33:34], 0.0).then_inc(setup_dve.sem, 1)
            dve.wait_ge(setup_act.sem, 1)
            le = lam_e
            for l in range(DEPTH):
                dst = par1[:, l, PAR1["neg_lam"]:PAR1["neg_lam"] + 1]
                setup_link(tt(dst, le[:, l, 1:2], le[:, l, 0:1], ALU.subtract))
                setup_link(dve.tensor_scalar(dst, dst, -LAMBDA_INIT[l], None, ALU.add))
                g_ = par1[:, l, PAR1["subln"]:PAR1["subln"] + A_V]
                dve.tensor_scalar(g_, g_, 1.0 - LAMBDA_INIT[l], None, ALU.mult)
                g_ = par2[:, l, PAR2["neg_a"]:PAR2["neg_a"] + 8]
                dve.tensor_scalar(g_, g_, -1.0, None, ALU.mult)
                g_ = par2[:, l, PAR2["o_norm"]:PAR2["o_norm"] + HD]
                dve.tensor_scalar(g_, g_, 0.5, None, ALU.mult)
            dve.wait_ge(setup_act.sem, 2)
            for half_ in range(2):
                dve.tensor_copy(pcos[:, :, n_f * half_:n_f * (half_ + 1)], trig[:, 0])
            dve.tensor_copy(psin[:, :, :], trig[:, 1])
            dve.tensor_scalar(pnsin[:, :, :], trig[:, 1], -1.0, None, ALU.mult)
            dve.wait_ge(setup_pe.sem, 1)
            for i, n in enumerate((NR1, NR1, NR2, NR2)):
                dst = (par1 if i < 2 else par2)[:, i % 2, 0:n]
                setup_link(dve.tensor_copy(dst, bank[0][:, i * P:i * P + n]))
            g_ = par2[:, :, PAR2["b_gate_2"]:PAR2["b_gate_2"] + 24]
            setup_link(dve.tensor_scalar(g_, g_, 0.5, None, ALU.mult))
            dve.wait_ge(setup_x.sem, 16)
            dve.memset(stat_all[:, 32:33], 0.0).then_inc(x_new.sem, 1)
            layers(dve, 0, layer)
            last_norm(0)
            layers(dve, 1, layer)
            last_norm(1)

        @block.gpsimd
        def _(pool):
            link = pool_chain.link

            def tt(o, i0, i1, op):
                return pool.tensor_tensor(o, i0, i1, op)

            def root(var, o, n, done):
                return tt(o, var, neg_half[:, 0:n], ALU.pow).then_inc(done.sem, 1)

            def norm(L, m, t, h):
                if (t, h) != (0, 0):
                    return
                pool.wait_ge(*ss_done(L, 2 * m + 2))
                link(tt(x_var, x_ss, cst("eps")[:, 0:TT], ALU.add))
                root(x_var, x_rstd, TT, rstd_done)

            def rotate(src, lo, hi, cos, nsin, sin, ta, tb, done):
                tt(ta, src, cos, ALU.mult)
                tt(tb[0], hi, nsin, ALU.mult)
                link(tt(tb[1], lo, sin, ALU.mult))
                return tt(src, ta, tb[2], ALU.add)

            def rope_attention(L, t):
                n = A_ROT // 2
                src = v(aqk[:, t], g=16, d=A_QK)
                ta, tb = v(rope_a[:, 0:256], g=16, d=A_ROT), v(rope_b[:, 0:256], g=16, d=A_ROT)

                def table(name, w):
                    return v(cst(name), t=TT, n=w)[:, t].unsqueeze(1).to_broadcast([P, 16, w])

                rotate(src[:, :, 0:A_ROT], src[:, :, 0:n], src[:, :, n:A_ROT], table("rope_cos", A_ROT),
                       table("rope_nsin", n), table("rope_sin", n), ta,
                       (tb[:, :, 0:n], tb[:, :, n:A_ROT], tb), None).then_inc(roped.sem, 1)
                pool.wait_ge(*roped(L, t + 1))

            def rope_retention(L, t):
                n = R_QK // 2
                src = v(rqk[:, t], w=2, h=4, d=R_QK)
                ta, tb = v(rope_a, w=2, h=4, d=R_QK), v(rope_b, w=2, h=4, d=R_QK)

                def table(name, w_):
                    t_ = v(cst(name), t=TT, w=2, n=w_)[:, t]
                    return t_.unsqueeze(2).to_broadcast([P, 2, 4, w_])

                cos, nsin, sin = table("ret_cos", R_QK), table("ret_nsin", n), table("ret_sin", n)
                for w in range(2):
                    rotate(src[:, w], src[:, w, :, 0:n], src[:, w, :, n:R_QK], cos[:, w], nsin[:, w], sin[:, w],
                           ta[:, w], (tb[:, w, :, 0:n], tb[:, w, :, n:R_QK], tb[:, w]), None)\
                        .then_inc(*((roped.sem, 1) if w else (pool_half, 1)))
                pool.wait_ge(*roped(L, t + 3))

            def d1(L, o):
                n, part = o // 2, o % 2
                if n == 1:
                    pool.wait_ge(*drained(L, ("d", part)))
                    pool.wait_ge(*drained(L, ("d", 2 + part)))
                    rope_attention(L, part)
                elif n == 2:
                    pool.wait_ge(*drained(L, ("d", o)))
                    rope_retention(L, part)
                    if part == 1:
                        tt(v(kz, h=4, d=R_QK), v(rqk[:, 0], w=2, h=4, d=R_QK)[:, 1],
                           cst("zeta").unsqueeze(2).to_broadcast([P, 4, R_QK]), ALU.mult).then_inc(roped.sem, 1)

            def branch(L, i, jp):
                order = (1, 0, 2) if L[0] == 0 else (0, 1, 2)
                n = order.index(i) * 4 + jp
                if n < 4:
                    return
                pool.wait_ge(*drained(L, ("br", i, jp)))
                if n >= 8:
                    pool.wait_ge(*added(L, n - 7))
                o = merged[:, 2 * jp:2 * jp + 2].rearrange("p a b -> p (a b)")
                tt(o, o, br_tmps[L[0]][:, n % 2], ALU.add).then_inc(added.sem, 1)

            def finish(L, kind, qb):
                if kind == "diff":
                    pool.wait_ge(*o_var(L, qb + 1))
                    root(a_ss[:, 4 * qb:4 * qb + 4], a_rs[:, 4 * qb:4 * qb + 4], 4, o_rstd)

            def r_finish(L, t):
                pool.wait_ge(*o_var(L, 2 + t + 1))
                root(r_ss2[:, 4 * t:4 * t + 4], r_rs2[:, 4 * t:4 * t + 4], 4, o_rstd)

            def small_values(L):
                pool.wait_ge(*m_ss_done(L, 1))
                ss_, rs_ = (t_[:, :, :].rearrange("p a b -> p (a b)") for t_ in (m_ss, m_rstd))
                link(tt(ss_, ss_, cst("eps")[:, 0:4], ALU.add))
                link(tt(rs_, ss_, neg_half[:, 0:4], ALU.pow))
                n = M_ROPE // 2
                for t in range(TT):
                    kr = mraw[:, t, 392:424]
                    tt(mraw[:, t, 8:264], mraw[:, t, 8:264], m_rstd[:, t, 0:1].to_broadcast([P, M_QR]), ALU.mult)
                    tt(mraw[:, t, 264:392], mraw[:, t, 264:392], m_rstd[:, t, 1:2].to_broadcast([P, M_KVR]), ALU.mult)\
                        .then_inc(m_norm_done.sem, 1)
                    tb = m_rope_b[:, 0:M_ROPE]
                    link(rotate(kr, kr[:, 0:n], kr[:, n:M_ROPE], pcos[:, t], pnsin[:, t], psin[:, t],
                                m_rope_a[:, 0:M_ROPE], (tb[:, 0:n], tb[:, n:M_ROPE], tb), None))

            def up(L, t, i):
                if i != 3:
                    return
                for k in range(4):
                    pool.wait_ge(*drained(L, ("u", t, k)))
                n = M_ROPE // 2
                q_ = v(mqk[:, 0, t], h=8, n=M_QK)[:, :, HD:M_QK]

                def table(t_):
                    return t_[:, t].unsqueeze(1).to_broadcast([P, 8, t_.shape[2]])

                ta, tb = v(m_rope_a, h=8, n=M_ROPE), v(m_rope_b, h=8, n=M_ROPE)
                rotate(q_, q_[:, :, 0:n], q_[:, :, n:M_ROPE], table(pcos), table(pnsin), table(psin), ta,
                       (tb[:, :, 0:n], tb[:, :, n:M_ROPE], tb), None)
                pool.tensor_copy(v(mqk[:, 1, t], h=8, n=M_QK)[:, :, HD:M_QK],
                                 mraw[:, t, 392:424].unsqueeze(1).to_broadcast([P, 8, M_ROPE]))\
                    .then_inc(m_roped.sem, 1)
                pool.wait_ge(*m_roped(L, t + 1))

            def d_stats(L, t):
                pool.wait_ge(*l2_var(L, t + 1))
                pool.tensor_tensor(d_rs[:, 0:8], d_ss[:, 0:8], neg_half, ALU.pow)
                root(d_ss[:, 8:16], d_rs[:, 8:16], 8, l2_rstd)

            def d_scaled(L, t):
                def over(t_):
                    return t_.unsqueeze(2).to_broadcast([P, 8, HD])

                pool.wait_ge(*kn_done(L, t + 1))
                pool.wait_ge(*eg_done(L, t + 1))
                pool.wait_ge(*drained(L, ("DT", t, 2)))
                k_, kb = v(d_tok[:, 1], a=8, b=HD), v(d_kb, a=8, b=HD)
                tt(v(d_w, a=8, b=HD), kb, over(eg[:, 0:8]), ALU.mult)
                tt(v(d_vb, a=8, b=HD), v(d_tok[:, 2], a=8, b=HD), over(half_beta[:, t]), ALU.mult)
                tt(v(d_kdec, a=8, b=HD), k_, over(eg[:, 8:16]), ALU.mult).then_inc(kw_done.sem, 1)

            def level(L, t, b, g):
                if b == 2:
                    pool.wait_ge(*drained(L, ("K1", t, g)))
                else:
                    pool.wait_ge(*filled(L, ("Y", t, b // 2, g)))
                tt(d_C[:, 4 * g:4 * g + 4], d_M[:, 4 * g:4 * g + 4],
                   cst(f"below{b}").unsqueeze(1).to_broadcast([P, 4, P]), ALU.mult).then_inc(level_done.sem, 1)

            def d_finish(L, t):
                pool.wait_ge(*dn_var(L, t + 1))
                root(d_ss2[:, 8 * t:8 * t + 8], d_rs2[:, 8 * t:8 * t + 8], 8, dn_rstd)

            parts1 = {"norm": norm, "d": d1, "br": branch, "F": finish, "RF": r_finish}
            parts2 = {"norm": norm, "br": branch, "SM": small_values, "u": up, "DP": d_stats,
                      "DP2": d_scaled, "Y": level, "DF": d_finish}

            def layer(L):
                pool_chain.layer(pool, L)
                pool.wait_ge(*par_done(L, 1))
                for step in PLANS[L[0]].steps:
                    part = (parts1, parts2)[L[0]].get(step[0])
                    if part:
                        part(L, *step[1:])
                pool_chain.end()

            def last_norm(blk):
                pool.wait_ge(end_ss.sem, TT * (blk + 1))
                tt(x_var, x_ss, cst("eps")[:, 0:TT], ALU.add).then_inc(end_var, 1)
                pool.wait_ge(end_var, blk + 1)
                root(x_var, x_rstd, TT, end_rstd)

            layers(pool, 0, layer)
            last_norm(0)
            layers(pool, 1, layer)
            last_norm(1)


_INPUTS = ["x", "norm_g", "w_in", "attn_lambda", "attn_subln_g", "conv_w", "w_branch", "w_out", "final_norm_g",
           "positions_2", "ffn1_norm_2", "ffn1_w_gu_2", "ffn1_w_down_2", "mix_norm_2", "w_in_2", "b_gate_2",
           "fox_b_f_2", "mla_q_norm_2", "mla_w_uq_2", "mla_kv_norm_2", "mla_w_ukv_2", "dn_conv_w_2",
           "dn_a_log_2", "dn_dt_bias_2", "dn_o_norm_2", "w_br_fox_2", "w_br_mla_2", "w_br_dn_2", "w_out_2",
           "ffn2_norm_2", "ffn2_w_gu_2", "ffn2_w_down_2", "final_norm_2"]


def kernel(**inputs):
    import concourse.bacc as bacc
    from concourse.bass_utils import run_bass_kernel_spmd

    nc = bacc.Bacc("TRN2", target_bir_lowering=False, num_devices=1)
    arrays = {name: np.ascontiguousarray(inputs[name]) for name in _INPUTS}
    arrays["consts"] = CONSTS
    aps = {name: nc.dram_tensor(f"in_{name}", t.shape, mybir.dt.from_np(t.dtype), kind="ExternalInput").ap()
           for name, t in arrays.items()}
    out = nc.dram_tensor("out_x", (1, SEQ, DM), F32, kind="ExternalOutput").ap()
    build(nc, aps, out)
    result = run_bass_kernel_spmd(nc, [{f"in_{name}": t for name, t in arrays.items()}], core_ids=[0])
    return result.results[0]["out_x"]
```

```python
import math
from contextlib import ExitStack

import numpy as np

import concourse.bass as bass
from concourse import mybir
from concourse.alu_op_type import AluOpType as ALU

F32 = mybir.dt.float32
F32R = mybir.dt.float32r
I32 = mybir.dt.int32
ACT = mybir.ActivationFunctionType
X = mybir.AxisListType.X

P = 128
SEQ = 256
TT = SEQ // P
DM = 1024
KD = DM // P
DEPTH = 2
EPS = 1e-6
NEG = -1e30

A_HEADS, A_QK, A_V, A_ROT = 4, 64, 128, 16
R_HEADS, R_QK, R_V = 4, 64, 128
IN1 = 8704
D_FF = 2816
FT = D_FF // P
FOX_H, MLA_H, DN_H, HD = 8, 8, 8, 64
M_QR, M_KVR, M_ROPE, M_QK = 256, 128, 32, 96
IN2 = 7096
CHUNK = 64

RING = 4
SLOT = 2048
HIGHS = 3
DOWNS = FT // 2
HID = 8


def norm_steps(m):
    return [("norm", m, t, half) for t in range(TT) for half in range(2)]


def dense(a, b):
    return [("d", o) for o in range(a, b)]


LATENCY = {"DP": 3, "DG": 2, "R1": 1.5, "DP2": 4, "DX": 0.7, "K1": 1.5, "L1": 2, "Y": 1.6, "ZT": 1.5, "X1": 4, "X3": 2,
           "IN": 2, "DF": 4, "F": 3, "T": 1.5}


def merge(chain, filling):
    out, done, put = [], 0.0, 0
    total = sum(LATENCY.get(s[0], 1) for s in chain)
    for s in chain:
        out.append(s)
        done += LATENCY.get(s[0], 1)
        while put < len(filling) and done / total >= (put + 1) / (len(filling) + 1):
            out.append(filling[put])
            put += 1
    return out + filling[put:]


def attention_slots(kind):
    slots = []
    for s in range(10):
        if s < 8:
            slots.append(("S", kind, s))
        if 0 <= s - 1 < 8:
            slots.append(("T", kind, s - 1))
        if 0 <= s - 2 < 8:
            slots.append(("V", kind, s - 2))
        if s - 2 in (3, 7):
            slots.append(("F", kind, (s - 2) // 4))
        if s - 3 == 3:
            slots.append(("F2", kind, 0))
    return slots + [("F2", kind, 1), ("FT", kind, 0), ("FT", kind, 1)]


LAST_BRANCH = [("br", 2, 0), ("br", 2, 1), ("ms", 0), ("br", 2, 2), ("ms", 1), ("br", 2, 3), ("ms", 2), ("ms", 3)]

STEPS1 = (
    norm_steps(0) + dense(0, 6) + [("AT", 0), ("d", 6), ("AT", 1), ("d", 7), ("RT", 0), ("d", 8), ("RT", 1)]
    + merge(attention_slots("diff"), dense(9, 28))
    + merge([("RI", 0), ("RK",), ("RI", 1), ("RV", 0), ("RC",), ("RF", 0), ("RV", 1),
             ("RF2", 0), ("RF", 1)], dense(28, 34))
    + [("br", 1, jp) for jp in range(4)] + [("br", 0, 0), ("RFT", 0), ("RF2", 1), ("br", 0, 1), ("br", 0, 2), ("RFT", 1), ("br", 0, 3)]
    + LAST_BRANCH + [("wo", q) for q in range(4)]
)


def ffn_steps(f):
    out = []
    for j in range(FT):
        out.append(("gu", f, j))
        if j >= 1:
            out.append(("hs", f, j - 1))
        if j >= 3 and j % 2:
            out.append(("dn", f, (j - 3) // 2))
    return out + [("hs", f, FT - 1), ("dn", f, DOWNS - 1)]


def delta_steps(t):
    out = [("DT", t, s) for s in range(3)] + [("DP", t), ("DG", t), ("R1", t, 0), ("R1", t, 1), ("DP2", t)]
    out += [("DX", t, s, g) for s in range(3) for g in range(2)]
    for name in ("QK", "K1", "L1"):
        out += [(name, t, g) for g in range(2)]
    for b in (2, 4, 8, 16):
        out += [("Y", t, b, g) for g in range(2)] + [("Z", t, b, g) for g in range(2)]
    out += [("Y", t, 32, g) for g in range(2)] + [("ZT", t, g) for g in range(2)]
    out += [("W", t, g) for g in range(2)] + [("U", t)]
    if t:
        out.append(("DF2", t - 1))
    for c in range(2):
        out += [("X1", t, c), ("X2", t, c)]
        if (t, c) != (TT - 1, 1):
            out += [("X3", t, c)]
    return out + [("IN", t), ("DF", t)]


STEPS2 = (
    norm_steps(0) + ffn_steps(0) + norm_steps(1)
    + dense(0, 4) + [("SM",)] + dense(4, 7) + [("FC",), ("d", 7), ("MC", 0), ("MC", 1)]
    + merge(attention_slots("fox"), dense(8, 14))
    + [("u", t, i) for t in range(TT) for i in range(4)]
    + [("MT", t, w, half) for t in range(TT) for w in range(2) for half in range(2)]
    + merge(attention_slots("mla"), dense(14, 16))
    + merge(delta_steps(0) + delta_steps(1),
            dense(16, 28) + [("br", i, jp) for i in (0, 1) for jp in range(4)])
    + [("DFT", 0), ("DF2", 1), ("DFT", 1)]
    + LAST_BRANCH + [("wo", q) for q in range(4)]
    + norm_steps(2) + ffn_steps(1)
)


def banks_of(blk, step):
    k = step[0]
    if k in ("d", "u", "br", "wo"):
        return ["dense"]
    if k == "gu":
        return ["dense"]
    if k == "norm":
        return [4 + 2 * step[2] + step[3]]
    if k == "dn":
        return [4, 5, 6, 7] if step[2] == 0 else []
    if k == "S":
        return [4, 5]
    if k in ("T", "FT", "RFT", "DFT"):
        return [6]
    if k == "V":
        return [7]
    if k in ("R1", "QK", "K1", "L1", "Y", "W"):
        return [4 + step[-1]]
    if k in ("DX", "MT", "ZT"):
        return [6 + step[-1]]
    if k == "Z":
        return [6 + step[-1], 4 + step[-1]]
    return {"AT": [6, 7], "RT": [7], "RI": [4, 5], "RK": [6], "RV": [7], "RC": [4, 5], "FC": [7],
            "MC": [7], "DT": [6], "DG": [7], "U": [6], "X1": [4], "X2": [5], "X3": [6],
            "IN": [7]}.get(k, [])


def piece_of(blk, step):
    k = step[0]
    if k == "d":
        return ("in", step[1])
    if k == "br":
        return ("br", step[1], step[2] // 2)
    if k == "wo":
        return ("wo", step[1])
    if k == "u":
        return ("u", step[2] // 2)
    if k == "gu":
        return ("gu", step[1], step[2])
    if k == "dn":
        return ("down", step[1], step[2])
    return None


class Plan:

    def __init__(self, blk, steps):
        self.steps, self.uses, self.dense_uses = steps, {}, 0
        self.per_layer = [0] * 8
        self.pieces, self.slot, self.last = [], {}, {}
        for s in steps:
            got = []
            for b in banks_of(blk, s):
                if b == "dense":
                    b = self.dense_uses % 4
                    self.dense_uses += 1
                got.append((b, self.per_layer[b]))
                self.per_layer[b] += 1
            self.uses[s] = got
            p = piece_of(blk, s)
            if p is not None:
                if p not in self.slot:
                    self.slot[p] = 0
                    self.pieces.append(p)
                self.last[p] = s
        self.split = [p for p in self.pieces if p[0] not in ("br", "u")]
        self.n_split = {p: m for m, p in enumerate(self.split)}
        n, m = len(self.pieces), len(self.split)
        n_from = self.pieces.index(("u", 0)) if blk else 0
        m_from = self.split.index(("in", 14) if blk else ("wo", 0))
        self.slot = {p: (i + (-n % RING if i >= n_from else 0)) % RING for i, p in enumerate(self.pieces)}
        self.high = {p: (i + (-m % HIGHS if i >= m_from else 0)) % HIGHS for i, p in enumerate(self.split)}
        at = {s: i for i, s in enumerate(steps)}

        def before_in(ring, p):
            same = [q for q in ring if ring[q] == ring[p]]
            return same[same.index(p) - 1] if same.index(p) else None

        self.before_in_slot = {p: before_in(self.slot, p) for p in self.pieces}
        self.before_in_high = {p: before_in(self.high, p) for p in self.split}
        self.last_in_slot = {self.slot[p]: p for p in self.pieces}
        self.last_in_high = {self.high[p]: p for p in self.split}
        splits_at = {}
        for m, p in enumerate(self.split):
            n = self.pieces.index(p)
            first_use = min(i for s, i in at.items() if piece_of(blk, s) == p)
            freed = [at[self.last[q]] for k in range(n + 1)
                     for q in [self.before_in_slot[self.pieces[k]]] if q is not None]
            after = 3 if m else -1
            if freed:
                later = [i for s, i in at.items() if max(freed) < i < first_use and piece_of(blk, s)]
                after = max(after, min(later) if later else max(freed))
            for q in self.split[:m + 1]:
                if self.before_in_high[q] is not None:
                    after = max(after, at[self.last[self.before_in_high[q]]])
            assert after < first_use, (blk, p)
            splits_at.setdefault(after, []).append(("split", p))
        self.steps = list(splits_at.get(-1, []))
        for i, s in enumerate(steps):
            self.steps += [s] + splits_at.get(i, [])


PLANS = [Plan(0, STEPS1), Plan(1, STEPS2)]


def shape_constants():
    f = np.float32
    i, j = np.arange(P)[:, None], np.arange(P)[None, :]
    cols, at = [], {}

    def add(name, a):
        a = np.asarray(a, np.float64).astype(f).reshape(P, -1)
        at[name] = (sum(c.shape[1] for c in cols), a.shape[1])
        cols.append(a)

    add("ident", np.eye(P))
    add("causal", np.concatenate([np.zeros((P, P)), np.where(j > i, NEG, 0.0)], 1))
    for b in (1, 2, 4, 8, 16, 32):
        add(f"below{b}", -1.0 * ((i // (2 * b) == j // (2 * b)) & (j % (2 * b) >= b) & (i % (2 * b) < b)))
    same = i // CHUNK == j // CHUNK
    add("decay_mask", np.where((j >= i) & same, 0.0, NEG))
    add("tri", 1.0 * (i <= j))
    add("tri_chunk", 1.0 * ((i <= j) & same))
    add("same_chunk", 1.0 * same)
    add("ones", np.ones((P, P)))
    log_g = np.log(1.0 - 2.0 ** (-5.0 - np.arange(R_HEADS)))
    add("ret_decay", np.stack([np.where(j >= i, np.exp(np.maximum(j - i, 0) * g), 0.0) for g in log_g], 1))
    add("zeta", np.exp((P - 1 - np.arange(P))[:, None] * log_g[None]))
    add("xi", np.exp((np.arange(P) + 1.0)[:, None] * log_g[None]))
    pos = np.arange(SEQ, dtype=f).reshape(TT, P)
    inv = (500000.0 ** (-np.arange(0, A_ROT, 2) / A_ROT)).astype(f)
    ang = (pos[..., None] * inv).astype(f).astype(np.float64).transpose(1, 0, 2)
    add("rope_cos", np.concatenate([np.cos(ang)] * 2, -1))
    add("rope_nsin", -np.sin(ang))
    add("rope_sin", np.sin(ang))
    inv = (1.0 / (10000.0 ** np.linspace(0.0, 1.0, R_QK // 2))).astype(f)
    ang = (pos[..., None] * inv).astype(f).astype(np.float64).transpose(1, 0, 2)
    k_scale = np.array([1.0, R_QK ** -0.5])[None, None, :, None]
    add("ret_cos", np.concatenate([np.cos(ang)] * 2, -1)[:, :, None] * k_scale)
    add("ret_nsin", -np.sin(ang)[:, :, None] * k_scale)
    add("ret_sin", np.sin(ang)[:, :, None] * k_scale)
    add("inv_freq", np.tile((10000.0 ** (-np.arange(M_ROPE // 2) / (M_ROPE // 2))).astype(f), (P, 1)))
    add("minus_half", np.full((P, 16), -0.5))
    add("eps", np.full((P, 8), EPS))
    return np.concatenate(cols, 1), at


CONSTS, CONST_AT = shape_constants()

ROWS1 = [("norm_g", 8), ("conv_w", 12)]
ROWS2 = [("ffn1_norm_2", 8), ("mix_norm_2", 8), ("ffn2_norm_2", 8), ("b_gate_2", 24),
         ("dn_conv_w_2", 48), ("mla_q_norm_2", 2), ("mla_kv_norm_2", 1)]
NR1, NR2 = sum(n for _, n in ROWS1), sum(n for _, n in ROWS2)
PAR1 = {"norm_g": 0, "conv_w": 8, "neg_lam": NR1, "subln": NR1 + 1}
NP1 = NR1 + 1 + A_V
PAR2 = {"ffn1_norm_2": 0, "mix_norm_2": 8, "ffn2_norm_2": 16, "b_gate_2": 24, "dn_conv_w_2": 48,
        "mla_q_norm_2": 96, "mla_kv_norm_2": 98, "f_bias": NR2, "dt_bias": NR2 + 8, "neg_a": NR2 + 16,
        "o_norm": NR2 + 24}
NP2 = NR2 + 24 + HD

LAMBDA_INIT = [0.8 - 0.6 * math.exp(-0.3 * layer) for layer in range(DEPTH)]


def build(nc, a, out):
    stack = ExitStack()
    with stack:
        def sb(name, n, dt=F32):
            return stack.enter_context(nc.sbuf_tensor(name, [P, n], dt))

        def sb_split(name, n):
            with nc.sbuf_tensor(name, [P, n], F32) as values:
                pass
            return values, sb(name + "_low", n, F32R)

        def v(ap, **kw):
            names = list(kw)
            return ap.rearrange("p (%s) -> p %s" % (" ".join(names), " ".join(names)),
                                **{n: kw[n] for n in names[:-1]})

        const = sb("const", CONSTS.shape[1])

        def cst(name):
            o, n = CONST_AT[name]
            return const[:, o:o + n]

        ident = cst("ident")
        x = sb("x", TT * DM)
        xv = v(x[:, :], t=TT, n=DM)
        h_raw_, h_low_ = sb_split("hT", KD * SEQ)
        hT = v(h_raw_[:, :], k=KD, n=SEQ)
        merged = hT
        h_low = v(h_low_[:, :], k=KD, n=SEQ)
        h_high = v(sb("h_high", KD * SEQ, F32R)[:, :], k=KD, n=SEQ)
        ring, ring_low = sb_split("ring", RING * SLOT)
        ring_high = sb("ring_high", HIGHS * SLOT, F32R)

        gates_, gates_low = sb_split("gates", 3 * KD * SEQ)
        gates = v(gates_[:, :], i=3, j=KD, n=SEQ)
        xs = v(gates_[:, 0:TT * DM], t=TT, n=DM)
        squares = v(gates_[:, 2048:4096], t=TT, n=DM)
        diag = v(gates_[:, 0:TT * P], t=TT, n=P)
        hid = v(gates_[:, 0:HID * SEQ], j=HID, n=SEQ)
        hid_low = v(gates_low[:, 0:HID * SEQ], j=HID, n=SEQ)
        hid_high = v(gates_low[:, 4096:4096 + HID * SEQ], j=HID, n=SEQ)
        ffn_tanh = v(gates_[:, 2048:2048 + 4 * SEQ], j=4, n=SEQ)
        ffn_gate = v(gates_[:, 3072:3072 + 4 * SEQ], j=4, n=SEQ)
        par1 = v(sb("par1", DEPTH * NP1)[:, :], l=DEPTH, n=NP1)
        par2 = v(sb("par2", DEPTH * NP2)[:, :], l=DEPTH, n=NP2)
        par = sb("par", max(NP1, NP2))
        stat = sb("stat", 8)
        pos_tab = sb("pos_tab", TT * 64)
        pcos = v(pos_tab[:, 0:64], t=TT, n=32)
        pnsin = v(pos_tab[:, 64:96], t=TT, n=16)
        psin = v(pos_tab[:, 96:128], t=TT, n=16)

        SCRATCH = 22200
        stat_all = sb("stat_all", 40)
        stat2 = sb("stat2", 48)
        x_ss, x_var, x_rstd = stat_all[:, 24:26], stat_all[:, 26:28], stat_all[:, 28:30]
        neg_half = cst("minus_half")
        scratch = sb("scratch", SCRATCH)
        final_gain = scratch[:, 0:DM]

        class Room:

            def __init__(self, memory, size, at=0):
                self.memory, self.size, self.at = memory, size, at

            def take(self, **kw):
                n = math.prod(kw.values())
                assert self.at + n <= self.size, (self.at, n, self.size)
                view = self.memory[:, self.at:self.at + n]
                self.at += n
                return v(view, **kw) if len(kw) > 1 else view

        def par_(name, n, table):
            return par[:, table[name]:table[name] + n]

        r = Room(scratch, SCRATCH)
        fox_T = r.take(j=4, n=SEQ)
        mla_T = r.take(j=4, n=SEQ)
        conv_y = r.take(s=3, j=4, n=SEQ)
        dz = r.take(t=TT, n=512)
        small = Room(scratch, SCRATCH, r.at)
        r.at += 640
        delta_from = r.at
        at_sc = r.take(u=2, c=2, n=SEQ)
        at_wT = r.take(u=2, n=2 * SEQ)
        at_bias = r.take(u=2, c=2)
        at_max = r.take(u=2, c=2)
        at_sum = r.take(t=TT, h=8)
        at_rcp = r.take(t=TT, h=8)
        at_o = r.take(t=TT, n=512)
        at_sq = r.take(n=512)
        th = r.take(u=2, n=512)
        attention_to = r.at
        fqT = r.take(j=4, n=SEQ)
        fkT = r.take(j=4, n=SEQ)
        fv = r.take(t=TT, n=512)
        craw = r.take(u=2, j=2, n=SEQ)
        both = v(scratch[:, attention_to:attention_to + 4096], w=2, h=8, n=SEQ)
        mqkT = both
        neg_c = r.take(n=SEQ)
        mv = r.take(t=TT, n=512)
        g = Room(gates_, 3 * KD * SEQ)
        mraw = g.take(t=TT, n=440)
        cT3 = g.take(j=3, n=SEQ)
        mqk = g.take(w=2, t=TT, n=MLA_H * M_QK)
        m_rope_a = g.take(n=256)
        m_rope_b = g.take(n=256)
        z = small.take(t=TT, n=16)
        z_abs = small.take(t=TT, n=16)
        z_log = small.take(t=TT, n=16)
        beta_t = small.take(t=TT, n=8)
        beta = small.take(t=TT, n=8)
        half_beta = small.take(t=TT, n=8)
        log_f = small.take(t=TT, n=8)
        dgate = small.take(t=TT, n=8)
        m_ss = small.take(t=TT, n=2)
        m_rstd = small.take(t=TT, n=2)
        gc = small.take(n=24)
        eg = small.take(n=16)
        gl_raw = small.take(c=2, h=8)
        gl = small.take(c=2, h=8)
        gc_rows = small.take(n=P)
        d_ss = small.take(n=16)
        d_rs = small.take(n=16)
        r = Room(scratch, SCRATCH, delta_from)
        d_tok = r.take(s=3, n=512)
        d_kb = r.take(n=512)
        d_w = r.take(n=512)
        d_vb = r.take(n=512)
        d_kdec = r.take(n=512)
        d_T3 = r.take(s=3, h=8, n=P)
        d_decay = r.take(h=8, n=P)
        d_M = r.take(h=8, n=P)
        d_QK = r.take(h=8, n=P)
        d_inv = r.take(h=8, n=P)
        d_invT = r.take(h=8, n=P)
        d_wT = r.take(h=8, n=P)
        d_S = r.take(n=512)
        d_S1 = r.take(n=512)
        d_cross = r.take(n=512)
        br_tmp2 = r.take(u=2, n=512)
        d_sq, d_o = d_S1, d_cross
        d_C = d_decay
        d_Y = d_T3[:, 2]
        d_u = d_kb
        d_vn = d_tok[:, 0]
        dn_T = conv_y[:, 0]
        r = Room(scratch, SCRATCH, attention_to)
        at_w = r.take(u=2, n=SEQ)
        aqk = r.take(t=TT, n=1024)
        rqk = r.take(t=TT, n=512)
        av = r.take(t=TT, n=512)
        rv = r.take(t=TT, n=512)
        az = r.take(t=TT, n=512)
        r = Room(scratch, SCRATCH)
        aqT = r.take(j=4, n=SEQ)
        akT = r.take(j=4, n=SEQ)
        rqkT = r.take(j=4, n=SEQ)
        cu = r.take(j=4, n=SEQ)
        cy = r.take(j=4, n=SEQ)
        rz = r.take(t=TT, n=512)
        assert r.at <= delta_from
        r = Room(scratch, SCRATCH, attention_to + 512 + 2048 + 4096)
        kz = r.take(n=256)
        r_state = r.take(n=256)
        rope_a = r.take(n=512)
        rope_b = r.take(n=512)
        th_c = r.take(u=2, n=512)
        inner = v(aqk[:, 0], t=TT, n=512)
        r_cross = aqk[:, 1, 0:512]
        r_sq = aqk[:, 1, 512:1024]
        r_o = rqk
        br_tmps = v(scratch[:, delta_from:delta_from + 1024], u=2, n=512), br_tmp2
        aT, rT, cT = aqT, akT, cu
        a_ss = stat_all[:, 8:16]
        a_rs = stat_all[:, 16:24]
        r_ss2, r_rs2 = stat2[:, 0:8], stat2[:, 8:16]
        d_ss2, d_rs2 = stat2[:, 16:32], stat2[:, 32:48]
        m_junk = g.take(t=TT, n=M_QR + M_KVR)
        g0 = Room(gates_, 3 * KD * SEQ, 4096)
        par_rows = g0.take(i=2 * DEPTH, n=P)
        lam_rows = g0.take(n=DEPTH * 4 * A_QK)
        lam_p = g0.take(l=DEPTH, r=2, d=A_QK)
        lam_s = g0.take(l=DEPTH, r=2)
        lam_e = g0.take(l=DEPTH, r=2)
        pos_f = g0.take(t=TT, o=1).rearrange("p t o -> p (t o)")
        ang = g0.take(t=TT, n=M_ROPE // 2)
        turns = g0.take(i=2, t=TT, n=M_ROPE // 2)
        trig = g0.take(i=2, t=TT, n=M_ROPE // 2)
        pos_i = sb("pos_i", TT, I32)

        bank = [stack.enter_context(nc.psum_tensor(f"bank{b}", [P, 512], F32)) for b in range(8)]

        class Signal:
            def __init__(self, name, k1=0, k2=0, before=0, between=0):
                self.sem = stack.enter_context(nc.semaphore(name))
                self.k, self.start = (k1, k2), (before, before + DEPTH * k1 + between)

            def __call__(self, L, n):
                blk, l = L
                if self.k[blk] == 0:
                    return self.sem, self.start[blk] + n
                return self.sem, l * self.k[blk] + (self.start[blk] + n)

        filled_ = [Signal(f"filled{b}", *(p.per_layer[b] for p in PLANS), before=PLANS[0].per_layer[b])
                   for b in range(8)]
        drained_ = [Signal(f"drained{b}", *(p.per_layer[b] for p in PLANS)) for b in range(8)]

        def filled(L, step, j=0):
            b, n = PLANS[L[0]].uses[step][j]
            return filled_[b](L, n + 1)

        def drained(L, step, j=0):
            b, n = PLANS[L[0]].uses[step][j]
            return drained_[b](L, n + 1)

        def bank_of(L, step, j=0):
            return bank[PLANS[L[0]].uses[step][j][0]]

        def fills(L, step, j=0):
            return filled_[PLANS[L[0]].uses[step][j][0]].sem

        def drains(L, step, j=0):
            return drained_[PLANS[L[0]].uses[step][j][0]].sem

        def dmas_of(blk, piece):
            kind = piece[0]
            if kind == "gu":
                f, j = piece[1:]
                w = f"ffn{f + 1}_w_gu_2"
                return [(w, 0, KD, P * j, P, 0, 256), (w, 0, KD, D_FF + P * j, P, P, 256)]
            if kind == "down":
                f, d = piece[1:]
                return [(f"ffn{f + 1}_w_down_2", 256 * d, 2, 0, DM, 0, DM)]
            if kind == "u":
                return [(("mla_w_uq_2", 0, 2, 0, 768, 0, 768), ("mla_w_ukv_2", 0, 1, 0, 1024, 0, 1024))[piece[1]]]
            if kind == "br":
                i, h = piece[1:]
                name, row = (("w_branch", 512 * i) if blk == 0 else
                             (("w_br_fox_2", "w_br_mla_2", "w_br_dn_2")[i], 0))
                return [(name, row, 4, 512 * h, 512, 0, 512)]
            if kind == "wo":
                return [("w_out" if blk == 0 else "w_out_2", 0, KD, 256 * piece[1], 256, 0, 256)]
            n, h = piece[1] // 2, piece[1] % 2
            if blk == 0:
                start = [0, 512, 4096, 1024, 4608, 1536, 5120, 2048, 3072, 2560, 3584]
                return [("w_in", 0, KD, (start[n] if n < 11 else 5632 + 512 * (n - 11)) + 256 * h, 256, 0, 256)]
            if n == 0:
                return [("w_in_2", 0, KD, 1536, 256, 0, 256)] if h == 0 else \
                    [("w_in_2", 0, KD, 1720, 240, 0, 256), ("w_in_2", 0, KD, 4008, 16, 240, 256)]
            start = [None, 0, 512, 1024, 1960, 2472, 2984, 3496]
            return [("w_in_2", 0, KD, (start[n] if n < 8 else 4024 + 512 * (n - 8)) + 256 * h, 256, 0, 256)]

        landed_count = [{}, {}]
        slot_total = [[0] * RING, [0] * RING]
        for blk in range(2):
            for piece in PLANS[blk].pieces:
                s = PLANS[blk].slot[piece]
                slot_total[blk][s] += 16 * len(dmas_of(blk, piece))
                landed_count[blk][piece] = slot_total[blk][s]
        landed_ = [Signal(f"weights_landed{s}", slot_total[0][s], slot_total[1][s]) for s in range(RING)]

        def landed(L, piece):
            return landed_[PLANS[L[0]].slot[piece]](L, landed_count[L[0]][piece])

        def in_slot(memory, n, tiles, width):
            return v(memory[:, n * SLOT:n * SLOT + tiles * width], k=tiles, n=width)

        def weights(L, piece, tiles, width):
            return in_slot(ring, PLANS[L[0]].slot[piece], tiles, width)

        def weights_split(L, piece, tiles, width):
            return (in_slot(ring_high, PLANS[L[0]].high[piece], tiles, width),
                    in_slot(ring_low, PLANS[L[0]].slot[piece], tiles, width))

        def used(L, piece):
            step = PLANS[L[0]].last[piece]
            if step[0] != "dn":
                return filled(L, step)
            if step[2] < DOWNS - 1:
                return hid_used(L, step[1] * (DOWNS - 1) + step[2] + 1)
            return filled(L, ("dn", step[1], 0), 3)

        w_high = Signal("w_high", *(len(p.split) for p in PLANS))
        w_low = Signal("w_low", *(len(p.split) for p in PLANS))
        x_high = Signal("x_high", 4, 12)
        x_low = Signal("x_low", 4, 12)
        m_high = Signal("m_high", 4, 4)
        m_low = Signal("m_low", 4, 4)
        hid_hi_done = Signal("hid_hi_done", 0, 2 * FT)
        hid_lo_done = Signal("hid_lo_done", 0, 2 * FT)
        x_new = Signal("x_new", 1, 3, before=1, between=1)
        ss_done = Signal("ss_done", 2, 6)
        rstd_done = Signal("rstd_done", 1, 3)
        diag_done = Signal("diag_done", 2, 6)
        end_ss = Signal("end_ss", 0, 0)
        end_rstd = Signal("end_rstd")
        end_gain = Signal("end_gain")
        end_out = Signal("end_out")
        bias_done = Signal("bias_done", 8, 16)
        exp_done = Signal("exp_done", 16, 32)
        mix_done = Signal("mix_done", 8, 0)
        o_var = Signal("o_var", 4, 0)
        o_rstd = Signal("o_rstd", 4, 0)
        o_done = Signal("o_done", 4, 6)
        tanh_done = Signal("tanh_done", 6, 2)
        par_done = Signal("par_done", 1, 1)
        roped = Signal("roped", 5, 0)
        c_done = Signal("c_done", 2, 0)
        added = Signal("added", 4, 4)
        summed = Signal("summed", 4, 4)
        ffn_tanh_done = Signal("ffn_tanh_done", 0, 2 * FT)
        hid_used = Signal("hid_used", 0, 2 * (DOWNS - 1))
        craw_done = Signal("craw_done", 0, 6)
        taps_done = Signal("taps_done", 0, 6)
        ctanh_done = Signal("ctanh_done", 0, 6)
        conv2_done = Signal("conv2_done", 0, 6)
        z_done = Signal("z_done", 0, 1)
        zlog_done = Signal("zlog_done", 0, 1)
        small_done = Signal("small_done", 0, 1)
        m_ss_done = Signal("m_ss_done", 0, 1)
        m_norm_done = Signal("m_norm_done", 0, 2)
        m_roped = Signal("m_roped", 0, 2)
        dlt_done = Signal("dlt_done", 0, 2)
        eg_done = Signal("eg_done", 0, 2)
        l2_var = Signal("l2_var", 0, 2)
        l2_rstd = Signal("l2_rstd", 0, 2)
        kn_done = Signal("kn_done", 0, 2)
        kw_done = Signal("kw_done", 0, 2)
        arg_done = Signal("arg_done", 0, 4)
        decay_done = Signal("decay_done", 0, 4)
        inv2_done = Signal("inv2_done", 0, 4)
        level_done = Signal("level_done", 0, 20)
        state_zero = Signal("state_zero", 0, 1)
        dn_var = Signal("dn_var", 0, 2)
        dn_rstd = Signal("dn_rstd", 0, 2)
        setup_const = Signal("setup_const")
        setup_dma = Signal("setup_dma")
        setup_x = Signal("setup_x")
        setup_pe = Signal("setup_pe")
        setup_act = Signal("setup_act")
        setup_dve = Signal("setup_dve")

        setup_shared = Signal("setup_shared")
        setup_chain = stack.enter_context(nc.semaphore("setup_chain"))
        end_var = stack.enter_context(nc.semaphore("end_var"))
        stored = stack.enter_context(nc.semaphore("stored"))
        waits_met = stack.enter_context(nc.semaphore("waits_met"))
        pool_half = stack.enter_context(nc.semaphore("pool_half"))
        ROWS_LANDED = 16 * (len(ROWS1) + len(ROWS2))
        SHARED_LANDED = 16 * (5 + 2)
        FOX_DONE = 4

        class Chain:

            def __init__(self, name, k1, k2, before):
                self.links = Signal(name, k1, k2, before=before)
                self.n, self.before = 0, before

            def layer(self, eng, L):
                self.eng, self.L, self.n = eng, L, 0

            def link(self, ins):
                self.n += 1
                ins.then_inc(self.links.sem, 1)
                self.eng.wait_ge(*self.links(self.L, self.n))

            def end(self):
                k = self.links.k[self.L[0]]
                assert self.n < k, (self.n, k)
                self.eng.sem_inc(self.links.sem, k - self.n)

        block = stack.enter_context(nc.Block())
        dve_chain = Chain("dve_chain", 120, 300, 0)
        pool_chain = Chain("pool_chain", 60, 100, 0)
        act_chain = Chain("act_chain", 10, 10, 0)
        def layers(eng, blk, layer):
            with eng.Fori(0, DEPTH) as l:
                layer((blk, l))

        def of_layer(t, l):
            if isinstance(l, int):
                return t[l]
            names = " ".join("abcd"[:len(t.shape) - 1])
            first = names.split()[0]
            return t[bass.ds(l, 1)].rearrange(f"o {names} -> (o {first}){names[1:]}")

        def quarter_of(t_, k0, k1, n0, n1):
            return t_[:, k0:k1, n0:n1]

        FOX_SCALE = HD ** -0.5

        @block.sync
        def _(sp):
            sp.dma_start(const[:, :], a["consts"][:, :]).then_inc(setup_const.sem, 16)
            for i, (names, n) in enumerate(((ROWS1, NR1), (ROWS2, NR2))):
                at = 0
                for name, rows in names:
                    src = a[name]
                    if len(src.shape) == 3:
                        src = src.rearrange("l w c -> l (w c)")
                    sp.dma_start(par_rows[at:at + rows, 2 * i:2 * i + DEPTH, :],
                                 src.rearrange("l (r c) -> r l c", c=P)).then_inc(setup_dma.sem, 16)
                    at += rows
            sp.dma_start(xv, a["x"][0].rearrange("(t p) n -> p t n", p=P)).then_inc(setup_x.sem, 16)

            def load(L, piece):
                blk, l = L
                for name, row, tiles, col, n, to, width in dmas_of(blk, piece):
                    src = a[name]
                    if name == "w_branch":
                        src = src.rearrange("l b r c -> l (b r) c")
                    src = of_layer(src, l)[row:row + tiles * P, col:col + n].rearrange("(k p) c -> p k c", p=P)
                    sp.dma_start(weights(L, piece, tiles, width)[:, :, to:to + n], src)\
                      .then_inc(landed_[PLANS[blk].slot[piece]].sem, 16)

            def head(L, before):
                for n, piece in enumerate(PLANS[L[0]].pieces[:RING]):
                    if before is not None:
                        plan = PLANS[before[0]]
                        sp.wait_ge(*used(before, plan.last_in_slot[PLANS[L[0]].slot[piece]]))
                    load(L, piece)

            def tail(L):
                plan = PLANS[L[0]]
                for piece in plan.pieces[RING:]:
                    sp.wait_ge(*used(L, plan.before_in_slot[piece]))
                    load(L, piece)

            head((0, 0), None)
            for blk in range(2):
                with sp.Fori(0, DEPTH - 1) as l:
                    tail((blk, l))
                    head((blk, l + 1), (blk, l))
                last = (blk, DEPTH - 1)
                tail(last)
                if blk == 0:
                    head((1, 0), last)
                sp.wait_ge(*drained(last, ("br", 2, 3)))
                gain = a["final_norm_g"] if blk == 0 else a["final_norm_2"]
                sp.dma_start(final_gain, gain.partition_broadcast(P)).then_inc(end_gain.sem, 16)
            for t in range(TT):
                sp.wait_ge(end_out.sem, TT + t + 1)
                sp.dma_start(out[0, t * P:(t + 1) * P, :], xs[:, t, :]).then_inc(stored, 16)
            sp.wait_ge(stored, 16 * TT)

        @block.tensor
        def _(pe):
            seen = set()

            def claim(L, step, j=0):
                b, n = PLANS[L[0]].uses[step][j]
                if n:
                    pe.wait_ge(*drained_[b](L, n))
                return bank[b]

            def arrived(L, piece):
                if piece not in seen:
                    seen.add(piece)
                    m = PLANS[L[0]].n_split.get(piece)
                    pe.wait_ge(*(landed(L, piece) if m is None else w_low(L, m + 1)))

            def stand_alone():
                pe.sem_inc(waits_met, 1)

            def tmajor(acc, lhs, rhs, n_k):
                for k in range(n_k):
                    mm = pe.matmul(acc, lhs(k), rhs(k), start=(k == 0), stop=(k == n_k - 1))
                return mm

            def in_parts(acc, lhs, rhs, start=True, stop=True):
                pe.matmul(acc, lhs[0], rhs[0], start=start, stop=False)
                pe.matmul(acc, lhs[0], rhs[1], start=False, stop=False)
                return pe.matmul(acc, lhs[1], rhs[0], start=False, stop=stop)

            def dense_product(acc, lhs, rhs):
                for k in range(KD):
                    mm = in_parts(acc, lhs(k), rhs(k), start=(k == 0), stop=(k == KD - 1))
                return mm

            def both(pair, *where):
                return tuple(t_[(slice(None),) + where] for t_ in pair)

            h_parts = h_high, h_low
            hid_parts = hid_high, hid_low

            def turn(out_, in_):
                n = in_.shape[0]
                return pe.transpose(out_, in_, ident[0:n, 0:n])

            def norm(L, m, t, half_):
                acc = claim(L, ("norm", m, t, half_))
                if half_ == 0:
                    pe.wait_ge(*diag_done(L, 2 * m + t + 1))
                for i in range(4):
                    k = 4 * half_ + i
                    mm = pe.matmul(acc[:, i * P:(i + 1) * P], xv[:, t, k * P:(k + 1) * P], diag[:, t],
                                   start=True, stop=True)
                mm.then_inc(fills(L, ("norm", m, t, half_)), 1)

            def h_ready(L, m):
                pe.wait_ge(*x_low(L, 4 * m + 4))

            def tokens_out(o, blk):
                return o // 2 < 7 if blk == 0 else o // 2 in (0, 3, 7)

            def d(L, o):
                step = ("d", o)
                if o == 0:
                    h_ready(L, 0 if L[0] == 0 else 1)
                arrived(L, ("in", o))
                acc = claim(L, step)
                w = weights_split(L, ("in", o), KD, 256)
                for i in range(2):
                    part = slice(i * P, (i + 1) * P)
                    to = acc[:, i * 256:(i + 1) * 256]
                    if tokens_out(o, L[0]):
                        mm = dense_product(to, lambda k: both(h_parts, k, part), lambda k: both(w, k))
                    else:
                        mm = dense_product(to, lambda k: both(w, k, part), lambda k: both(h_parts, k))
                mm.then_inc(fills(L, step), 1)

            def branch(L, i, jp):
                step = ("br", i, jp)
                if L[0] == 0:
                    if i == 1:
                        src = cT
                        if jp == 0:
                            pe.wait_ge(*c_done(L, 2))
                    else:
                        src = aT if i == 0 else rT
                        if jp == 0:
                            pe.wait_ge(*drained(L, ("FT", "diff", TT - 1) if i == 0 else ("RFT", TT - 1)))
                else:
                    src = (fox_T, mla_T, dn_T)[i]
                    if jp == 0:
                        pe.wait_ge(*drained(L, (("FT", "fox", TT - 1), ("FT", "mla", TT - 1), ("DFT", TT - 1))[i]))
                piece = ("br", i, jp // 2)
                arrived(L, piece)
                acc = claim(L, step)
                w = weights(L, piece, 4, 512)
                for jj in range(2):
                    c = (2 * (jp % 2) + jj) * P
                    mm = tmajor(acc[:, jj * SEQ:(jj + 1) * SEQ], lambda k: w[:, k, c:c + P],
                                lambda k: src[:, k, :], 4)
                mm.then_inc(fills(L, step), 1)

            def wo(L, q):
                step = ("wo", q)
                arrived(L, ("wo", q))
                acc = claim(L, step)
                w = weights_split(L, ("wo", q), KD, 256)
                for t in range(TT):
                    for k in range(KD):
                        if q == t == 0 and k % 2 == 0:
                            pe.wait_ge(*m_low(L, k // 2 + 1))
                        mm = in_parts(acc[:, t * 256:(t + 1) * 256], both(h_parts, k, slice(t * P, (t + 1) * P)),
                                      both(w, k), start=(k == 0), stop=(k == KD - 1))
                mm.then_inc(fills(L, step), 1)

            def unit(kind, u):
                return u // 4, u % 4, u + 8 * (kind == "mla")

            def scores(L, kind, u):
                qb, pair, _ = unit(kind, u)
                n = (qb + 1) * P
                q_cols = slice(qb * P, (qb + 1) * P)
                if u % 4 == 0:
                    if kind == "diff":
                        for j in range(2):
                            pe.wait_ge(*drained(L, ("AT", qb), j))
                    elif kind == "fox" and u == 0:
                        for o in range(2, 6):
                            pe.wait_ge(*drained(L, ("d", o)))
                        pe.wait_ge(*drained(L, ("FC",)))
                    elif kind == "mla" and u == 0:
                        for h in range(2):
                            pe.wait_ge(*drained(L, ("MT", TT - 1, 1, h)))
                for c in range(2):
                    acc = claim(L, ("S", kind, u), c)
                    rows = slice(64 * c, 64 * c + 64)
                    if kind == "diff":
                        mm = pe.matmul(acc[:, 0:n], aqT[rows, pair, q_cols], akT[rows, pair, 0:n],
                                       start=True, stop=True)
                    elif kind == "fox":
                        pe.matmul(acc[:, 0:n], fqT[rows, pair, q_cols], fkT[rows, pair, 0:n],
                                  start=True, stop=False)
                        h = 2 * pair + c
                        mm = pe.matmul(acc[:, 0:n], ident[:, h:h + 1].to_broadcast([P, P]), neg_c[:, 0:n],
                                       start=False, stop=True)
                    else:
                        h = 2 * pair + c
                        mm = pe.matmul(acc[:, 0:n], mqkT[0:M_QK, 0, h, q_cols], mqkT[0:M_QK, 1, h, 0:n],
                                       start=True, stop=True)
                    mm.then_inc(fills(L, ("S", kind, u), c), 1)

            def probabilities_turned(L, kind, u):
                qb, pair, n_u = unit(kind, u)
                acc = claim(L, ("T", kind, u))
                nk = qb + 1
                if kind == "diff":
                    pe.wait_ge(*mix_done(L, n_u + 1))
                    for kb in range(nk):
                        mm = turn(acc[:, kb * P:(kb + 1) * P], at_w[:, u % 2, kb * P:(kb + 1) * P])
                else:
                    pe.wait_ge(*exp_done(L, 2 * n_u + 2))
                    for c in range(2):
                        for kb in range(nk):
                            to = (c * nk + kb) * P
                            mm = turn(acc[:, to:to + P], at_sc[:, u % 2, c, kb * P:(kb + 1) * P])
                mm.then_inc(fills(L, ("T", kind, u)), 1)

            def values(L, kind, u):
                qb, pair, _ = unit(kind, u)
                nk = qb + 1
                acc = claim(L, ("V", kind, u))
                pe.wait_ge(*drained(L, ("T", kind, u)))
                if u % 4 == 0:
                    if kind == "mla":
                        for i in (2, 3):
                            pe.wait_ge(*drained(L, ("u", qb, i)))
                    elif u == 0:
                        for o in (6, 7):
                            pe.wait_ge(*drained(L, ("d", o)))
                if kind == "diff":
                    mm = tmajor(acc[:, 0:P], lambda kb: at_wT[:, u % 2, kb * P:(kb + 1) * P],
                                lambda kb: av[:, kb, pair * P:(pair + 1) * P], nk)
                else:
                    vals = fv if kind == "fox" else mv
                    for c in range(2):
                        h = 2 * pair + c
                        mm = tmajor(acc[:, c * HD:(c + 1) * HD],
                                    lambda kb: at_wT[:, u % 2, (c * nk + kb) * P:(c * nk + kb + 1) * P],
                                    lambda kb: vals[:, kb, h * HD:(h + 1) * HD], nk)
                mm.then_inc(fills(L, ("V", kind, u)), 1)

            def four_turned(L, step, src):
                acc = claim(L, step)
                for i in range(4):
                    mm = turn(acc[:, i * P:(i + 1) * P], src[:, i * P:(i + 1) * P])
                mm.then_inc(fills(L, step), 1)

            def result_turned(L, kind, qb):
                pe.wait_ge(*o_done(L, {"diff": 0, "fox": 0, "mla": 2}[kind] + qb + 1))
                four_turned(L, ("FT", kind, qb), at_o[:, qb])

            def a_turned(L, t):
                pe.wait_ge(*roped(L, t + 1))
                for j in range(2):
                    acc = claim(L, ("AT", t), j)
                    for i in range(4):
                        mm = turn(acc[:, i * P:(i + 1) * P], aqk[:, t, (4 * j + i) * P:(4 * j + i + 1) * P])
                    mm.then_inc(fills(L, ("AT", t), j), 1)

            def r_turned(L, t):
                pe.wait_ge(*roped(L, t + 3))
                four_turned(L, ("RT", t), rqk[:, t])

            def r_inner(L, t):
                pe.wait_ge(*drained(L, ("RT", t)))
                for par_h in range(2):
                    acc = claim(L, ("RI", t), par_h)
                    rows = slice(64 * par_h, 64 * par_h + 64)
                    for hh in range(2):
                        mm = pe.matmul(acc[:, hh * P:(hh + 1) * P], rqkT[rows, 2 + hh, t * P:(t + 1) * P],
                                       rqkT[rows, hh, t * P:(t + 1) * P], start=True, stop=True)
                    mm.then_inc(fills(L, ("RI", t), par_h), 1)

            def r_state_(L):
                acc = claim(L, ("RK",))
                pe.wait_ge(*roped(L, 5))
                for o in (8, 9):
                    pe.wait_ge(*drained(L, ("d", o)))
                for h in range(R_HEADS):
                    rows = slice(64 * (h % 2), 64 * (h % 2) + 64)
                    mm = pe.matmul(acc[rows, (h // 2) * P:(h // 2 + 1) * P], kz[:, h * R_QK:(h + 1) * R_QK],
                                   rv[:, 0, h * P:(h + 1) * P], start=True, stop=True)
                mm.then_inc(fills(L, ("RK",)), 1)

            def r_values(L, t):
                acc = claim(L, ("RV", t))
                for o in (8, 9):
                    pe.wait_ge(*drained(L, ("d", o)))
                for j in range(2):
                    pe.wait_ge(*drained(L, ("RI", t), j))
                for h in range(R_HEADS):
                    at = (h % 2) * 256 + (h // 2) * P
                    mm = pe.matmul(acc[:, h * P:(h + 1) * P], inner[:, t, at:at + P],
                                   rv[:, t, h * P:(h + 1) * P], start=True, stop=True)
                mm.then_inc(fills(L, ("RV", t)), 1)

            def r_cross_(L):
                pe.wait_ge(*drained(L, ("RK",)))
                for par_h in range(2):
                    acc = claim(L, ("RC",), par_h)
                    rows = slice(64 * par_h, 64 * par_h + 64)
                    for hh in range(2):
                        mm = pe.matmul(acc[:, hh * P:(hh + 1) * P], rqkT[rows, hh, P:SEQ],
                                       r_state[rows, hh * P:(hh + 1) * P], start=True, stop=True)
                    mm.then_inc(fills(L, ("RC",), par_h), 1)

            def r_result_turned(L, t):
                pe.wait_ge(*o_done(L, 2 + t + 1))
                four_turned(L, ("RFT", t), r_o[:, t])

            def gate_up(L, f, j):
                if j == 0:
                    h_ready(L, 0 if f == 0 else 2)
                piece = ("gu", f, j)
                arrived(L, piece)
                acc = claim(L, ("gu", f, j))
                w = weights_split(L, piece, KD, 256)
                for s in range(2):
                    part = slice(s * P, (s + 1) * P)
                    mm = dense_product(acc[:, s * SEQ:(s + 1) * SEQ], lambda k: both(w, k, part),
                                       lambda k: both(h_parts, k))
                mm.then_inc(fills(L, ("gu", f, j)), 1)

            def down(L, f, dd):
                piece = ("down", f, dd)
                arrived(L, piece)
                first = ("dn", f, 0)
                if dd == 0:
                    for j in range(4):
                        claim(L, first, j)
                w = weights_split(L, piece, 2, DM)
                pe.wait_ge(*hid_lo_done(L, f * FT + 2 * dd + 2))
                for kk in range(2):
                    j = 2 * dd + kk
                    for t in range(TT):
                        for h in range(2):
                            mm = in_parts(bank[4 + 2 * t + h][:, :],
                                          both(hid_parts, j % HID, slice(t * P, (t + 1) * P)),
                                          both(w, kk, slice(h * 512, (h + 1) * 512)),
                                          start=(j == 0), stop=(j == FT - 1))
                            if j == FT - 1:
                                mm.then_inc(fills(L, first, 2 * t + h), 1)
                if dd < DOWNS - 1:
                    mm.then_inc(hid_used.sem, 1)

            def fox_decays(L):
                acc = claim(L, ("FC",))
                pe.wait_ge(*small_done(L, 1))
                tri, ones = cst("tri"), cst("ones")
                pe.matmul(acc[0:8, 0:P], log_f[:, 0], tri, start=True, stop=True)
                pe.matmul(acc[0:8, P:SEQ], log_f[:, 0], ones, start=True, stop=False)
                pe.matmul(acc[0:8, P:SEQ], log_f[:, 1], tri, start=False, stop=True)\
                  .then_inc(fills(L, ("FC",)), 1)

            def latents_turned(L, t):
                acc = claim(L, ("MC", t))
                pe.wait_ge(*m_norm_done(L, t + 1))
                for i in range(3):
                    mm = turn(acc[:, i * P:(i + 1) * P], mraw[:, t, 8 + i * P:8 + (i + 1) * P])
                mm.then_inc(fills(L, ("MC", t)), 1)

            def up(L, t, i):
                arrived(L, ("u", i // 2))
                if i == 0:
                    pe.wait_ge(*drained(L, ("MC", t)))
                acc = claim(L, ("u", t, i))
                tok = slice(t * P, (t + 1) * P)
                if i < 2:
                    wq = weights(L, ("u", 0), 2, 768)
                    n = 512 if i == 0 else 256
                    mm = tmajor(acc[:, 0:n], lambda k: cT3[:, k, tok], lambda k: wq[:, k, i * 512:i * 512 + n], 2)
                else:
                    wkv = weights(L, ("u", 1), 1, 1024)
                    mm = pe.matmul(acc[:, :], cT3[:, 2, tok], wkv[:, 0, (i - 2) * 512:(i - 1) * 512],
                                   start=True, stop=True)
                mm.then_inc(fills(L, ("u", t, i)), 1)

            def mla_turned(L, t, w, half_):
                step = ("MT", t, w, half_)
                acc = claim(L, step)
                pe.wait_ge(*m_roped(L, t + 1))
                for i in range(4):
                    c = (4 * half_ + i) * M_QK
                    mm = turn(acc[0:M_QK, i * P:(i + 1) * P], mqk[:, w, t, c:c + M_QK])
                mm.then_inc(fills(L, step), 1)

            def heads(g):
                return range(4 * g, 4 * g + 4)

            def grid(acc, g, h, n=P):
                return acc[:, (h - 4 * g) * n:(h - 4 * g + 1) * n]

            def d_tokens(L, t, s):
                step = ("DT", t, s)
                acc = claim(L, step)
                pe.wait_ge(*conv2_done(L, 2 * s + 2))
                for i in range(4):
                    mm = turn(acc[:, i * P:(i + 1) * P], conv_y[:, s, i, t * P:(t + 1) * P])
                mm.then_inc(fills(L, step), 1)

            def d_decays(L, t):
                acc = claim(L, ("DG", t))
                pe.wait_ge(*small_done(L, 1))
                g = dgate[:, t]
                same = cst("same_chunk")
                pe.matmul(acc[:, 0:8], cst("tri_chunk"), g, start=True, stop=True)
                pe.matmul(acc[:, 8:16], same, g, start=True, stop=True)
                for c in range(2):
                    pe.matmul(acc[0:64, 16 + 8 * c:24 + 8 * c], same[:, 64 * c:64 * c + 64], g,
                              start=True, stop=True)
                pe.matmul(acc[0:8, 32:32 + P], g, cst("tri_chunk"), start=True, stop=True)\
                  .then_inc(fills(L, ("DG", t)), 1)

            def d_rows(L, t, g):
                acc = claim(L, ("R1", t, g))
                pe.wait_ge(*drained(L, ("DG", t)))
                for h in heads(g):
                    mm = pe.matmul(grid(acc, g, h), ident[0:8, h:h + 1].to_broadcast([8, P]),
                                   gc_rows[0:8, :], start=True, stop=True)
                mm.then_inc(fills(L, ("R1", t, g)), 1)

            def d_turned(L, t, s, g):
                step = ("DX", t, s, g)
                acc = claim(L, step)
                pe.wait_ge(*kn_done(L, t + 1))
                src = (d_tok[:, 0], d_tok[:, 1], d_kb)[s]
                stand_alone()
                for h in heads(g):
                    mm = turn(grid(acc, g, h)[0:64], src[:, h * HD:(h + 1) * HD])
                mm.then_inc(fills(L, step), 1)

            def d_products(L, name, t, g):
                acc = claim(L, (name, t, g))
                s = 0 if name == "QK" else 2
                pe.wait_ge(*drained(L, ("DX", t, max(s, 1), g)))
                for h in heads(g):
                    mm = pe.matmul(grid(acc, g, h), d_T3[0:64, 1, h], d_T3[0:64, s, h], start=True, stop=True)
                mm.then_inc(fills(L, (name, t, g)), 1)

            def d_first(L, t, g):
                acc = claim(L, ("L1", t, g))
                pe.wait_ge(*inv2_done(L, 2 * t + g + 1))
                for h in heads(g):
                    mm = turn(grid(acc, g, h), d_invT[:, h])
                mm.then_inc(fills(L, ("L1", t, g)), 1)

            def d_y(L, t, b, g):
                acc = claim(L, ("Y", t, b, g))
                i = (2, 4, 8, 16, 32).index(b)
                pe.wait_ge(*level_done(L, 10 * t + 2 * i + g + 1))
                for h in heads(g):
                    mm = pe.matmul(grid(acc, g, h), d_C[:, h], d_inv[:, h], start=True, stop=True)
                mm.then_inc(fills(L, ("Y", t, b, g)), 1)

            def d_z(L, t, b, g):
                step = ("Z", t, b, g)
                acc = claim(L, step, 0)
                pe.wait_ge(*drained(L, ("Y", t, b, g)))
                for h in heads(g):
                    mm = pe.matmul(grid(acc, g, h), d_Y[:, h], d_invT[:, h], start=True, stop=True)
                mm.then_inc(fills(L, step, 0), 1)
                acc = claim(L, step, 1)
                for h in heads(g):
                    mm = pe.matmul(grid(acc, g, h), d_invT[:, h], d_Y[:, h], start=True, stop=True)
                mm.then_inc(fills(L, step, 1), 1)

            def d_zt(L, t, g):
                acc = claim(L, ("ZT", t, g))
                pe.wait_ge(*drained(L, ("Y", t, 32, g)))
                for h in heads(g):
                    mm = pe.matmul(grid(acc, g, h), d_Y[:, h], d_invT[:, h], start=True, stop=True)
                mm.then_inc(fills(L, ("ZT", t, g)), 1)

            def d_wt(L, t, g):
                acc = claim(L, ("W", t, g))
                pe.wait_ge(*drained(L, ("ZT", t, g)))
                pe.wait_ge(*kw_done(L, t + 1))
                for h in heads(g):
                    mm = pe.matmul(grid(acc, g, h)[0:64], d_w[:, h * HD:(h + 1) * HD], d_invT[:, h],
                                   start=True, stop=True)
                mm.then_inc(fills(L, ("W", t, g)), 1)

            def d_ut(L, t):
                acc = claim(L, ("U", t))
                for h in range(DN_H):
                    mm = pe.matmul(acc[:, h * HD:(h + 1) * HD], d_invT[:, h], d_vb[:, h * HD:(h + 1) * HD],
                                   start=True, stop=True)
                mm.then_inc(fills(L, ("U", t)), 1)

            def state_ready(L, t, c):
                if (t, c) == (0, 0):
                    pe.wait_ge(*state_zero(L, 1))
                else:
                    pe.wait_ge(*drained(L, ("X3", t, 0) if c else ("X3", t - 1, 1)))

            def d_x1(L, t, c):
                acc = claim(L, ("X1", t, c))
                if c == 0:
                    pe.wait_ge(*drained(L, ("W", t, 1)))
                state_ready(L, t, c)
                rows = slice(64 * c, 64 * c + 64)
                stand_alone()
                for h in range(DN_H):
                    mm = pe.matmul(acc[rows, h * HD:(h + 1) * HD], d_wT[0:64, h, rows],
                                   d_S[0:64, h * HD:(h + 1) * HD], start=True, stop=True)
                mm.then_inc(fills(L, ("X1", t, c)), 1)

            def d_x2(L, t, c):
                acc = claim(L, ("X2", t, c))
                rows = slice(64 * c, 64 * c + 64)
                stand_alone()
                for h in range(DN_H):
                    mm = pe.matmul(acc[rows, h * HD:(h + 1) * HD], d_T3[0:64, 0, h, rows],
                                   d_S[0:64, h * HD:(h + 1) * HD], start=True, stop=True)
                mm.then_inc(fills(L, ("X2", t, c)), 1)

            def d_x3(L, t, c):
                acc = claim(L, ("X3", t, c))
                pe.wait_ge(*drained(L, ("X1", t, c)))
                rows = slice(64 * c, 64 * c + 64)
                stand_alone()
                for h in range(DN_H):
                    mm = pe.matmul(acc[0:64, h * HD:(h + 1) * HD], d_kdec[rows, h * HD:(h + 1) * HD],
                                   d_vn[rows, h * HD:(h + 1) * HD], start=True, stop=True)
                mm.then_inc(fills(L, ("X3", t, c)), 1)

            def d_in(L, t):
                acc = claim(L, ("IN", t))
                pe.wait_ge(*drained(L, ("X1", t, 1)))
                pe.wait_ge(*drained(L, ("QK", t, 1)))
                for h in range(DN_H):
                    mm = pe.matmul(acc[:, h * HD:(h + 1) * HD], d_QK[:, h], d_vn[:, h * HD:(h + 1) * HD],
                                   start=True, stop=True)
                mm.then_inc(fills(L, ("IN", t)), 1)

            def d_result_turned(L, t):
                pe.wait_ge(*o_done(L, FOX_DONE + t + 1))
                four_turned(L, ("DFT", t), dz[:, t])

            parts = {
                "norm": norm, "d": d, "br": branch, "wo": wo, "S": scores, "T": probabilities_turned,
                "V": values, "FT": result_turned, "AT": a_turned, "RT": r_turned, "RI": r_inner,
                "RK": r_state_, "RV": r_values, "RC": r_cross_, "RFT": r_result_turned, "gu": gate_up,
                "dn": down, "FC": fox_decays, "MC": latents_turned, "u": up, "MT": mla_turned,
                "DT": d_tokens, "DG": d_decays, "R1": d_rows, "DX": d_turned,
                "QK": lambda L, t, g: d_products(L, "QK", t, g), "K1": lambda L, t, g: d_products(L, "K1", t, g),
                "L1": d_first, "Y": d_y, "Z": d_z, "ZT": d_zt, "W": d_wt, "U": d_ut, "X1": d_x1,
                "X2": d_x2, "X3": d_x3, "IN": d_in, "DFT": d_result_turned,
            }

            def layer(L):
                seen.clear()
                for step in PLANS[L[0]].steps:
                    if step[0] in parts:
                        parts[step[0]](L, *step[1:])

            for b in range(8):
                pe.sem_inc(filled_[b].sem, PLANS[0].per_layer[b])
            pe.wait_ge(setup_const.sem, 16)
            pe.wait_ge(setup_dma.sem, ROWS_LANDED)
            for i, n in enumerate((NR1, NR1, NR2, NR2)):
                mm = pe.transpose(bank[0][:, i * P:i * P + n], par_rows[0:n, i, :], ident[0:n, 0:n])
            mm.then_inc(setup_pe.sem, 1)
            layers(pe, 0, layer)
            layers(pe, 1, layer)

        @block.scalar
        def _(act):
            def copy(o, i):
                return act.activation(o, i, ACT.Copy)

            def norm_sums(L, m):
                act.wait_ge(*x_new(L, m))
                if L[0] == 1 and m == 0:
                    act.wait_ge(*par_done(L, 1))
                for t in range(TT):
                    act.activation(squares[:, t], xv[:, t], ACT.Square, scale=DM ** -0.5,
                                   accum_out=x_ss[:, t:t + 1])\
                       .then_inc(ss_done.sem, 1)

            def norm(L, m, t, h):
                if (t, h) == (0, 0):
                    norm_sums(L, m)
                act.wait_ge(*drained(L, ("norm", m, t, h)))
                part = 4 * h, 4 * h + 4, t * P, (t + 1) * P
                copy(quarter_of(h_high, *part), quarter_of(hT, *part)).then_inc(x_high.sem, 1)

            def split_weights(L, piece):
                plan = PLANS[L[0]]
                m = plan.n_split[piece]
                act.wait_ge(*landed(L, piece))
                if plan.before_in_high[piece] is not None:
                    act.wait_ge(*used(L, plan.before_in_high[piece]))
                elif m == 0:
                    act.wait_ge(*used((L[0], L[1] - 1), plan.last_in_high[plan.high[piece]]))
                at, to = plan.slot[piece] * SLOT, plan.high[piece] * SLOT
                copy(ring_high[:, to:to + SLOT], ring[:, at:at + SLOT]).then_inc(w_high.sem, 1)

            def split_hidden(L, f, j):
                act.wait_ge(*drained(L, ("gu", f, j)))
                copy(hid_high[:, j % HID], hid[:, j % HID]).then_inc(hid_hi_done.sem, 1)

            def split_merged(L, jp):
                act.wait_ge(*summed(L, jp + 1))
                copy(h_high[:, 2 * jp:2 * jp + 2, :], merged[:, 2 * jp:2 * jp + 2, :]).then_inc(m_high.sem, 1)

            def read(L, step, o, rows=slice(0, P), n=None, j=0):
                act.wait_ge(*filled(L, step, j))
                src = bank_of(L, step, j)[rows, 0:n if n else math.prod(o.shape[1:])]
                if len(o.shape) == 3:
                    src = v(src, a=o.shape[1], b=o.shape[2])
                copy(o, src).then_inc(drains(L, step, j), 1)

            def tanh_half(L, step, n_done, done, o):
                act.wait_ge(*filled(L, step))
                act.activation(o, bank_of(L, step)[:, :], ACT.Tanh, scale=0.5).then_inc(done.sem, 1)

            def pair(t_, j):
                return t_[:, 2 * j:2 * j + 2, :]

            def columns(t_, part):
                return t_[:, :, 256 * part:256 * part + 256]

            def d1(L, o):
                step, n, part = ("d", o), o // 2, o % 2
                if n < 2:
                    read(L, step, aqk[:, :, n * 512 + 256 * part:n * 512 + 256 * part + 256])
                elif n == 2:
                    read(L, step, columns(rqk, part))
                elif n == 3:
                    read(L, step, columns(av, part))
                elif n == 4:
                    read(L, step, columns(rv, part))
                elif n in (5, 6, 10):
                    i = {5: 0, 6: 2, 10: 4}[n] + part
                    if i >= 2:
                        before = {2: 10, 3: 11, 4: 12, 5: 13}[i]
                        act.wait_ge(*drained(L, ("d", before)))
                    tanh_half(L, step, i, tanh_done, th[:, i % 2])
                elif n == 7:
                    read(L, step, pair(cu, part))
                elif n >= 11:
                    i, j = (n - 11) // 2, ((n - 11) % 2) * 4 + 2 * part
                    act.wait_ge(*filled(L, step))
                    act.activation(gates[:, i, j:j + 2, :], v(bank_of(L, step)[:, :], a=2, b=SEQ), ACT.Tanh,
                                   scale=0.5).then_inc(drains(L, step), 1)

            def d2(L, o):
                step, n, part = ("d", o), o // 2, o % 2
                if n == 0:
                    act.wait_ge(*filled(L, step))
                    src = v(bank_of(L, step)[:, :], a=2, b=256)
                    copy(mraw[:, :, 256:440] if part else mraw[:, :, 0:256], src[:, :, 72 * part:256])\
                        .then_inc(drains(L, step), 1)
                elif n == 1:
                    read(L, step, pair(fqT, part))
                elif n == 2:
                    read(L, step, pair(fkT, part))
                elif n == 3:
                    read(L, step, columns(fv, part))
                elif n < 7:
                    i, s = o - 8, n - 4
                    act.wait_ge(*filled(L, step))
                    acc = bank_of(L, step)
                    if i >= 2:
                        act.wait_ge(*taps_done(L, i - 1))
                    copy(craw[:, i % 2], v(acc[:, :], a=2, b=SEQ)).then_inc(craw_done.sem, 1)
                    for jj in range(2):
                        col = 3 * 12 + 4 * s + 2 * part + jj
                        ins = act.activation(conv_y[:, s, 2 * part + jj], acc[:, jj * SEQ:(jj + 1) * SEQ],
                                             ACT.Copy, scale=par_("dn_conv_w_2", 48, PAR2)[:, col:col + 1])
                    ins.then_inc(drains(L, step), 1)
                    if i >= 1:
                        conv_tanh(L, i - 1)
                    if i == 5:
                        conv_tanh(L, 5)
                elif n == 7:
                    if part == 0:
                        act.wait_ge(*conv2_done(L, 6))
                    tanh_half(L, step, part, tanh_done, th[:, part])
                else:
                    i, j = (n - 8) // 2, ((n - 8) % 2) * 4 + 2 * part
                    act.wait_ge(*filled(L, step))
                    for jj in range(2):
                        col = 8 * i + j + jj
                        ins = act.activation(gates[:, i, j + jj, :], bank_of(L, step)[:, jj * SEQ:(jj + 1) * SEQ],
                                             ACT.Tanh, scale=0.5,
                                             bias=par_("b_gate_2", 24, PAR2)[:, col:col + 1])
                    ins.then_inc(drains(L, step), 1)

            def conv_tanh(L, i):
                act.wait_ge(*taps_done(L, i + 1))
                if i >= 2:
                    act.wait_ge(*conv2_done(L, i - 1))
                s, part = i // 2, i % 2
                act.activation(th[:, i % 2], conv_y[:, s, 2 * part:2 * part + 2].rearrange("p a b -> p (a b)"),
                               ACT.Tanh, scale=0.5).then_inc(ctanh_done.sem, 1)

            def scores(L, kind, u):
                qb, pair_, n_u = u // 4, u % 4, u + 8 * (kind == "mla")
                n = (qb + 1) * P
                scale = M_QK ** -0.5 if kind == "mla" else HD ** -0.5
                act.wait_ge(*bias_done(L, n_u + 1))
                for c in range(2):
                    act.activation(at_sc[:, u % 2, c, 0:n], at_sc[:, u % 2, c, 0:n], ACT.Exp,
                                   bias=at_bias[:, u % 2, c:c + 1], scale=scale,
                                   accum_out=at_sum[:, qb, 2 * pair_ + c:2 * pair_ + c + 1])\
                       .then_inc(exp_done.sem, 1)

            def turned(L, kind, u):
                n = (u // 4 + 1) * P * (1 if kind == "diff" else 2)
                if u >= 2:
                    act.wait_ge(*filled(L, ("V", kind, u - 2)))
                read(L, ("T", kind, u), at_wT[:, u % 2, 0:n])

            def values(L, kind, u):
                read(L, ("V", kind, u), at_o[:, u // 4, (u % 4) * P:(u % 4 + 1) * P])

            def result(L, kind, qb):
                dst = {"diff": aT, "fox": fox_T, "mla": mla_T}[kind]
                read(L, ("FT", kind, qb), dst[:, :, qb * P:(qb + 1) * P])

            def a_turned(L, t):
                read(L, ("AT", t), aqT[:, :, t * P:(t + 1) * P], j=0)
                read(L, ("AT", t), akT[:, :, t * P:(t + 1) * P], j=1)

            def gate_up(L, f, j):
                act.wait_ge(*filled(L, ("gu", f, j)))
                if j >= 4:
                    act.wait_ge(*drained(L, ("gu", f, j - 4)))
                act.activation(ffn_tanh[:, j % 4], bank_of(L, ("gu", f, j))[:, 0:SEQ], ACT.Tanh, scale=0.5)\
                   .then_inc(ffn_tanh_done.sem, 1)

            def small_values(L):
                act.wait_ge(*z_done(L, 1))
                act_chain.link(act.activation(z_log[:, :, :], z_abs[:, :, :], ACT.Exp, scale=-1.0))
                for t in range(TT):
                    ins = act.activation(beta_t[:, t], mraw[:, t, 424:432], ACT.Tanh, scale=0.5)
                act_chain.link(ins)
                act.activation(z_log[:, :, :], z_log[:, :, :], ACT.Ln, bias=cst("ones")[:, 0:1])\
                   .then_inc(zlog_done.sem, 1)
                for t in range(TT):
                    act.activation(m_junk[:, t, 0:M_QR], mraw[:, t, 8:8 + M_QR], ACT.Square, scale=M_QR ** -0.5,
                                   accum_out=m_ss[:, t, 0:1])
                    ins = act.activation(m_junk[:, t, M_QR:M_QR + M_KVR], mraw[:, t, 264:392], ACT.Square, scale=M_KVR ** -0.5,
                                         accum_out=m_ss[:, t, 1:2])
                ins.then_inc(m_ss_done.sem, 1)

            def up(L, t, i):
                step = ("u", t, i)
                if i < 2:
                    read(L, step, mqk[:, 0, t, i * 512:i * 512 + (512 if i == 0 else 256)])
                else:
                    act.wait_ge(*filled(L, step))
                    src = v(bank_of(L, step)[:, :], a=4, b=P)
                    hs = slice(4 * (i - 2), 4 * (i - 2) + 4)
                    copy(v(mqk[:, 1, t], h=8, n=M_QK)[:, hs, 0:HD], src[:, :, 0:HD])
                    copy(v(mv[:, t], h=8, n=HD)[:, hs, :], src[:, :, HD:P]).then_inc(drains(L, step), 1)

            def mla_turned(L, t, w, h_):
                step = ("MT", t, w, h_)
                act.wait_ge(*filled(L, step))
                if (t, w, h_) == (0, 0, 0):
                    act.wait_ge(*conv2_done(L, 6))
                copy(mqkT[0:M_QK, w, 4 * h_:4 * h_ + 4, t * P:(t + 1) * P],
                     v(bank_of(L, step)[0:M_QK, :], a=4, b=P)).then_inc(drains(L, step), 1)

            def d_decays(L, t):
                act.wait_ge(*dlt_done(L, t + 1))
                act.activation(eg[:, 0:16], gc[:, 0:16], ACT.Exp)
                act.activation(gl[0:64], gl_raw[0:64], ACT.Exp).then_inc(eg_done.sem, 1)

            def d_rows(L, t, g):
                act.wait_ge(*arg_done(L, 2 * t + g + 1))
                act.activation(d_decay[:, 4 * g:4 * g + 4], d_decay[:, 4 * g:4 * g + 4], ACT.Exp)\
                   .then_inc(decay_done.sem, 1)

            def quarter(t_, g):
                return t_[:, 4 * g:4 * g + 4, :]

            def small_rows(L, step, t_, g):
                act.wait_ge(*filled(L, step))
                copy(t_[0:64, 4 * g:4 * g + 4, :], v(bank_of(L, step)[0:64, :], a=4, b=P))\
                    .then_inc(drains(L, step), 1)

            splits = {"split": split_weights, "hs": split_hidden, "ms": split_merged}
            parts1 = splits | {
                "norm": norm, "d": d1, "S": scores, "T": turned, "V": values, "FT": result, "AT": a_turned,
                "RT": lambda L, t: read(L, ("RT", t), rqkT[:, :, t * P:(t + 1) * P]),
                "RK": lambda L: read(L, ("RK",), r_state[:, :]),
                "RFT": lambda L, t: read(L, ("RFT", t), rT[:, :, t * P:(t + 1) * P]),
            }
            parts2 = splits | {
                "norm": norm, "d": d2, "S": scores, "T": turned, "V": values, "FT": result, "gu": gate_up,
                "SM": small_values, "u": up, "MT": mla_turned,
                "DT": lambda L, t, s: read(L, ("DT", t, s), d_tok[:, s]),
                "DG": d_decays, "R1": d_rows,
                "DX": lambda L, t, s, g: small_rows(L, ("DX", t, s, g), d_T3[:, s], g),
                "L1": lambda L, t, g: read(L, ("L1", t, g), quarter(d_inv, g)),
                "Y": lambda L, t, b, g: read(L, ("Y", t, b, g), quarter(d_Y, g)),
                "W": lambda L, t, g: small_rows(L, ("W", t, g), d_wT, g),
                "U": lambda L, t: read(L, ("U", t), d_u),
                "DFT": lambda L, t: read(L, ("DFT", t), dn_T[:, :, t * P:(t + 1) * P]),
            }

            def layer(L):
                act_chain.layer(act, L)
                for step in PLANS[L[0]].steps:
                    part = (parts1, parts2)[L[0]].get(step[0])
                    if part:
                        part(L, *step[1:])
                act_chain.end()

            def last_norm(blk):
                act.wait_ge(*x_new((blk, DEPTH), 0))
                for t in range(TT):
                    act.activation(squares[:, t], xv[:, t], ACT.Square, scale=DM ** -0.5,
                                   accum_out=x_ss[:, t:t + 1])\
                       .then_inc(end_ss.sem, 1)

            for name, table, dst, n in (("attn_subln_g", par1, PAR1["subln"], A_V),
                                        ("fox_b_f_2", par2, PAR2["f_bias"], 8),
                                        ("dn_dt_bias_2", par2, PAR2["dt_bias"], 8),
                                        ("dn_a_log_2", par2, PAR2["neg_a"], 8),
                                        ("dn_o_norm_2", par2, PAR2["o_norm"], HD)):
                act.dma_start(table[:, :, dst:dst + n], a[name].partition_broadcast(P))\
                   .then_inc(setup_shared.sem, 16)
            act.dma_start(lam_rows, a["attn_lambda"].rearrange("l r d -> (l r d)").partition_broadcast(P))\
               .then_inc(setup_shared.sem, 16)
            act.dma_start(pos_i[:, :], a["positions_2"][0].rearrange("(t p) -> p t", p=P),
                          allow_slow_non_contiguous=True).then_inc(setup_shared.sem, 16)
            act.wait_ge(setup_shared.sem, SHARED_LANDED)
            act.activation(par2[:, :, PAR2["neg_a"]:PAR2["neg_a"] + 8], par2[:, :, PAR2["neg_a"]:PAR2["neg_a"] + 8],
                           ACT.Exp)
            act.wait_ge(setup_dve.sem, 1)
            act.activation(lam_e, lam_s, ACT.Exp).then_inc(setup_act.sem, 1)
            act.wait_ge(setup_dve.sem, 2)
            act.activation(trig[:, :, :, :], trig[:, :, :, :], ACT.Sin).then_inc(setup_act.sem, 1)
            layers(act, 0, layer)
            last_norm(0)
            act.wait_ge(*x_new((1, 0), 0))
            layers(act, 1, layer)
            last_norm(1)

        @block.vector
        def _(dve):
            link = dve_chain.link

            def tt(o, i0, i1, op):
                return dve.tensor_tensor(o, i0, i1, op)

            def stt(o, i0, s, i1, op0, op1):
                return dve.scalar_tensor_tensor(o, i0, s, i1, op0, op1)

            def over(t_, n):
                return t_.unsqueeze(2).to_broadcast([t_.shape[0], t_.shape[1], n])

            def again(t_, n):
                return t_.unsqueeze(1).to_broadcast([t_.shape[0], n, t_.shape[1]])

            def parameters(L):
                dve.wait_ge(*x_new(L, 0))
                n, table = (NP1, par1) if L[0] == 0 else (NP2, par2)
                src = table[:, bass.ds(L[1], 1), :].rearrange("p o n -> p (o n)")
                dve.tensor_copy(par[:, 0:n], src).then_inc(par_done.sem, 1)
                dve.wait_ge(*par_done(L, 1))

            def norm(L, m, t, h):
                step = ("norm", m, t, h)
                if (t, h) == (0, 0):
                    dve.wait_ge(*rstd_done(L, m + 1))
                    for tok in range(TT):
                        dve.tensor_scalar(diag[:, tok], ident, x_rstd[:, tok:tok + 1], None, ALU.mult)\
                           .then_inc(diag_done.sem, 1)
                name, table = (("norm_g", PAR1) if L[0] == 0 else
                               (("ffn1_norm_2", "mix_norm_2", "ffn2_norm_2")[m], PAR2))
                gain = par_(name, 8, table)[:, 4 * h:4 * h + 4]
                dve.wait_ge(*filled(L, step))
                tt(hT[:, 4 * h:4 * h + 4, t * P:(t + 1) * P], v(bank_of(L, step)[:, :], a=4, b=P),
                   over(gain, P), ALU.mult).then_inc(drains(L, step), 1)
                i = 2 * t + h
                if i:
                    split_x(L, m, i - 1)
                if i == 3:
                    split_x(L, m, 3)

            def less_high(low, value, high):
                return tt(low, value, high.bitcast(F32), ALU.subtract)

            def split_x(L, m, i):
                dve.wait_ge(*x_high(L, 4 * m + i + 1))
                part = 4 * (i % 2), 4 * (i % 2) + 4, i // 2 * P, (i // 2 + 1) * P
                less_high(quarter_of(h_low, *part), quarter_of(hT, *part), quarter_of(h_high, *part))\
                    .then_inc(x_low.sem, 1)

            def split_weights(L, piece):
                plan = PLANS[L[0]]
                m = plan.n_split[piece]
                at, to = plan.slot[piece] * SLOT, plan.high[piece] * SLOT
                dve.wait_ge(*w_high(L, m + 1))
                less_high(ring_low[:, at:at + SLOT], ring[:, at:at + SLOT], ring_high[:, to:to + SLOT])\
                    .then_inc(w_low.sem, 1)

            def split_hidden(L, f, j):
                dve.wait_ge(*hid_hi_done(L, f * FT + j + 1))
                less_high(hid_low[:, j % HID], hid[:, j % HID], hid_high[:, j % HID]).then_inc(hid_lo_done.sem, 1)

            def split_merged(L, jp):
                dve.wait_ge(*m_high(L, jp + 1))
                two = slice(2 * jp, 2 * jp + 2)
                less_high(h_low[:, two, :], merged[:, two, :], h_high[:, two, :]).then_inc(m_low.sem, 1)

            def columns(t_, part):
                return t_[:, :, 256 * part:256 * part + 256]

            def silu2(L, step, done, th_, o):
                dve.wait_ge(*done)
                y = bank_of(L, step)[:, :]
                if len(o.shape) == 3:
                    th_, y = v(th_, a=2, b=256), v(y, a=2, b=256)
                stt(o, th_, 1.0, y, ALU.add, ALU.mult).then_inc(drains(L, step), 1)
                dve.wait_ge(*drained(L, step))

            def d1(L, o):
                step, n, part = ("d", o), o // 2, o % 2
                if n == 5:
                    silu2(L, step, tanh_done(L, part + 1), th[:, part], columns(az, part))
                    for t in range(TT):
                        o_ = v(az[:, t, 256 * part:256 * part + 256], h=2, n=P)
                        ins = tt(o_, o_, again(par_("subln", A_V, PAR1), 2), ALU.mult)
                    link(ins)
                elif n == 6:
                    silu2(L, step, tanh_done(L, part + 3), th[:, part], columns(rz, part))
                elif n == 8:
                    dve.wait_ge(*filled(L, step))
                    dve.wait_ge(*drained(L, ("d", 14 + part)))
                    tt(cu[:, 2 * part:2 * part + 2, :], cu[:, 2 * part:2 * part + 2, :],
                       v(bank_of(L, step)[:, :], a=2, b=SEQ), ALU.mult).then_inc(drains(L, step), 1)
                    dve.wait_ge(*drained(L, step))
                    w = par_("conv_w", 12, PAR1)
                    tiles = (2 * part, 2 * part + 1)
                    for j in tiles:
                        ins = dve.tensor_scalar(cy[:, j], cu[:, j], w[:, 8 + j:9 + j], None, ALU.mult)
                    link(ins)
                    for back, tap in ((1, 1), (2, 0)):
                        for j in tiles:
                            ins = stt(cy[:, j, back:SEQ], cu[:, j, 0:SEQ - back], w[:, 4 * tap + j:4 * tap + j + 1],
                                      cy[:, j, back:SEQ], ALU.mult, ALU.add)
                        link(ins)
                elif n == 9:
                    dve.wait_ge(*filled(L, step))
                    tt(cy[:, 2 * part:2 * part + 2, :], cy[:, 2 * part:2 * part + 2, :],
                       v(bank_of(L, step)[:, :], a=2, b=SEQ), ALU.mult).then_inc(drains(L, step), 1)
                elif n == 10:
                    silu2(L, step, tanh_done(L, part + 5), th[:, part], th_c[:, part])
                    dve.wait_ge(*drained(L, ("d", 18 + part)))
                    tt(cT[:, 2 * part:2 * part + 2, :], cy[:, 2 * part:2 * part + 2, :],
                       v(th_c[:, part], a=2, b=SEQ), ALU.mult).then_inc(c_done.sem, 1)

            def branch(L, i, jp):
                step = ("br", i, jp)
                order = (1, 0, 2) if L[0] == 0 else (0, 1, 2)
                tmps = br_tmps[L[0]]
                n = order.index(i) * 4 + jp
                dve.wait_ge(*filled(L, step))
                gate = gates[:, i, 2 * jp:2 * jp + 2].rearrange("p a b -> p (a b)")
                if n < 4:
                    o = merged[:, 2 * jp:2 * jp + 2].rearrange("p a b -> p (a b)")
                else:
                    o = tmps[:, n % 2]
                    if n == 8:
                        dve.wait_ge(*added(L, 4))
                    elif n in (6, 7):
                        dve.wait_ge(*added(L, n - 5))
                    elif n > 9:
                        dve.wait_ge(*summed(L, n - 9))
                if jp == 0:
                    for p_ in range(4):
                        dve.wait_ge(*drained(L, ("d", (22 if L[0] == 0 else 16) + 4 * i + p_)))
                stt(o, gate, 1.0, bank_of(L, step)[:, :], ALU.add, ALU.mult).then_inc(drains(L, step), 1)
                if n >= 8:
                    dve.wait_ge(*drained(L, step))
                    total = merged[:, 2 * jp:2 * jp + 2].rearrange("p a b -> p (a b)")
                    tt(total, total, o, ALU.add).then_inc(summed.sem, 1)

            def wo(L, q):
                step = ("wo", q)
                dve.wait_ge(*filled(L, step))
                cols = xv[:, :, 256 * q:256 * q + 256]
                stt(cols, v(bank_of(L, step)[:, :], a=2, b=256), 0.25 if L[0] == 0 else 0.5, cols,
                    ALU.mult, ALU.add).then_inc(drains(L, step), 1)
                if q == 3:
                    for i in range(4):
                        dve.wait_ge(*drained(L, ("wo", i)))
                    dve.memset(stat_all[:, 32:33], 0.0).then_inc(x_new.sem, 1)

            def scores(L, kind, u):
                qb, pair, n_u = u // 4, u % 4, u + 8 * (kind == "mla")
                n = (qb + 1) * P
                scale = M_QK ** -0.5 if kind == "mla" else HD ** -0.5
                if u >= 2:
                    dve.wait_ge(*filled(L, ("T", kind, u - 2)))
                for c in range(2):
                    dve.wait_ge(*filled(L, ("S", kind, u), c))
                    tt(at_sc[:, u % 2, c, 0:n], bank_of(L, ("S", kind, u), c)[:, 0:n],
                       cst("causal")[:, SEQ - n:SEQ], ALU.add).then_inc(drains(L, ("S", kind, u), c), 1)
                for c in range(2):
                    dve.wait_ge(*drained(L, ("S", kind, u), c))
                link(dve.reduce_max(at_max[:, u % 2], at_sc[:, u % 2, :, 0:n], X))
                dve.tensor_scalar(at_bias[:, u % 2], at_max[:, u % 2], -scale, None, ALU.mult)\
                   .then_inc(bias_done.sem, 1)
                if kind == "diff":
                    s2 = at_rcp[:, qb, 2 * pair:2 * pair + 2]
                    dve.wait_ge(*exp_done(L, 2 * n_u + 2))
                    link(dve.reciprocal(s2, at_sum[:, qb, 2 * pair:2 * pair + 2]))
                    link(tt(s2[:, 1:2], s2[:, 1:2], par_("neg_lam", 1, PAR1), ALU.mult))
                    link(dve.tensor_scalar(at_w[:, u % 2, 0:n], at_sc[:, u % 2, 0, 0:n], s2[:, 0:1], None, ALU.mult))
                    stt(at_w[:, u % 2, 0:n], at_sc[:, u % 2, 1, 0:n], s2[:, 1:2], at_w[:, u % 2, 0:n],
                        ALU.mult, ALU.add).then_inc(mix_done.sem, 1)

            def variance(src, sq, ss, groups, n, inv_n, eps, done):
                link(tt(sq, src, src, ALU.mult))
                link(dve.reduce_sum(ss, v(sq, a=groups, b=n), X))
                dve.tensor_scalar(ss, ss, inv_n, eps, ALU.mult, ALU.add).then_inc(done.sem, 1)

            def normed(src, rstd, groups, n, factor, done):
                link(tt(v(src, a=groups, b=n), v(src, a=groups, b=n), over(rstd, n), ALU.mult))
                tt(factor[0], src, factor[1], ALU.mult).then_inc(done.sem, 1)

            def finish(L, kind, qb):
                dve.wait_ge(*drained(L, ("V", kind, 4 * qb + 3)))
                if kind == "diff":
                    variance(at_o[:, qb], at_sq, a_ss[:, 4 * qb:4 * qb + 4], A_HEADS, A_V, 1.0 / A_V, EPS, o_var)
                else:
                    dve.wait_ge(*exp_done(L, 2 * (4 * qb + 4) + 16 * (kind == "mla")))
                    link(dve.reciprocal(at_rcp[:, qb], at_sum[:, qb]))
                    tt(v(at_o[:, qb], h=8, n=HD), v(at_o[:, qb], h=8, n=HD), over(at_rcp[:, qb], HD),
                       ALU.mult).then_inc(o_done.sem, 1)

            def finish2(L, kind, qb):
                if kind == "diff":
                    dve.wait_ge(*o_rstd(L, qb + 1))
                    normed(at_o[:, qb], a_rs[:, 4 * qb:4 * qb + 4], A_HEADS, A_V, (at_o[:, qb], az[:, qb]), o_done)

            def r_inner(L, t):
                decay = v(cst("ret_decay"), hh=2, par=2, n=P)
                for p_ in range(2):
                    dve.wait_ge(*filled(L, ("RI", t), p_))
                    tt(v(inner[:, t, p_ * 256:(p_ + 1) * 256], a=2, b=P),
                       v(bank_of(L, ("RI", t), p_)[:, 0:256], a=2, b=P), decay[:, :, p_, :],
                       ALU.mult).then_inc(drains(L, ("RI", t), p_), 1)

            def r_cross_(L):
                xi = v(cst("xi"), hh=2, par=2)
                for p_ in range(2):
                    dve.wait_ge(*filled(L, ("RC",), p_))
                    tt(v(r_cross, hh=2, par=2, n=P)[:, :, p_, :], v(bank_of(L, ("RC",), p_)[:, 0:256], a=2, b=P),
                       over(xi[:, :, p_], P), ALU.mult).then_inc(drains(L, ("RC",), p_), 1)

            def r_values(L, t):
                dve.wait_ge(*filled(L, ("RV", t)))
                acc = bank_of(L, ("RV", t))[:, :]
                if t == 0:
                    dve.tensor_copy(r_o[:, 0], acc).then_inc(drains(L, ("RV", t)), 1)
                else:
                    for p_ in range(2):
                        dve.wait_ge(*drained(L, ("RC",), p_))
                    tt(r_o[:, 1], r_cross, acc, ALU.add).then_inc(drains(L, ("RV", t)), 1)

            def r_finish(L, t):
                dve.wait_ge(*drained(L, ("RV", t)))
                variance(r_o[:, t], r_sq, r_ss2[:, 4 * t:4 * t + 4], R_HEADS, R_V, 1.0 / R_V, EPS, o_var)

            def r_finish2(L, t):
                dve.wait_ge(*o_rstd(L, 2 + t + 1))
                normed(r_o[:, t], r_rs2[:, 4 * t:4 * t + 4], R_HEADS, R_V, (r_o[:, t], rz[:, t]), o_done)

            def gate_up(L, f, j):
                step = ("gu", f, j)
                acc = bank_of(L, step)
                dve.wait_ge(*ffn_tanh_done(L, f * FT + j + 1))
                link(stt(ffn_gate[:, j % 4], ffn_tanh[:, j % 4], 1.0, acc[:, 0:SEQ], ALU.add, ALU.mult))
                if j >= HID:
                    dve.wait_ge(*hid_used(L, f * (DOWNS - 1) + (j - HID) // 2 + 1))
                tt(hid[:, j % HID], ffn_gate[:, j % 4], acc[:, SEQ:2 * SEQ], ALU.mult).then_inc(drains(L, step), 1)

            def down(L, f, dd):
                if dd < DOWNS - 1:
                    return
                first = ("dn", f, 0)
                for t in range(TT):
                    for h in range(2):
                        dve.wait_ge(*filled(L, first, 2 * t + h))
                        cols = xv[:, t, h * 512:(h + 1) * 512]
                        stt(cols, bank_of(L, first, 2 * t + h)[:, :], 0.25, cols, ALU.mult, ALU.add)\
                            .then_inc(drains(L, first, 2 * t + h), 1)
                for j in range(4):
                    dve.wait_ge(*drained(L, first, j))
                dve.memset(stat_all[:, 32:33], 0.0).then_inc(x_new.sem, 1)

            def small_values(L):
                for o in range(2):
                    dve.wait_ge(*drained(L, ("d", o)))
                for t in range(TT):
                    tt(z[:, t, 0:8], mraw[:, t, 0:8], par_("f_bias", 8, PAR2), ALU.add)
                    ins = tt(z[:, t, 8:16], mraw[:, t, 432:440], par_("dt_bias", 8, PAR2), ALU.add)
                link(ins)
                stt(z_abs[:, :, :], z[:, :, :], -1.0, z[:, :, :], ALU.mult, ALU.max).then_inc(z_done.sem, 1)
                dve.wait_ge(*zlog_done(L, 1))
                stt(log_f[:, :, :], z[:, :, 0:8], 0.0, z_log[:, :, 0:8], ALU.min, ALU.subtract)
                link(stt(dgate[:, :, :], z[:, :, 8:16], 0.0, z_log[:, :, 8:16], ALU.max, ALU.add))
                tt(dgate[:, :, :], dgate[:, :, :], again(par_("neg_a", 8, PAR2), TT), ALU.mult)
                dve.tensor_scalar(beta[:, :, :], beta_t[:, :, :], 0.5, 0.5, ALU.mult, ALU.add)
                dve.tensor_scalar(half_beta[:, :, :], beta_t[:, :, :], 0.25, 0.25, ALU.mult, ALU.add)\
                   .then_inc(small_done.sem, 1)

            def fox_decays(L):
                dve.wait_ge(*filled(L, ("FC",)))
                link(dve.memset(neg_c, 0.0))
                dve.tensor_scalar(neg_c[0:8], bank_of(L, ("FC",))[0:8, 0:SEQ], -1.0 / FOX_SCALE, None, ALU.mult)\
                   .then_inc(drains(L, ("FC",)), 1)

            def latents(L, t):
                step = ("MC", t)
                dve.wait_ge(*filled(L, step))
                gain = par[:, PAR2["mla_q_norm_2"]:PAR2["mla_q_norm_2"] + 3]
                tt(cT3[:, :, t * P:(t + 1) * P], v(bank_of(L, step)[:, 0:384], a=3, b=P), over(gain, P),
                   ALU.mult).then_inc(drains(L, step), 1)

            def taps(L, i):
                s, part = i // 2, i % 2
                w = par_("dn_conv_w_2", 48, PAR2)
                tiles = (2 * part, 2 * part + 1)
                dve.wait_ge(*craw_done(L, i + 1))
                dve.wait_ge(*drained(L, ("d", 8 + i)))
                for back in (1, 2, 3):
                    for jj, j in enumerate(tiles):
                        col = (3 - back) * 12 + 4 * s + j
                        ins = stt(conv_y[:, s, j, back:SEQ], craw[:, i % 2, jj, 0:SEQ - back], w[:, col:col + 1],
                                  conv_y[:, s, j, back:SEQ], ALU.mult, ALU.add)
                    if back < 3:
                        link(ins)
                ins.then_inc(taps_done.sem, 1)
                dve.wait_ge(*taps_done(L, i + 1))

            def conv_silu2(L, i):
                s, part = i // 2, i % 2
                dve.wait_ge(*ctanh_done(L, i + 1))
                y = conv_y[:, s, 2 * part:2 * part + 2].rearrange("p a b -> p (a b)")
                stt(y, th[:, i % 2], 1.0, y, ALU.add, ALU.mult).then_inc(conv2_done.sem, 1)

            def d2(L, o):
                n, part = o // 2, o % 2
                if 4 <= n < 7:
                    taps(L, o - 8)
                    if o > 8:
                        conv_silu2(L, o - 9)
                    if o == 13:
                        conv_silu2(L, 5)
                elif n == 7:
                    silu2(L, ("d", o), tanh_done(L, part + 1), th[:, part], columns(dz, part))
                    for t in range(TT):
                        o_ = v(dz[:, t, 256 * part:256 * part + 256], h=4, n=HD)
                        ins = tt(o_, o_, again(par_("o_norm", HD, PAR2), 4), ALU.mult)
                    link(ins)

            def quarter(t_, g):
                return t_[:, 4 * g:4 * g + 4, :]

            def grid(acc):
                return v(acc[:, :], a=4, b=P)

            def d_stats(L, t):
                for s in range(2):
                    dve.wait_ge(*drained(L, ("DT", t, s)))
                    link(tt(d_sq, d_tok[:, s], d_tok[:, s], ALU.mult))
                    link(dve.reduce_sum(d_ss[:, 8 * s:8 * s + 8], v(d_sq, a=8, b=HD), X))
                dve.tensor_scalar(d_ss, d_ss, 4 * EPS, None, ALU.add).then_inc(l2_var.sem, 1)

            def d_decays(L, t):
                step = ("DG", t)
                dve.wait_ge(*filled(L, step))
                acc = bank_of(L, step)
                dve.tensor_copy(gl_raw[0:64], v(acc[0:64, 16:32], a=2, b=8))
                dve.tensor_copy(gc[:, 16:24], acc[:, 8:16])
                link(dve.tensor_copy(gc[:, 0:8], acc[:, 0:8]))
                dve.tensor_copy(gc_rows[0:8], acc[0:8, 32:32 + P]).then_inc(drains(L, step), 1)
                tt(gc[:, 8:16], gc[:, 16:24], gc[:, 0:8], ALU.subtract).then_inc(dlt_done.sem, 1)

            def d_rows(L, t, g):
                step = ("R1", t, g)
                dve.wait_ge(*filled(L, step))
                o = quarter(d_decay, g)
                tt(o, grid(bank_of(L, step)), over(gc[:, 4 * g:4 * g + 4], P), ALU.subtract)\
                    .then_inc(drains(L, step), 1)
                dve.wait_ge(*drained(L, step))
                tt(o, o, again(cst("decay_mask"), 4), ALU.add).then_inc(arg_done.sem, 1)

            def d_scaled(L, t):
                dve.wait_ge(*l2_rstd(L, t + 1))
                q_, k_ = v(d_tok[:, 0], a=8, b=HD), v(d_tok[:, 1], a=8, b=HD)
                link(tt(k_, k_, over(d_rs[:, 8:16], HD), ALU.mult))
                stt(q_, q_, HD ** -0.5, over(d_rs[:, 0:8], HD), ALU.mult, ALU.mult)
                tt(v(d_kb, a=8, b=HD), k_, over(beta[:, t], HD), ALU.mult).then_inc(kn_done.sem, 1)

            def d_products(L, name, t, g):
                step = (name, t, g)
                dve.wait_ge(*filled(L, step))
                dve.wait_ge(*decay_done(L, 2 * t + g + 1))
                tt(quarter(d_QK if name == "QK" else d_M, g), grid(bank_of(L, step)), quarter(d_decay, g),
                   ALU.mult).then_inc(drains(L, step), 1)

            def d_first(L, t, g):
                dve.wait_ge(*drained(L, ("K1", t, g)))
                o = quarter(d_invT, g)
                link(tt(o, quarter(d_M, g), again(cst("below1"), 4), ALU.mult))
                tt(o, o, again(ident, 4), ALU.add).then_inc(inv2_done.sem, 1)

            def d_z(L, t, b, g):
                step = ("Z", t, b, g)
                dve.wait_ge(*filled(L, step, 1))
                o = quarter(d_invT, g)
                tt(o, o, grid(bank_of(L, step, 0)), ALU.add).then_inc(drains(L, step, 0), 1)
                o = quarter(d_inv, g)
                tt(o, o, grid(bank_of(L, step, 1)), ALU.add).then_inc(drains(L, step, 1), 1)

            def d_zt(L, t, g):
                dve.wait_ge(*filled(L, ("ZT", t, g)))
                o = quarter(d_invT, g)
                tt(o, o, grid(bank_of(L, ("ZT", t, g))), ALU.add).then_inc(drains(L, ("ZT", t, g)), 1)

            def d_x1(L, t, c):
                if (t, c) == (0, 0):
                    dve.memset(d_S[0:64], 0.0).then_inc(state_zero.sem, 1)
                    dve.wait_ge(*state_zero(L, 1))
                rows = slice(64 * c, 64 * c + 64)
                dve.wait_ge(*filled(L, ("X1", t, c)))
                dve.wait_ge(*drained(L, ("U", t)))
                tt(d_vn[rows], d_u[rows], bank_of(L, ("X1", t, c))[rows, :], ALU.subtract)\
                    .then_inc(drains(L, ("X1", t, c)), 1)

            def d_x2(L, t, c):
                rows = slice(64 * c, 64 * c + 64)
                if (t, c) == (1, 0):
                    dve.wait_ge(*o_done(L, FOX_DONE + t))
                dve.wait_ge(*filled(L, ("X2", t, c)))
                tt(v(d_cross[rows], a=8, b=HD), v(bank_of(L, ("X2", t, c))[rows, :], a=8, b=HD),
                   over(eg[rows, 0:8], HD), ALU.mult).then_inc(drains(L, ("X2", t, c)), 1)

            def d_x3(L, t, c):
                if (t, c) != (0, 0):
                    dve.wait_ge(*drained(L, ("X3", t, 0) if c else ("X3", t - 1, 1)))
                link(tt(v(d_S1[0:64], a=8, b=HD), v(d_S[0:64], a=8, b=HD), over(gl[0:64, c], HD), ALU.mult))
                dve.wait_ge(*filled(L, ("X3", t, c)))
                tt(d_S[0:64], d_S1[0:64], bank_of(L, ("X3", t, c))[0:64, :], ALU.add)\
                    .then_inc(drains(L, ("X3", t, c)), 1)

            def d_in(L, t):
                dve.wait_ge(*filled(L, ("IN", t)))
                dve.wait_ge(*drained(L, ("X2", t, 1)))
                tt(d_o, d_cross, bank_of(L, ("IN", t))[:, :], ALU.add).then_inc(drains(L, ("IN", t)), 1)

            def d_finish(L, t):
                dve.wait_ge(*drained(L, ("IN", t)))
                variance(d_o, d_sq, d_ss2[:, 8 * t:8 * t + 8], DN_H, HD, 1.0 / HD, EPS, dn_var)

            def d_finish2(L, t):
                dve.wait_ge(*dn_rstd(L, t + 1))
                normed(d_o, d_rs2[:, 8 * t:8 * t + 8], DN_H, HD, (dz[:, t], dz[:, t]), o_done)

            splits = {"split": split_weights, "hs": split_hidden, "ms": split_merged}
            parts1 = splits | {"norm": norm, "d": d1, "br": branch, "wo": wo, "S": scores, "F": finish, "F2": finish2,
                      "RI": r_inner, "RC": r_cross_, "RV": r_values, "RF": r_finish, "RF2": r_finish2}
            parts2 = splits | {"norm": norm, "d": d2, "br": branch, "wo": wo, "S": scores, "F": finish, "gu": gate_up,
                      "dn": down, "SM": small_values, "FC": fox_decays, "MC": latents, "DP": d_stats,
                      "DG": d_decays, "R1": d_rows, "DP2": d_scaled,
                      "QK": lambda L, t, g: d_products(L, "QK", t, g),
                      "K1": lambda L, t, g: d_products(L, "K1", t, g), "L1": d_first, "Z": d_z, "ZT": d_zt,
                      "X1": d_x1, "X2": d_x2, "X3": d_x3, "IN": d_in, "DF": d_finish, "DF2": d_finish2}

            def layer(L):
                dve_chain.layer(dve, L)
                parameters(L)
                for step in PLANS[L[0]].steps:
                    part = (parts1, parts2)[L[0]].get(step[0])
                    if part:
                        part(L, *step[1:])
                dve_chain.end()

            def last_norm(blk):
                dve.wait_ge(end_rstd.sem, blk + 1)
                dve.wait_ge(end_gain.sem, 16 * (blk + 1))
                for t in range(TT):
                    stt(xs[:, t] if blk else xv[:, t], xv[:, t], x_rstd[:, t:t + 1], final_gain, ALU.mult, ALU.mult)\
                        .then_inc(end_out.sem, 1)
                if blk == 0:
                    dve.wait_ge(end_out.sem, TT)
                    dve.memset(stat_all[:, 32:33], 0.0).then_inc(x_new.sem, 1)

            n_link = [0]

            def setup_link(ins):
                n_link[0] += 1
                ins.then_inc(setup_chain, 1)
                dve.wait_ge(setup_chain, n_link[0])

            dve.wait_ge(setup_shared.sem, SHARED_LANDED)
            lr = v(lam_rows, l=DEPTH, r=4, d=A_QK)
            setup_link(tt(lam_p[:, :, :, :], lr[:, :, 0:4:2, :], lr[:, :, 1:4:2, :], ALU.mult))
            dve.reduce_sum(lam_s, lam_p[:, :, :, :], X).then_inc(setup_dve.sem, 1)
            setup_link(dve.tensor_copy(pos_f[:, :], pos_i[:, :]))
            dve.wait_ge(setup_const.sem, 16)
            n_f = M_ROPE // 2
            setup_link(tt(ang[:, :, :], over(pos_f[:, :], n_f), again(cst("inv_freq"), TT), ALU.mult))
            two_pi = 2.0 * math.pi
            c1 = float(np.float32(6.28125))
            c2 = float(np.float32(np.floor((two_pi - c1) * 2 ** 21) / 2 ** 21))
            c3 = float(np.float32(two_pi - c1 - c2))
            magic = 12582912.0
            for i, turn_ in enumerate((0.25, 0.0)):
                k_ = turns[:, i]
                setup_link(dve.tensor_scalar(k_, ang[:, :, :], 1.0 / two_pi, turn_, ALU.mult, ALU.add))
                setup_link(dve.tensor_scalar(k_, k_, magic, None, ALU.add))
                setup_link(dve.tensor_scalar(k_, k_, -magic, None, ALU.add))
                t_ = trig[:, i]
                setup_link(stt(t_, k_, -c1, ang[:, :, :], ALU.mult, ALU.add))
                setup_link(stt(t_, k_, -c2, t_, ALU.mult, ALU.add))
                setup_link(stt(t_, k_, -c3, t_, ALU.mult, ALU.add))
                setup_link(dve.tensor_scalar(t_, t_, math.pi / 2 if i == 0 else 0.0, None, ALU.add))
                ins = dve.tensor_scalar(t_, t_, 3.1415925, -3.1415925, ALU.min, ALU.max)
                setup_link(ins)
            setup_link(dve.memset(stat_all[:, 33:34], 0.0))
            dve.memset(stat_all[:, 33:34], 0.0).then_inc(setup_dve.sem, 1)
            dve.wait_ge(setup_act.sem, 1)
            le = lam_e
            for l in range(DEPTH):
                dst = par1[:, l, PAR1["neg_lam"]:PAR1["neg_lam"] + 1]
                setup_link(tt(dst, le[:, l, 1:2], le[:, l, 0:1], ALU.subtract))
                setup_link(dve.tensor_scalar(dst, dst, -LAMBDA_INIT[l], None, ALU.add))
                g_ = par1[:, l, PAR1["subln"]:PAR1["subln"] + A_V]
                dve.tensor_scalar(g_, g_, 1.0 - LAMBDA_INIT[l], None, ALU.mult)
                g_ = par2[:, l, PAR2["neg_a"]:PAR2["neg_a"] + 8]
                dve.tensor_scalar(g_, g_, -1.0, None, ALU.mult)
                g_ = par2[:, l, PAR2["o_norm"]:PAR2["o_norm"] + HD]
                dve.tensor_scalar(g_, g_, 0.5, None, ALU.mult)
            dve.wait_ge(setup_act.sem, 2)
            for half_ in range(2):
                dve.tensor_copy(pcos[:, :, n_f * half_:n_f * (half_ + 1)], trig[:, 0])
            dve.tensor_copy(psin[:, :, :], trig[:, 1])
            dve.tensor_scalar(pnsin[:, :, :], trig[:, 1], -1.0, None, ALU.mult)
            dve.wait_ge(setup_pe.sem, 1)
            for i, n in enumerate((NR1, NR1, NR2, NR2)):
                dst = (par1 if i < 2 else par2)[:, i % 2, 0:n]
                setup_link(dve.tensor_copy(dst, bank[0][:, i * P:i * P + n]))
            g_ = par2[:, :, PAR2["b_gate_2"]:PAR2["b_gate_2"] + 24]
            setup_link(dve.tensor_scalar(g_, g_, 0.5, None, ALU.mult))
            dve.wait_ge(setup_x.sem, 16)
            dve.memset(stat_all[:, 32:33], 0.0).then_inc(x_new.sem, 1)
            layers(dve, 0, layer)
            last_norm(0)
            layers(dve, 1, layer)
            last_norm(1)

        @block.gpsimd
        def _(pool):
            link = pool_chain.link

            def tt(o, i0, i1, op):
                return pool.tensor_tensor(o, i0, i1, op)

            def root(var, o, n, done):
                return tt(o, var, neg_half[:, 0:n], ALU.pow).then_inc(done.sem, 1)

            def norm(L, m, t, h):
                if (t, h) != (0, 0):
                    return
                pool.wait_ge(*ss_done(L, 2 * m + 2))
                link(tt(x_var, x_ss, cst("eps")[:, 0:TT], ALU.add))
                root(x_var, x_rstd, TT, rstd_done)

            def rotate(src, lo, hi, cos, nsin, sin, ta, tb, done):
                tt(ta, src, cos, ALU.mult)
                tt(tb[0], hi, nsin, ALU.mult)
                link(tt(tb[1], lo, sin, ALU.mult))
                return tt(src, ta, tb[2], ALU.add)

            def rope_attention(L, t):
                n = A_ROT // 2
                src = v(aqk[:, t], g=16, d=A_QK)
                ta, tb = v(rope_a[:, 0:256], g=16, d=A_ROT), v(rope_b[:, 0:256], g=16, d=A_ROT)

                def table(name, w):
                    return v(cst(name), t=TT, n=w)[:, t].unsqueeze(1).to_broadcast([P, 16, w])

                rotate(src[:, :, 0:A_ROT], src[:, :, 0:n], src[:, :, n:A_ROT], table("rope_cos", A_ROT),
                       table("rope_nsin", n), table("rope_sin", n), ta,
                       (tb[:, :, 0:n], tb[:, :, n:A_ROT], tb), None).then_inc(roped.sem, 1)
                pool.wait_ge(*roped(L, t + 1))

            def rope_retention(L, t):
                n = R_QK // 2
                src = v(rqk[:, t], w=2, h=4, d=R_QK)
                ta, tb = v(rope_a, w=2, h=4, d=R_QK), v(rope_b, w=2, h=4, d=R_QK)

                def table(name, w_):
                    t_ = v(cst(name), t=TT, w=2, n=w_)[:, t]
                    return t_.unsqueeze(2).to_broadcast([P, 2, 4, w_])

                cos, nsin, sin = table("ret_cos", R_QK), table("ret_nsin", n), table("ret_sin", n)
                for w in range(2):
                    rotate(src[:, w], src[:, w, :, 0:n], src[:, w, :, n:R_QK], cos[:, w], nsin[:, w], sin[:, w],
                           ta[:, w], (tb[:, w, :, 0:n], tb[:, w, :, n:R_QK], tb[:, w]), None)\
                        .then_inc(*((roped.sem, 1) if w else (pool_half, 1)))
                pool.wait_ge(*roped(L, t + 3))

            def d1(L, o):
                if o == 3:
                    for i in range(4):
                        pool.wait_ge(*drained(L, ("d", i)))
                    for t in range(TT):
                        rope_attention(L, t)
                elif o == 5:
                    for i in (4, 5):
                        pool.wait_ge(*drained(L, ("d", i)))
                    for t in range(TT):
                        rope_retention(L, t)
                    tt(v(kz, h=4, d=R_QK), v(rqk[:, 0], w=2, h=4, d=R_QK)[:, 1],
                       cst("zeta").unsqueeze(2).to_broadcast([P, 4, R_QK]), ALU.mult).then_inc(roped.sem, 1)

            def branch(L, i, jp):
                order = (1, 0, 2) if L[0] == 0 else (0, 1, 2)
                n = order.index(i) * 4 + jp
                if n < 4:
                    return
                pool.wait_ge(*drained(L, ("br", i, jp)))
                if n >= 8:
                    return
                o = merged[:, 2 * jp:2 * jp + 2].rearrange("p a b -> p (a b)")
                tt(o, o, br_tmps[L[0]][:, n % 2], ALU.add).then_inc(added.sem, 1)

            def finish(L, kind, qb):
                if kind == "diff":
                    pool.wait_ge(*o_var(L, qb + 1))
                    root(a_ss[:, 4 * qb:4 * qb + 4], a_rs[:, 4 * qb:4 * qb + 4], 4, o_rstd)

            def r_finish(L, t):
                pool.wait_ge(*o_var(L, 2 + t + 1))
                root(r_ss2[:, 4 * t:4 * t + 4], r_rs2[:, 4 * t:4 * t + 4], 4, o_rstd)

            def small_values(L):
                pool.wait_ge(*m_ss_done(L, 1))
                ss_, rs_ = (t_[:, :, :].rearrange("p a b -> p (a b)") for t_ in (m_ss, m_rstd))
                link(tt(ss_, ss_, cst("eps")[:, 0:4], ALU.add))
                link(tt(rs_, ss_, neg_half[:, 0:4], ALU.pow))
                n = M_ROPE // 2
                for t in range(TT):
                    kr = mraw[:, t, 392:424]
                    tt(mraw[:, t, 8:264], mraw[:, t, 8:264], m_rstd[:, t, 0:1].to_broadcast([P, M_QR]), ALU.mult)
                    tt(mraw[:, t, 264:392], mraw[:, t, 264:392], m_rstd[:, t, 1:2].to_broadcast([P, M_KVR]), ALU.mult)\
                        .then_inc(m_norm_done.sem, 1)
                    tb = m_rope_b[:, 0:M_ROPE]
                    link(rotate(kr, kr[:, 0:n], kr[:, n:M_ROPE], pcos[:, t], pnsin[:, t], psin[:, t],
                                m_rope_a[:, 0:M_ROPE], (tb[:, 0:n], tb[:, n:M_ROPE], tb), None))

            def up(L, t, i):
                if i != 3:
                    return
                for k in range(4):
                    pool.wait_ge(*drained(L, ("u", t, k)))
                n = M_ROPE // 2
                q_ = v(mqk[:, 0, t], h=8, n=M_QK)[:, :, HD:M_QK]

                def table(t_):
                    return t_[:, t].unsqueeze(1).to_broadcast([P, 8, t_.shape[2]])

                ta, tb = v(m_rope_a, h=8, n=M_ROPE), v(m_rope_b, h=8, n=M_ROPE)
                rotate(q_, q_[:, :, 0:n], q_[:, :, n:M_ROPE], table(pcos), table(pnsin), table(psin), ta,
                       (tb[:, :, 0:n], tb[:, :, n:M_ROPE], tb), None)
                pool.tensor_copy(v(mqk[:, 1, t], h=8, n=M_QK)[:, :, HD:M_QK],
                                 mraw[:, t, 392:424].unsqueeze(1).to_broadcast([P, 8, M_ROPE]))\
                    .then_inc(m_roped.sem, 1)
                pool.wait_ge(*m_roped(L, t + 1))

            def d_stats(L, t):
                pool.wait_ge(*l2_var(L, t + 1))
                root(d_ss, d_rs, 16, l2_rstd)

            def d_scaled(L, t):
                def over(t_):
                    return t_.unsqueeze(2).to_broadcast([P, 8, HD])

                pool.wait_ge(*kn_done(L, t + 1))
                pool.wait_ge(*eg_done(L, t + 1))
                pool.wait_ge(*drained(L, ("DT", t, 2)))
                k_, kb = v(d_tok[:, 1], a=8, b=HD), v(d_kb, a=8, b=HD)
                tt(v(d_w, a=8, b=HD), kb, over(eg[:, 0:8]), ALU.mult)
                tt(v(d_vb, a=8, b=HD), v(d_tok[:, 2], a=8, b=HD), over(half_beta[:, t]), ALU.mult)
                tt(v(d_kdec, a=8, b=HD), k_, over(eg[:, 8:16]), ALU.mult).then_inc(kw_done.sem, 1)

            def level(L, t, b, g):
                if b == 2:
                    pool.wait_ge(*drained(L, ("K1", t, g)))
                else:
                    pool.wait_ge(*filled(L, ("Y", t, b // 2, g)))
                tt(d_C[:, 4 * g:4 * g + 4], d_M[:, 4 * g:4 * g + 4],
                   cst(f"below{b}").unsqueeze(1).to_broadcast([P, 4, P]), ALU.mult).then_inc(level_done.sem, 1)

            def d_finish(L, t):
                pool.wait_ge(*dn_var(L, t + 1))
                root(d_ss2[:, 8 * t:8 * t + 8], d_rs2[:, 8 * t:8 * t + 8], 8, dn_rstd)

            parts1 = {"norm": norm, "d": d1, "br": branch, "F": finish, "RF": r_finish}
            parts2 = {"norm": norm, "br": branch, "SM": small_values, "u": up, "DP": d_stats,
                      "DP2": d_scaled, "Y": level, "DF": d_finish}

            def layer(L):
                pool_chain.layer(pool, L)
                pool.wait_ge(*par_done(L, 1))
                for step in PLANS[L[0]].steps:
                    part = (parts1, parts2)[L[0]].get(step[0])
                    if part:
                        part(L, *step[1:])
                pool_chain.end()

            def last_norm(blk):
                pool.wait_ge(end_ss.sem, TT * (blk + 1))
                tt(x_var, x_ss, cst("eps")[:, 0:TT], ALU.add).then_inc(end_var, 1)
                pool.wait_ge(end_var, blk + 1)
                root(x_var, x_rstd, TT, end_rstd)

            layers(pool, 0, layer)
            last_norm(0)
            layers(pool, 1, layer)
            last_norm(1)


_INPUTS = ["x", "norm_g", "w_in", "attn_lambda", "attn_subln_g", "conv_w", "w_branch", "w_out", "final_norm_g",
           "positions_2", "ffn1_norm_2", "ffn1_w_gu_2", "ffn1_w_down_2", "mix_norm_2", "w_in_2", "b_gate_2",
           "fox_b_f_2", "mla_q_norm_2", "mla_w_uq_2", "mla_kv_norm_2", "mla_w_ukv_2", "dn_conv_w_2",
           "dn_a_log_2", "dn_dt_bias_2", "dn_o_norm_2", "w_br_fox_2", "w_br_mla_2", "w_br_dn_2", "w_out_2",
           "ffn2_norm_2", "ffn2_w_gu_2", "ffn2_w_down_2", "final_norm_2"]


def kernel(**inputs):
    import concourse.bacc as bacc
    from concourse.bass_utils import run_bass_kernel_spmd

    nc = bacc.Bacc("TRN2", target_bir_lowering=False, num_devices=1)
    arrays = {name: np.ascontiguousarray(inputs[name]) for name in _INPUTS}
    arrays["consts"] = CONSTS
    aps = {name: nc.dram_tensor(f"in_{name}", t.shape, mybir.dt.from_np(t.dtype), kind="ExternalInput").ap()
           for name, t in arrays.items()}
    out = nc.dram_tensor("out_x", (1, SEQ, DM), F32, kind="ExternalOutput").ap()
    build(nc, aps, out)
    result = run_bass_kernel_spmd(nc, [{f"in_{name}": t for name, t in arrays.items()}], core_ids=[0])
    return result.results[0]["out_x"]
```
